# Optimizing a Trainium2 kernel written in Bass

```python
import math
import jax
import jax.numpy as jnp
from jax import lax
import numpy as np
import jax, jax.numpy as jnp

D_MODEL = 1024
BATCH = 1
SEQ = 1024
DEPTH = 1

MIX_WIDTH = D_MODEL
PLE_DIM = 256
DA_WIDTH = MIX_WIDTH // 2
DA_HEADS = 4
DA_V_DIM = DA_WIDTH // DA_HEADS
DA_HEAD_DIM = DA_V_DIM // 2
ROT_DIM = DA_HEAD_DIM // 4
ROPE_THETA = 500000.0
Q_BLOCK = 128
HG_WIDTH = MIX_WIDTH - DA_WIDTH
HG_HEADS = 4
HG_KEY_DIM = HG_WIDTH // HG_HEADS
HG_VAL_DIM = HG_WIDTH // HG_HEADS
CHUNK = 64
D_FF = 2816
CONV_WIDTH = 3
EPS = 1e-6

IN_SPLIT_SIZES = (
    DA_HEADS * 2 * DA_HEAD_DIM,
    DA_HEADS * 2 * DA_HEAD_DIM,
    DA_HEADS * DA_V_DIM,
    HG_HEADS * HG_KEY_DIM,
    HG_HEADS * HG_KEY_DIM,
    HG_HEADS * HG_KEY_DIM,
    HG_HEADS * HG_VAL_DIM,
    HG_HEADS * HG_VAL_DIM,
)
IN_COLS = sum(IN_SPLIT_SIZES)
IN_SPLIT_POINTS = tuple(int(c) for c in np.cumsum(IN_SPLIT_SIZES)[:-1])


def rmsnorm(x, g, eps=EPS):
    xf = x.astype(jnp.float32)
    y = xf * lax.rsqrt(jnp.mean(xf * xf, axis=-1, keepdims=True) + eps)
    return (y * g.astype(jnp.float32)).astype(x.dtype)

def partial_rotary(t, positions):
    half = ROT_DIM // 2
    inv_freq = ROPE_THETA ** (-jnp.arange(half, dtype=jnp.float32) / half)
    ang = positions.astype(jnp.float32)[..., None] * inv_freq
    cos = jnp.cos(ang)[:, :, None, None, :]
    sin = jnp.sin(ang)[:, :, None, None, :]
    tr = t[..., :ROT_DIM].astype(jnp.float32)
    x1, x2 = tr[..., :half], tr[..., half:]
    rot = jnp.concatenate([x1 * cos - x2 * sin, x2 * cos + x1 * sin], axis=-1)
    return jnp.concatenate([rot.astype(t.dtype), t[..., ROT_DIM:]], axis=-1)

def diff_attention(q, k, v, lam_q1, lam_k1, lam_q2, lam_k2, subln_g, lambda_init):
    B, S = q.shape[0], q.shape[1]
    f32 = jnp.float32
    lam = (jnp.exp(jnp.sum(lam_q1.astype(f32) * lam_k1.astype(f32)))
           - jnp.exp(jnp.sum(lam_q2.astype(f32) * lam_k2.astype(f32))) + lambda_init)
    scale = DA_HEAD_DIM ** -0.5
    qb = (q * scale).reshape(B, S // Q_BLOCK, Q_BLOCK, DA_HEADS, 2, DA_HEAD_DIM)
    qb = qb.transpose(1, 0, 2, 3, 4, 5)

    def block(qblk):
        s = jnp.einsum('bqhmd,bkhmd->bhmqk', qblk, k, preferred_element_type=f32)
        a = jax.nn.softmax(s, axis=-1)
        w = a[:, :, 0] - lam * a[:, :, 1]
        return jnp.einsum('bhqk,bkhe->bqhe', w.astype(v.dtype), v)

    o = lax.map(block, qb)
    o = o.transpose(1, 0, 2, 3, 4).reshape(B, S, DA_HEADS, DA_V_DIM)
    o = rmsnorm(o, subln_g) * (1.0 - lambda_init)
    return o.reshape(B, S, DA_HEADS * DA_V_DIM)

def _to_chunks(t):
    z, b, s, h, e = t.shape
    return t.reshape(z, b, s // CHUNK, CHUNK, h, e).transpose(2, 0, 1, 4, 3, 5)

def hgrn2_bidirectional(q, zf, zb, v, g, lb_gamma, norm_g, layer):
    B, S = q.shape[0], q.shape[1]
    f32 = jnp.float32
    H, dk, dv = HG_HEADS, HG_KEY_DIM, HG_VAL_DIM
    lb_all = jnp.cumsum(jax.nn.softmax(lb_gamma.astype(f32), axis=1), axis=1)
    lb = lb_all[:, layer].reshape(2, 1, 1, H, dk)
    q4 = q.reshape(B, S, H, dk).astype(f32)
    v4 = v.reshape(B, S, H, dv).astype(f32)
    z = jnp.stack([zf.reshape(B, S, H, dk), zb.reshape(B, S, H, dk)[:, ::-1]], 0).astype(f32)
    log_f = jnp.log(lb + (1.0 - lb) * jax.nn.sigmoid(z))
    k_in = (1.0 - lb) * jax.nn.sigmoid(-z)
    qd = jnp.stack([q4, q4[:, ::-1]], 0)
    vd = jnp.stack([v4, v4[:, ::-1]], 0)
    xs = (_to_chunks(qd), _to_chunks(k_in), _to_chunks(vd), _to_chunks(log_f))
    tri = jnp.tril(jnp.ones((CHUNK, CHUNK), dtype=bool))[:, :, None]

    def step(state, inp):
        qc, kc, vc, gc = inp
        bcum = jnp.cumsum(gc, axis=-2)
        b_last = bcum[..., -1:, :]
        o_inter = jnp.einsum('zbhtk,zbhkv->zbhtv', qc * jnp.exp(bcum), state)
        diff = bcum[..., :, None, :] - bcum[..., None, :, :]
        decay = jnp.exp(jnp.where(tri, diff, -jnp.inf))
        attn = jnp.einsum('zbhtk,zbhtsk->zbhts', qc, decay * kc[..., None, :, :])
        o_intra = jnp.einsum('zbhts,zbhsv->zbhtv', attn, vc)
        k_dec = kc * jnp.exp(b_last - bcum)
        new_state = (jnp.exp(b_last[..., 0, :])[..., None] * state
                     + jnp.einsum('zbhsk,zbhsv->zbhkv', k_dec, vc))
        return new_state, o_inter + o_intra

    state0 = jnp.zeros((2, B, H, dk, dv), f32)
    _, ys = lax.scan(step, state0, xs)
    ys = ys.transpose(1, 2, 0, 4, 3, 5).reshape(2, B, S, H, dv)
    o = ys[0] + ys[1][:, ::-1]
    o = rmsnorm(o, norm_g) * jax.nn.silu(g.reshape(B, S, H, dv).astype(f32))
    return o.reshape(B, S, H * dv).astype(q.dtype)

def conv_glu(h, w_gate, w_up, conv_w, conv_b, w_down):
    S = h.shape[1]
    a = h @ w_gate
    u = h @ w_up
    pad = CONV_WIDTH // 2
    ap = jnp.pad(a, ((0, 0), (pad, pad), (0, 0)))
    c = conv_b
    for j in range(CONV_WIDTH):
        c = c + ap[:, j:j + S] * conv_w[j]
    return (jax.nn.gelu(c, approximate=False) * u) @ w_down

def first_inputs(seed: int = 0) -> dict:
    key = jax.random.key(seed)
    ks = jax.random.split(key, 24)
    f32 = jnp.float32

    def nrm(k, shape, scale):
        return jax.random.normal(k, shape, f32) * scale

    def gain(k, shape):
        return 1.0 + 0.05 * jax.random.normal(k, shape, f32)

    x = nrm(ks[0], (BATCH, SEQ, D_MODEL), 1.0)
    p = nrm(ks[1], (DEPTH, BATCH, SEQ, PLE_DIM), 1.0)
    offsets = jax.random.randint(ks[2], (BATCH, 1), 0, 1024, dtype=jnp.int32)
    positions = offsets + jnp.arange(SEQ, dtype=jnp.int32)[None, :]
    return {
        "x": x,
        "p": p,
        "positions": positions,
        "norm_mix_g": gain(ks[3], (DEPTH, D_MODEL)),
        "w_in": nrm(ks[4], (DEPTH, D_MODEL, IN_COLS), D_MODEL ** -0.5),
        "lam_q1": nrm(ks[5], (DEPTH, DA_HEAD_DIM), 0.1),
        "lam_k1": nrm(ks[6], (DEPTH, DA_HEAD_DIM), 0.1),
        "lam_q2": nrm(ks[7], (DEPTH, DA_HEAD_DIM), 0.1),
        "lam_k2": nrm(ks[8], (DEPTH, DA_HEAD_DIM), 0.1),
        "da_subln_g": gain(ks[9], (DEPTH, DA_V_DIM)),
        "hg_lb_gamma": gain(ks[10], (2, DEPTH + 1, HG_HEADS * HG_KEY_DIM)),
        "hg_norm_g": gain(ks[11], (DEPTH, HG_VAL_DIM)),
        "w_out": nrm(ks[12], (DEPTH, MIX_WIDTH, D_MODEL), MIX_WIDTH ** -0.5),
        "norm_ffn_g": gain(ks[13], (DEPTH, D_MODEL)),
        "w_ffn_gate": nrm(ks[14], (DEPTH, D_MODEL, D_FF), D_MODEL ** -0.5),
        "w_ffn_up": nrm(ks[15], (DEPTH, D_MODEL, D_FF), D_MODEL ** -0.5),
        "ffn_conv_w": nrm(ks[16], (DEPTH, CONV_WIDTH, D_FF), CONV_WIDTH ** -0.5),
        "ffn_conv_b": nrm(ks[17], (DEPTH, D_FF), 0.02),
        "w_ffn_down": nrm(ks[18], (DEPTH, D_FF, D_MODEL), D_FF ** -0.5),
        "norm_ple_g": gain(ks[19], (DEPTH, D_MODEL)),
        "w_ple": nrm(ks[20], (DEPTH, PLE_DIM, D_MODEL), PLE_DIM ** -0.5),
        "w_ple_gate": nrm(ks[21], (DEPTH, D_MODEL, D_MODEL), D_MODEL ** -0.5),
        "final_norm_g": gain(ks[22], (D_MODEL,)),
    }

def first_block(x, p, positions, norm_mix_g, w_in, lam_q1, lam_k1, lam_q2, lam_k2,
              da_subln_g, hg_lb_gamma, hg_norm_g, w_out, norm_ffn_g, w_ffn_gate,
              w_ffn_up, ffn_conv_w, ffn_conv_b, w_ffn_down, norm_ple_g, w_ple,
              w_ple_gate, final_norm_g):
    B, S = x.shape[0], x.shape[1]
    for i in range(DEPTH):
        h = rmsnorm(x, norm_mix_g[i])
        proj = h @ w_in[i]
        da_q, da_k, da_v, hg_q, hg_zf, hg_zb, hg_v, hg_g = jnp.split(proj, IN_SPLIT_POINTS, axis=-1)
        da_q = partial_rotary(da_q.reshape(B, S, DA_HEADS, 2, DA_HEAD_DIM), positions)
        da_k = partial_rotary(da_k.reshape(B, S, DA_HEADS, 2, DA_HEAD_DIM), positions)
        da_v = da_v.reshape(B, S, DA_HEADS, DA_V_DIM)
        lambda_init = 0.8 - 0.6 * math.exp(-0.3 * i)
        o_da = diff_attention(da_q, da_k, da_v, lam_q1[i], lam_k1[i], lam_q2[i], lam_k2[i],
                              da_subln_g[i], lambda_init)
        o_hg = hgrn2_bidirectional(hg_q, hg_zf, hg_zb, hg_v, hg_g, hg_lb_gamma, hg_norm_g[i], i)
        x = x + jnp.concatenate([o_da, o_hg], axis=-1) @ w_out[i]
        x = x + conv_glu(rmsnorm(x, norm_ffn_g[i]), w_ffn_gate[i], w_ffn_up[i],
                         ffn_conv_w[i], ffn_conv_b[i], w_ffn_down[i])
        gate = jax.nn.sigmoid(rmsnorm(x, norm_ple_g[i]) @ w_ple_gate[i])
        x = x + (p[i] @ w_ple[i]) * gate
    return rmsnorm(x, final_norm_g)


HEAD_DIM = 64
CONV_HEADS = 4
ATTN_HEADS = 8
SGU_HEADS = 4
CONV_W = CONV_HEADS * HEAD_DIM
ATTN_W = ATTN_HEADS * HEAD_DIM
SGU_W = SGU_HEADS * HEAD_DIM
D_MIX = CONV_W + ATTN_W + SGU_W
D_IN_PROJ = 3 * CONV_W + 3 * ATTN_W + 2 * SGU_W
CHUNK_2 = 128
D_FF_2 = 4 * D_MODEL


def rms_norm(x, g):
    xf = x.astype(jnp.float32)
    y = xf * lax.rsqrt(jnp.mean(xf * xf, axis=-1, keepdims=True) + EPS)
    return (y * g.astype(jnp.float32)).astype(x.dtype)

def short_conv(x, w):
    s = x.shape[1]
    xp = jnp.pad(x, ((0, 0), (CONV_WIDTH - 1, 0), (0, 0)))
    out = w[0] * xp[:, 0:s]
    for j in range(1, CONV_WIDTH):
        out = out + w[j] * xp[:, j:j + s]
    return out

def stick_breaking_attention(q, k, v):
    s_len = q.shape[1]
    scale = HEAD_DIM ** -0.5
    outs = []
    for qb in range(s_len // Q_BLOCK):
        start = qb * Q_BLOCK
        end = start + Q_BLOCK
        qi = q[:, start:end].astype(jnp.float32)
        kj = k[:, :end].astype(jnp.float32)
        vj = v[:, :end].astype(jnp.float32)
        z = jnp.einsum('bqhd,bkhd->bhqk', qi, kj) * scale
        t_pos = start + jnp.arange(Q_BLOCK)[:, None]
        s_pos = jnp.arange(end)[None, :]
        causal = s_pos < t_pos
        log_beta = jax.nn.log_sigmoid(z)
        log_rem = jnp.where(causal, jax.nn.log_sigmoid(-z), 0.0)
        suffix = lax.cumsum(log_rem, axis=3, reverse=True) - log_rem
        weights = jnp.where(causal, jnp.exp(log_beta + suffix), 0.0)
        o = jnp.einsum('bhqk,bkhd->bqhd', weights, vj)
        outs.append(o.astype(v.dtype))
    return jnp.concatenate(outs, axis=1)

def spatial_gating(u, v, g_v, w_s, b_s):
    bsz, s_len, _ = u.shape
    v = v.reshape(bsz, s_len, SGU_HEADS, HEAD_DIM)
    v = rms_norm(v, g_v.reshape(SGU_HEADS, HEAD_DIM))
    v = v.reshape(bsz, s_len // CHUNK_2, CHUNK_2, SGU_HEADS, HEAD_DIM)
    mask = jnp.tril(jnp.ones((CHUNK_2, CHUNK_2), dtype=w_s.dtype))
    w = w_s * mask
    sv = jnp.einsum('gts,bcsge->bctge', w, v) + b_s.T[:, :, None]
    return u * sv.reshape(bsz, s_len, SGU_W)

def second_inputs(seed: int = 0) -> dict:
    key = jax.random.key(seed)
    ks = jax.random.split(key, 17)

    def nrm(k, shape, scale):
        return jax.random.normal(k, shape, jnp.float32) * scale

    def gain(k, shape):
        return 1.0 + 0.05 * jax.random.normal(k, shape, jnp.float32)

    return {
        "x": nrm(ks[0], (BATCH, SEQ, D_MODEL), 1.0),
        "p": nrm(ks[1], (DEPTH, BATCH, SEQ, PLE_DIM), 1.0),
        "norm1_g": gain(ks[2], (DEPTH, D_MODEL)),
        "w_in": nrm(ks[3], (DEPTH, D_MODEL, D_IN_PROJ), D_MODEL ** -0.5),
        "conv_w": nrm(ks[4], (DEPTH, CONV_WIDTH, CONV_W), CONV_WIDTH ** -0.5),
        "q_norm_g": gain(ks[5], (DEPTH, HEAD_DIM)),
        "k_norm_g": gain(ks[6], (DEPTH, HEAD_DIM)),
        "sgu_norm_g": gain(ks[7], (DEPTH, SGU_W)),
        "sgu_w": nrm(ks[8], (DEPTH, SGU_HEADS, CHUNK_2, CHUNK_2), CHUNK_2 ** -0.5),
        "sgu_b": gain(ks[9], (DEPTH, SGU_HEADS, CHUNK_2)),
        "w_out": nrm(ks[10], (DEPTH, D_MIX, D_MODEL), D_MIX ** -0.5),
        "norm2_g": gain(ks[11], (DEPTH, D_MODEL)),
        "w_ff1": nrm(ks[12], (DEPTH, D_MODEL, D_FF_2), D_MODEL ** -0.5),
        "w_ff2": nrm(ks[13], (DEPTH, D_FF_2, D_MODEL), D_FF_2 ** -0.5),
        "norm3_g": gain(ks[14], (DEPTH, D_MODEL)),
        "w_ple_gate": nrm(ks[15], (DEPTH, D_MODEL, D_MODEL), D_MODEL ** -0.5),
        "w_ple_proj": nrm(ks[16], (DEPTH, PLE_DIM, D_MODEL), PLE_DIM ** -0.5),
    }

def second_block(x, p, norm1_g, w_in, conv_w, q_norm_g, k_norm_g, sgu_norm_g, sgu_w, sgu_b,
              w_out, norm2_g, w_ff1, w_ff2, norm3_g, w_ple_gate, w_ple_proj):
    bsz, s_len, _ = x.shape
    split_idx = list(np.cumsum([CONV_W, CONV_W, CONV_W, ATTN_W, ATTN_W, ATTN_W, SGU_W]))
    h = x
    for i in range(DEPTH):
        hn = rms_norm(h, norm1_g[i])
        proj = hn @ w_in[i]
        a_b, a_c, a_h, q, k, v, c_u, c_v = jnp.split(proj, split_idx, axis=-1)
        y_a = a_b * short_conv(a_c * a_h, conv_w[i])
        q = rms_norm(q.reshape(bsz, s_len, ATTN_HEADS, HEAD_DIM), q_norm_g[i])
        k = rms_norm(k.reshape(bsz, s_len, ATTN_HEADS, HEAD_DIM), k_norm_g[i])
        v = v.reshape(bsz, s_len, ATTN_HEADS, HEAD_DIM)
        y_b = stick_breaking_attention(q, k, v).reshape(bsz, s_len, ATTN_W)
        y_c = spatial_gating(jax.nn.gelu(c_u, approximate=False),
                             jax.nn.gelu(c_v, approximate=False),
                             sgu_norm_g[i], sgu_w[i], sgu_b[i])
        h = h + jnp.concatenate([y_a, y_b, y_c], axis=-1) @ w_out[i]
        f = jnp.square(jax.nn.relu(rms_norm(h, norm2_g[i]) @ w_ff1[i]))
        h = h + f @ w_ff2[i]
        gate = jax.nn.sigmoid(rms_norm(h, norm3_g[i]) @ w_ple_gate[i])
        h = h + gate * (p[i] @ w_ple_proj[i])
    return h


def setup_inputs(seed=0):
    out = dict(first_inputs(seed))
    for name, value in second_inputs(seed + 1).items():
        if name != "x":
            out[name + "_2"] = value
    return out


def reference(
    x, p, positions, norm_mix_g, w_in, lam_q1, lam_k1, lam_q2, lam_k2, da_subln_g, hg_lb_gamma,
    hg_norm_g, w_out, norm_ffn_g, w_ffn_gate, w_ffn_up, ffn_conv_w, ffn_conv_b, w_ffn_down,
    norm_ple_g, w_ple, w_ple_gate, final_norm_g, p_2, norm1_g_2, w_in_2, conv_w_2, q_norm_g_2,
    k_norm_g_2, sgu_norm_g_2, sgu_w_2, sgu_b_2, w_out_2, norm2_g_2, w_ff1_2, w_ff2_2, norm3_g_2,
    w_ple_gate_2, w_ple_proj_2,
):
    x = first_block(
        x, p, positions, norm_mix_g, w_in, lam_q1, lam_k1, lam_q2, lam_k2, da_subln_g,
        hg_lb_gamma, hg_norm_g, w_out, norm_ffn_g, w_ffn_gate, w_ffn_up, ffn_conv_w, ffn_conv_b,
        w_ffn_down, norm_ple_g, w_ple, w_ple_gate, final_norm_g,
    )
    return second_block(
        x, p_2, norm1_g_2, w_in_2, conv_w_2, q_norm_g_2, k_norm_g_2, sgu_norm_g_2, sgu_w_2,
        sgu_b_2, w_out_2, norm2_g_2, w_ff1_2, w_ff2_2, norm3_g_2, w_ple_gate_2, w_ple_proj_2,
    )


_drawn_inputs = setup_inputs


def setup_inputs(seed=0):
    import zlib

    import numpy as np

    out = dict(_drawn_inputs(seed))
    spreads = {}
    factors = {'lam_q1': 64.0,
     'hg_lb_gamma': 3.104,
     'ffn_conv_b': 5.149,
     'norm_ple_g': 6.537,
     'q_norm_g_2': 5.144,
     'k_norm_g_2': 7.132,
     'sgu_norm_g_2': 6.376,
     'sgu_b_2': 4.696,
     'norm3_g_2': 36.358}
    for name, (base, spread) in spreads.items():
        noise = np.random.default_rng([zlib.crc32(name.encode()), seed]).standard_normal(out[name].shape)
        drawn = base * np.exp(spread * noise) if base else spread * noise
        out[name] = jnp.asarray(drawn.astype(out[name].dtype))
    for name, factor in factors.items():
        out[name] = (out[name] * factor).astype(out[name].dtype)
    return out
```

```python
from contextlib import ExitStack

import numpy as np

import concourse.bass as bass
from concourse import mybir

F32 = mybir.dt.float32
F32R = mybir.dt.float32r
I32 = mybir.dt.int32
ALU = mybir.AluOpType
ACT = mybir.ActivationFunctionType
AX_X = mybir.AxisListType.X

P = 128
T = 1024
HALF = 512
KT = 8
FT = 22
FT2 = 32
PT = 2
GROUPS1 = (8, 8, 6)
GROUPS2 = (8, 8, 8, 8)
HEADS = 4
LEVELS = 7
EPS = 1e-6
SBUF_BASE = 16512
LAMBDA_INIT = 0.2
TWO_PI = 2.0 * np.pi

VEC = {}
_at = 0
for _name, _n in (("norm_mix", 8), ("norm_ffn", 8), ("norm_ple", 8), ("final", 8), ("norm1", 8),
                  ("norm2", 8), ("norm3", 8), ("conv_w0", FT), ("conv_w1", FT), ("conv_w2", FT),
                  ("conv_b", FT), ("conv2_w0", 2), ("conv2_w1", 2), ("conv2_w2", 2), ("qn", 1),
                  ("kn", 1), ("sgu_g", 2), ("subln", 1), ("hgn", 1), ("gamma0", 8), ("gamma1", 8),
                  ("lam", 4)):
    VEC[_name] = _at
    _at += _n
NVEC = _at
DER = {}
_at = 0
for _name, _n in (("fin_n1", 8), ("subln", 1), ("qn", 1), ("neg_lam", 1), ("lb", 8), ("omlb", 8),
                  ("g0", 8), ("g1", 8), ("lamp", 2), ("lame", 2), ("zero", 1)):
    DER[_name] = _at
    _at += _n
NDER = _at

U_DA = 0
U_HG = U_DA + 3 * HEADS
U_OUT = U_HG + 5 * HEADS
U_GU = []
U_DN = []
_u = U_OUT + KT
for _n in GROUPS1:
    U_GU.append(_u)
    _u += 2 * _n
    U_DN.append(_u)
    _u += KT
U_PLE = _u
U_SB = U_PLE + 2 * KT
U_CV = U_SB + 3 * HEADS
U_SG = U_CV + 3 * 2
U_OUT2 = U_SG + 2 * 2
U_F1 = []
U_F2 = []
_u = U_OUT2 + KT
for _n in GROUPS2:
    U_F1.append(_u)
    _u += _n
    U_F2.append(_u)
    _u += KT
U_PLE2 = _u
U_END = U_PLE2 + 2 * KT

N_MIX = 0
N_DA = 1
N_HG = N_DA + HEADS
N_FFN = N_HG + HEADS
N_PLE = N_FFN + 1
N_FIN = N_PLE + 1
N_1 = N_FIN + 1
N_QK = N_1 + 1
N_SG = N_QK + 2 * HEADS
N_2 = N_SG + 2
N_3 = N_2 + 1


F_MIX = 0
F_FF = F_MIX + KT
F_MIX2 = F_FF + FT
F_FF2 = F_MIX2 + KT
Q_MIX, Q_FFN, Q_PLE, Q_1, Q_2, Q_3 = range(0, 6 * KT, KT)

MAGIC = 1.5 * 2.0**23
_c2 = np.floor((TWO_PI - 6.28125) * 2.0**20) / 2.0**20
TURN = (6.28125, float(_c2), float(np.float32(TWO_PI - 6.28125 - _c2)))


def half_no(u, hf):
    return 2 * u + hf + 1


def stick_pieces():
    return [(th, i, hh) for th in range(2) for i in range(4 * th + 3, -1, -1) for hh in range(2)]


PIECES = stick_pieces()
NPC = len(PIECES)


def diagonal_no(p, n):
    in_pair = [i >= 4 * th for th, i, _ in PIECES]
    return sum(in_pair) * p + sum(in_pair[:n + 1])


def bass_two_blocks(nc, io):
    ctx = ExitStack()
    with ctx:
        def at(name, cols, off, dt=F32, parts=P):
            shape = [parts, *cols] if isinstance(cols, tuple) else [parts, cols]
            return nc.alloc_sbuf_tensor_at(name, shape, dt, offset=SBUF_BASE + off)

        def sem(name):
            return ctx.enter_context(nc.semaphore(name))


        KB = 1024
        a_hi = at("a_hi", (KT, T), 0, F32R)
        a_lo = at("a_lo", (KT, T), 32 * KB, F32R)
        b_hi = at("b_hi", (KT, T), 64 * KB, F32R)
        b_lo = at("b_lo", (KT, T), 96 * KB, F32R)
        x = at("x", (KT, T), 128 * KB)
        mix = at("mix", (KT, T), 128 * KB)
        w_raw = at("w_raw", (2, T), 160 * KB)
        w_hi = at("w_hi", (2, T), 168 * KB, F32R)
        w_lo = at("w_lo", (2, T), 176 * KB, F32R)
        rstd = at("rstd", T, 184 * KB)
        TMP = 188 * KB
        pad_a = at("pad_a", (2, 1032), TMP)
        sq = at("sq", (2, 1032), TMP)
        c_buf = at("c_buf", T, TMP + 8256)
        ss = at("ss", T, TMP + 8256 + 4096)
        CST = TMP + 8256 + 8192
        ident = at("ident", P, CST)
        cst = at("cst", 8, CST + 512)
        vec = at("vec", NVEC, CST + 544)
        VEC_END = CST + 544 + (4 * NVEC + 31) // 32 * 32
        der = at("der", NDER, VEC_END)
        sm = at("sm", (4, 16), VEC_END + (4 * NDER + 31) // 32 * 32)
        SM_END = VEC_END + (4 * NDER + 31) // 32 * 32 + 256
        rows = at("rows", (2, 16), SM_END)
        one = cst[:, 0:1]
        blk2 = cst[:, 1:3]
        invf = cst[:, 3:4]

        S0 = 64 * KB
        dq = at("dq", (2, T), S0)
        dv = at("dv", T, S0 + 8 * KB)
        dvt = at("dvt", (KT, P), S0 + 12 * KB)
        de = at("de", (2, 2, T), S0 + 16 * KB)
        dwt = at("dwt", (2, HALF), S0 + 32 * KB)
        dtmp = at("dtmp", T, S0 + 36 * KB)
        cosm = at("cosm", T, S0 + 40 * KB)
        sinm = at("sinm", T, S0 + 44 * KB)
        swapm = at("swapm", P, S0 + 48 * KB)
        ang = at("ang", T, S0 + 49 * KB)
        ang2 = at("ang2", T, S0 + 53 * KB)
        posi = at("posi", T, S0 + 57 * KB, mybir.dt.int32)
        hq = at("hq", T, S0)
        hz = at("hz", (2, T), S0 + 4 * KB)
        hv = at("hv", T, S0 + 12 * KB)
        hg = at("hg", T, S0 + 16 * KB)
        hvt = at("hvt", (KT, P), S0 + 20 * KB)
        hk = at("hk", (2, T), S0 + 24 * KB)
        hd = at("hd", (2, T), S0 + 32 * KB)
        hqt = at("hqt", (2, HALF), S0 + 40 * KB)
        hkt = at("hkt", (2, T), S0 + 44 * KB)
        hatt = at("hatt", T, S0 + 52 * KB)
        hkd = at("hkd", (KT, P), S0 + 56 * KB)
        heb = at("heb", (2, KT), S0 + 60 * KB)
        hmask = at("hmask", (2 * LEVELS, 64), S0 + 60 * KB + 256, I32)
        reset = at("reset", T, TMP + 8256)
        sk = at("sk", (2, T), S0)
        sv = at("sv", T, S0 + 8 * KB)
        svt = at("svt", (KT, P), S0 + 12 * KB)
        sz = at("sz", (4, HALF), S0 + 16 * KB)
        sl = at("sl", (4, HALF), S0 + 24 * KB)
        sp = at("sp", (4, HALF), S0 + 32 * KB)
        sph = at("sph", (4, HALF), S0 + 40 * KB, F32R)
        spl = at("spl", (4, HALF), S0 + 48 * KB, F32R)
        sw = at("sw", (4, HALF), S0 + 56 * KB)
        tri = at("tri", (2, P), TMP, F32R)
        tri_raw = at("tri_raw", (3, P), TMP + KB)
        ctri = tri_raw[:, 2, :]
        cc = at("cc", (3, T), S0)
        cp = at("cp", T + 8, S0 + 12 * KB)
        gv = at("gv", (2, T), S0 + 20 * KB)
        gvt = at("gvt", (KT, P), S0 + 28 * KB)
        gw = at("gw", (4, P), S0 + 32 * KB)
        gb = at("gb", (2, P), S0 + 34 * KB)
        gmask = at("gmask", P, S0 + 35 * KB)
        p_raw = at("p_raw", (PT, T), S0 + 16 * KB)

        ps = ctx.enter_context(nc.psum_tensor("ps", [P, 8, HALF], F32))

        def banks(a, n=2):
            return ps[:, a:a + n, :].rearrange("p a b -> p (a b)")

        x_back = nc.dram_tensor("x_back", (P, KT, T), F32, kind="Internal").ap()

        param_in = sem("param_in")
        w_in = [sem(f"w_in{s}") for s in range(2)]
        w_hi_done = sem("w_hi_done")
        w_split = sem("w_split")
        acc_full = sem("acc_full")
        acc_free = sem("acc_free")
        x_in = [sem(f"x_in{k}") for k in range(KT)]
        x_out = sem("x_out")
        out_done = sem("out_done")
        h_hi = sem("h_hi")
        h_lo = sem("h_lo")
        sq_ready = sem("sq_ready")
        ss_ready = sem("ss_ready")
        st_sum = sem("st_sum")
        st_var = sem("st_var")
        st_root = sem("st_root")
        st_inv = sem("st_inv")
        st_bc = sem("st_bc")
        rstd_ready = sem("rstd_ready")
        dve_step = sem("dve_step")
        act_step = sem("act_step")
        x_done = sem("x_done")
        xf_ready = sem("xf_ready")
        fx_ready = sem("fx_ready")
        pos_in = sem("pos_in")
        ang_ready = sem("ang_ready")
        cs_ready = sem("cs_ready")
        der_ready = sem("der_ready")
        lam_mm = sem("lam_mm")
        lam_exp = sem("lam_exp")
        swapped = sem("swapped")
        qk_ready = sem("qk_ready")
        v_tr = sem("v_tr")
        v_ready = sem("v_ready")
        scored = sem("scored")
        max_ready = sem("max_ready")
        exp_done = sem("exp_done")
        w_ready = sem("w_ready")
        w_tr = sem("w_tr")
        wt_ready = sem("wt_ready")
        o_mm = sem("o_mm")
        o_out = sem("o_out")
        o_sq = sem("o_sq")
        mix_ready = sem("mix_ready")
        hmask_in = sem("hmask_in")
        sig_done = sem("sig_done")
        f_ready = sem("f_ready")
        logf_done = sem("logf_done")
        d_ready = sem("d_ready")
        e_done = sem("e_done")
        qk_lvl = sem("qk_lvl")
        lvl_mm = sem("lvl_mm")
        att_put = sem("att_put")
        kd_ready = sem("kd_ready")
        kd_tr = sem("kd_tr")
        kdt_ready = sem("kdt_ready")
        kv_mm = sem("kv_mm")
        state_ready = sem("state_ready")
        silu_done = sem("silu_done")
        tri_in = sem("tri_in")
        tri_ready = sem("tri_ready")
        sq_qk = sem("sq_qk")
        z_mm = sem("z_mm")
        z_out = sem("z_out")
        l_ready = sem("l_ready")
        sp_ready = sem("sp_ready")
        sph_ready = sem("sph_ready")
        spl_ready = sem("spl_ready")
        suf_mm = sem("suf_mm")
        t_ready = sem("t_ready")
        sw_exp = sem("sw_exp")
        sw_ready = sem("sw_ready")
        so_mm = sem("so_mm")
        so_out = sem("so_out")
        gate_in = sem("gate_in")
        gelu_done = sem("gelu_done")
        gw_ready = sem("gw_ready")
        gn_ready = sem("gn_ready")
        g_tr = sem("g_tr")
        gt_ready = sem("gt_ready")
        gs_mm = sem("gs_mm")
        conv_done = sem("conv_done")
        act_done = sem("act_done")
        f_hi = sem("f_hi")
        f_lo = sem("f_lo")
        p_in = sem("p_in")
        p_hi = sem("p_hi")
        p_lo = sem("p_lo")
        pg_sig = sem("pg_sig")

        lam_ready = sem("lam_ready")
        g_ready = sem("g_ready")
        qd_ready = sem("qd_ready")
        ho_mm = sem("ho_mm")
        ho_out = sem("ho_out")
        s2_ready = sem("s2_ready")
        sq2_ready = sem("sq2_ready")
        sv_tr = sem("sv_tr")
        sv_ready = sem("sv_ready")
        qk2_ready = sem("qk2_ready")
        g_sq = sem("g_sq")
        g_done = sem("g_done")

        block = ctx.enter_context(nc.Block())

        @block.sync
        def _(sp_):
            sp_.dma_start(vec[:, :], io["vec"]).then_inc(param_in, 16)
            sp_.dma_start(ident[:, :], io["ident"]).then_inc(param_in, 16)
            sp_.dma_start(cst[:, :], io["cst"]).then_inc(param_in, 16)
            for k in range(KT):
                sp_.dma_start(x[:, k, :], io["x"][:, k, :]).then_inc(x_in[k], 16)
            sp_.dma_start(posi[:, :], io["pos"]).then_inc(pos_in, 16)
            sp_.dma_start(swapm[:, :], io["swap"]).then_inc(pos_in, 16)

            def weights(name, u0, n, cols=(T, T)):
                src = io[name]

                def load(i, s, u):
                    sp_.wait_ge(w_split, u - 1)
                    sp_.dma_start(w_raw[:, s, 0:cols[s]],
                                  src[bass.ds(2 * i + s, 1), :, 0:cols[s]].rearrange("u p n -> (u p) n")
                                  ).then_inc(w_in[s], 16)

                if u0 == 0:
                    for s in range(2):
                        sp_.dma_start(w_raw[:, s, :], src[s]).then_inc(w_in[s], 16)
                    with sp_.Fori(1, n // 2, 1) as i:
                        for s in range(2):
                            load(i, s, u0 + 2 * i + s)
                else:
                    with sp_.Fori(0, n // 2, 1) as i:
                        for s in range(2):
                            load(i, s, u0 + 2 * i + s)

            weights("w_mix", U_DA, U_OUT)
            weights("w_out", U_OUT, KT)
            for gi, n in enumerate(GROUPS1):
                weights(f"w_gu{gi}", U_GU[gi], 2 * n)
                weights(f"w_dn{gi}", U_DN[gi], KT, (n * P, n * P))
            weights("w_ple", U_PLE, 2 * KT, (T, PT * P))
            weights("w_mix2", U_SB, U_OUT2 - U_SB)
            weights("w_out2", U_OUT2, KT)
            for gi, n in enumerate(GROUPS2):
                weights(f"w_f1{gi}", U_F1[gi], n)
                weights(f"w_f2{gi}", U_F2[gi], KT)
            weights("w_ple2", U_PLE2, 2 * KT, (T, PT * P))
            sp_.wait_ge(out_done, 16 * KT)

        @block.gpsimd
        def _(pool):
            pool.memset(der[:, DER["zero"]:DER["zero"] + 1], 0.0).then_inc(der_ready, 1)
            pool.wait_ge(der_ready, 1)
            zero = der[:, DER["zero"]:DER["zero"] + 1]

            def split(u0, n, cols=(T, T)):
                def one_unit(u, s, turn, first):
                    pool.wait_ge(w_in[s], 16 * (turn + 1))
                    if not first:
                        pool.wait_ge(acc_full, half_no(u - 2, 1))
                    nc.gpsimd.tensor_tensor(w_hi[:, s, 0:cols[s]], w_raw[:, s, 0:cols[s]],
                                            zero.to_broadcast([P, cols[s]]), ALU.add).then_inc(w_hi_done, 1)
                    pool.wait_ge(w_hi_done, u + 1)
                    nc.gpsimd.tensor_tensor(w_lo[:, s, 0:cols[s]], w_raw[:, s, 0:cols[s]],
                                            w_hi[:, s, 0:cols[s]].bitcast(F32), ALU.subtract).then_inc(w_split, 1)

                if u0 == 0:
                    for s in range(2):
                        one_unit(s, s, 0, True)
                    with pool.Fori(1, n // 2, 1) as i:
                        for s in range(2):
                            one_unit(2 * i + s, s, i, False)
                else:
                    with pool.Fori(0, n // 2, 1) as i:
                        for s in range(2):
                            one_unit(u0 + 2 * i + s, s, u0 // 2 + i, False)

            split(U_DA, U_GU[0])
            for gi, n in enumerate(GROUPS1):
                split(U_GU[gi], 2 * n)
                split(U_DN[gi], KT, (n * P, n * P))
            split(U_PLE, 2 * KT, (T, PT * P))
            split(U_SB, U_PLE2 - U_SB)
            split(U_PLE2, 2 * KT, (T, PT * P))


        @block.tensor
        def _(pe):
            mm = nc.tensor.matmul

            def gemm_half(u, hf, s, hi, lo, nk, wait_k=None):
                if hf == 0:
                    pe.wait_ge(w_split, u + 1)
                if not (isinstance(u, int) and half_no(u, hf) <= 2):
                    pe.wait_ge(acc_free, half_no(u, hf) - 2)
                cols = slice(hf * HALF, hf * HALF + HALF)
                for k in range(nk):
                    if wait_k:
                        wait_k(k)
                    wh, wl = w_hi[:, s, k * P:(k + 1) * P], w_lo[:, s, k * P:(k + 1) * P]
                    mm(ps[:, hf, :], wh, hi[:, k, cols], start=(k == 0), stop=False)
                    mm(ps[:, hf, :], wh, lo[:, k, cols], start=False, stop=False)
                    last = mm(ps[:, hf, :], wl, hi[:, k, cols], start=False, stop=(k == nk - 1))
                last.then_inc(acc_full, 1)

            def gemm(u, s, hi, lo, nk, wait_k=None):
                gemm_half(u, 0, s, hi, lo, nk, wait_k)
                gemm_half(u, 1, s, hi, lo, nk)

            def gemm_loop(u0, n, hi, lo, nk, wait_k=None, first=0):
                with pe.Fori(first, n // 2, 1) as i:
                    for s in range(2):
                        gemm(u0 + 2 * i + s, s, hi, lo, nk, wait_k if s == 0 else None)

            def st_sums(src, rhs, ncol):
                for c in range(KT):
                    last = mm(ps[:, 7, c * ncol:(c + 1) * ncol], src[:, c * P:(c + 1) * P], rhs,
                              start=True, stop=True)
                last.then_inc(st_sum, 1)

            def st_bcast(n, ncol, bank):
                pe.wait_ge(st_inv, n + 1)
                rows_ = P // ncol
                for c in range(KT):
                    for j in range(ncol):
                        lhs = sm[:, 3, ncol * c + j:ncol * c + j + 1].to_broadcast([P, rows_])
                        last = mm(ps[rows_ * j:rows_ * (j + 1), bank + c // 4, (c % 4) * P:(c % 4 + 1) * P],
                                  lhs, ident[:, :], start=True, stop=True)
                last.then_inc(st_bc, 1)

            def transposes(src, bank, done):
                for c in range(KT):
                    last = nc.tensor.transpose(ps[:, bank + c // 4, (c % 4) * P:(c % 4 + 1) * P],
                                               src[:, c * P:(c + 1) * P], ident[:, :])
                last.then_inc(done, 1)

            def normed_unit(n, q0, u0, ss_count):
                gemm_half(u0, 0, 0, a_hi, a_lo, KT, lambda k: pe.wait_ge(h_lo, q0 + k + 1))
                pe.wait_ge(ss_ready, ss_count)
                st_sums(ss, one, 1)
                gemm_half(u0, 1, 0, a_hi, a_lo, KT)
                st_bcast(n, 1, 5)

            pe.wait_ge(param_in, 48)
            pe.wait_ge(lam_ready, 1)
            mm(ps[:, 7, 0:2], one[0:64, :].to_broadcast([64, P]), der[0:64, DER["lamp"]:DER["lamp"] + 2],
               start=True, stop=True).then_inc(lam_mm, 1)
            pe.wait_ge(lam_exp, 1)
            normed_unit(N_MIX, 0, U_DA, KT)

            def scores(h, qt):
                g = KT * h + qt
                for m in range(2):
                    if g > 0:
                        pe.wait_ge(exp_done, 2 * (g - 1) + m + 1)
                    r = slice(64 * m, 64 * m + 64)
                    for hf in range(2):
                        last = mm(ps[:, 2 + 2 * m + hf, :], dq[r, 0, qt * P:(qt + 1) * P],
                                  dq[r, 1, hf * HALF:(hf + 1) * HALF], start=True, stop=True)
                    last.then_inc(scored, 1)

            def weigh(h, qt):
                g = KT * h + qt
                pe.wait_ge(w_ready, g + 1)
                for r in range(2):
                    if g or r:
                        pe.wait_ge(wt_ready, 2 * g + r)
                    for c in range(4):
                        last = nc.tensor.transpose(ps[:, 6, c * P:(c + 1) * P],
                                                   de[:, g % 2, 0, (4 * r + c) * P:(4 * r + c + 1) * P],
                                                   ident[:, :])
                    last.then_inc(w_tr, 1)
                if qt == 4:
                    pe.wait_ge(o_out, 2 * h + 1)
                for c in range(KT):
                    if c % 4 == 0:
                        pe.wait_ge(wt_ready, 2 * g + c // 4 + 1)
                    last = mm(ps[:, 7, (qt % 4) * P:(qt % 4 + 1) * P], dvt[:, c, :],
                              dwt[:, c // 4, (c % 4) * P:(c % 4 + 1) * P], start=(c == 0),
                              stop=(c == KT - 1))
                last.then_inc(o_mm, 1)

            for h in range(HEADS):
                u = U_DA + 3 * h
                for j in range(3):
                    if u + j > 0:
                        gemm(u + j, (u + j) % 2, a_hi, a_lo, KT)
                pe.wait_ge(pos_in, 32)
                pe.wait_ge(rstd_ready, 1)
                if h:
                    pe.wait_ge(mix_ready, h)
                for t in range(2):
                    pe.wait_ge(acc_free, half_no(u + t, 1))
                    for hf in range(2):
                        last = mm(ps[:, 2 + 2 * t + hf, :], swapm[:, :], dq[:, t, hf * HALF:(hf + 1) * HALF],
                                  start=True, stop=True)
                    last.then_inc(swapped, 1)
                pe.wait_ge(acc_free, half_no(u + 2, 1))
                transposes(dv, 6, v_tr)
                pe.wait_ge(v_ready, h + 1)
                pe.wait_ge(qk_ready, 2 * h + 2)
                scores(h, 0)
                for qt in range(KT):
                    if qt + 1 < KT:
                        scores(h, qt + 1)
                    weigh(h, qt)
                pe.wait_ge(o_sq, h + 1)
                st_sums(ang, one, 1)
                st_bcast(N_DA + h, 1, 2)

            for h in range(HEADS):
                u = U_HG + 5 * h
                for j in range(5):
                    gemm(u + j, (u + j) % 2, a_hi, a_lo, KT)
                pe.wait_ge(mix_ready, HEADS + h)
                pe.wait_ge(acc_free, half_no(u + 3, 1))
                transposes(hv, 2, v_tr)
                pe.wait_ge(qk_lvl, 15 * h + 1)
                for c in range(KT):
                    last = mm(ps[:, 4 + c // 4, (c % 4) * P:(c % 4 + 1) * P], hd[:, 0, c * P:(c + 1) * P],
                              hq[:, c * P:(c + 1) * P], start=True, stop=True)
                last.then_inc(lvl_mm, 1)
                for l in range(2 * LEVELS):
                    n = 15 * h + 1 + l
                    pe.wait_ge(qk_lvl, n + 1)
                    pe.wait_ge(att_put, n if l < 2 else n - 1)
                    for c in range(KT):
                        last = mm(ps[:, 4 + l % 2, c * 64:(c + 1) * 64], hkt[:, l % 2, c * P:(c + 1) * P],
                                  hqt[:, l % 2, c * 64:(c + 1) * 64], start=True, stop=True)
                    last.then_inc(lvl_mm, 1)
                for d in range(2):
                    n = 2 * h + d
                    pe.wait_ge(kd_ready, n + 1)
                    pe.wait_ge(v_ready, HEADS + h + 1)
                    if n:
                        pe.wait_ge(kdt_ready, n)
                    transposes(hkt[:, d, :], 2, kd_tr)
                    pe.wait_ge(kdt_ready, n + 1)
                    pe.wait_ge(att_put, 15 * h + 15)
                    if d:
                        pe.wait_ge(state_ready, 2 * h + 1)
                    for c in range(KT):
                        last = mm(ps[:, 4 + c // 4, (c % 4) * P:(c % 4 + 1) * P], hkd[:, c, :],
                                  hvt[:, c, :], start=True, stop=True)
                    last.then_inc(kv_mm, 1)
                pe.wait_ge(state_ready, 2 * h + 2)
                pe.wait_ge(qd_ready, 2 * h + 2)
                for c in range(KT):
                    t = slice(c * P, (c + 1) * P)
                    parts = [(hvt[:, c, :], hatt[:, t])]
                    if c > 0:
                        parts.append((hk[:, 0, t], hz[:, 0, t]))
                    if c < KT - 1:
                        parts.append((hk[:, 1, t], hz[:, 1, t]))
                    for n, (lhs, rhs) in enumerate(parts):
                        last = mm(ps[:, 6 + c // 4, (c % 4) * P:(c % 4 + 1) * P], lhs, rhs,
                                  start=(n == 0), stop=(n == len(parts) - 1))
                last.then_inc(ho_mm, 1)
                pe.wait_ge(o_sq, HEADS + h + 1)
                st_sums(hv, one, 1)
                st_bcast(N_HG + h, 1, 4)

            def mixed_out(u0, f0):
                gemm_half(u0, 0, 0, b_hi, b_lo, KT, lambda k: pe.wait_ge(f_lo, f0 + k + 1))
                gemm_half(u0, 1, 0, b_hi, b_lo, KT)
                gemm(u0 + 1, 1, b_hi, b_lo, KT)
                gemm_loop(u0, KT, b_hi, b_lo, KT, first=1)

            mixed_out(U_OUT, F_MIX)
            f = F_FF
            for gi, n in enumerate(GROUPS1):
                if gi == 0:
                    normed_unit(N_FFN, Q_FFN, U_GU[0], Q_FFN + KT)
                    gemm(U_GU[0] + 1, 1, a_hi, a_lo, KT)
                    gemm_loop(U_GU[0], 2 * n, a_hi, a_lo, KT, first=1)
                else:
                    gemm_loop(U_GU[gi], 2 * n, a_hi, a_lo, KT)
                f += n
                gemm_loop(U_DN[gi], KT, b_hi, b_lo, n,
                          lambda k: k == n - 1 and pe.wait_ge(f_lo, f))

            def embedding(n, q0, u0, turn):
                normed_unit(n, q0, u0, q0 + KT)
                gemm(u0 + 1, 1, b_hi, b_lo, PT, lambda k: pe.wait_ge(p_lo, 2 * turn + k + 1))
                with pe.Fori(1, KT, 1) as i:
                    gemm(u0 + 2 * i, 0, a_hi, a_lo, KT)
                    gemm(u0 + 2 * i + 1, 1, b_hi, b_lo, PT)

            embedding(N_PLE, Q_PLE, U_PLE, 0)

            gemm_half(U_SB, 0, 0, a_hi, a_lo, KT, lambda k: pe.wait_ge(h_lo, Q_1 + k + 1))
            pe.wait_ge(ss_ready, Q_1 + KT)
            st_sums(ss, one, 1)
            pe.wait_ge(s2_ready, KT)
            pe.wait_ge(st_var, N_FIN + 1)
            st_sums(c_buf, one, 1)
            gemm_half(U_SB, 1, 0, a_hi, a_lo, KT)
            st_bcast(N_1, 1, 5)
            pe.wait_ge(rstd_ready, 4)
            for c in range(KT):
                last = mm(ps[:, 5 + c // 4, (c % 4) * P:(c % 4 + 1) * P], sm[:, 0, c:c + 1].to_broadcast([P, P]),
                          ident[:, :], start=True, stop=True)
            last.then_inc(st_bc, 1)

            def piece(p, n):
                return NPC * p + n

            def logits(p, n):
                th, i, hh = PIECES[n]
                c0 = max(0, i - 4 * th) * P
                s = piece(p, n)
                if s >= 2:
                    pe.wait_ge(z_out, s - 1)
                r = slice(64 * hh, 64 * hh + 64)
                mm(ps[:, 2 + s % 2, c0:], sk[r, 1, i * P:(i + 1) * P],
                   sk[r, 0, th * HALF + c0:(th + 1) * HALF], start=True, stop=True).then_inc(z_mm, 1)

            def suffix(p, n, which):
                th, i, hh = PIECES[n]
                c0 = max(0, i - 4 * th) * P
                s = piece(p, n)
                first = which == 0 and i == 4 * th + 3
                if which == 0:
                    pe.wait_ge(spl_ready, s + 1)
                else:
                    pe.wait_ge(t_ready, s + 1)
                if first and th:
                    pe.wait_ge(t_ready, s - 1)
                for m, part in enumerate((sph, spl)):
                    last = mm(ps[:, 4 + hh, c0:], tri[:, which, :], part[:, s % 4, c0:],
                              start=(first and m == 0), stop=(m == 1), skip_group_check=True)
                if which == 0:
                    last.then_inc(suf_mm, 1)

            def values(p, n):
                th, i, hh = PIECES[n]
                c0 = max(0, i - 4 * th) * P
                s = piece(p, n)
                if i >= 4 * th:
                    pe.wait_ge(sw_ready, diagonal_no(p, n))
                else:
                    pe.wait_ge(sw_exp, s + 1)
                if i == 4 * th + 3 and (p or th):
                    pe.wait_ge(so_out, 4 * p + 2 * th + hh - 1)
                last = mm(ps[:, 6 + hh, c0:], svt[:, i, :], sw[:, s % 4, c0:], start=(i == 4 * th + 3),
                          stop=(i == 0), skip_group_check=True)
                last.then_inc(so_mm, 1)

            pe.wait_ge(tri_ready, 2)
            for p in range(HEADS):
                u = U_SB + 3 * p
                for j in range(3):
                    if j or p:
                        gemm(u + j, (u + j) % 2, a_hi, a_lo, KT)
                if p == 0:
                    pe.wait_ge(xf_ready, KT)
                for t in range(2):
                    pe.wait_ge(sq_qk, 2 * p + t + 1)
                    if p and t == 0:
                        pe.wait_ge(so_out, 4 * p)
                    st_sums(c_buf, blk2, 2)
                    if t:
                        pe.wait_ge(qk2_ready, 2 * p + t)
                    st_bcast(N_QK + 2 * p + t, 2, 4)
                pe.wait_ge(acc_free, half_no(u + 2, 1))
                transposes(sv, 2, sv_tr)
                pe.wait_ge(sv_ready, p + 1)
                pe.wait_ge(qk2_ready, 2 * p + 2)
                for n in range(NPC + 3):
                    if n < NPC:
                        logits(p, n)
                    if 1 <= n <= NPC:
                        suffix(p, n - 1, 0)
                    if 2 <= n <= NPC + 1 and PIECES[n - 2][1] > 0:
                        suffix(p, n - 2, 1)
                    if n >= 3:
                        values(p, n - 3)

            for j in range(6):
                gemm(U_CV + j, (U_CV + j) % 2, a_hi, a_lo, KT)
            pe.wait_ge(so_out, 4 * HEADS)
            pe.wait_ge(gw_ready, 1)
            for j in range(2):
                u = U_SG + 2 * j
                gemm(u, u % 2, a_hi, a_lo, KT)
                gemm(u + 1, (u + 1) % 2, a_hi, a_lo, KT)
                pe.wait_ge(g_sq, j + 1)
                if j:
                    pe.wait_ge(g_done, 2 * j)
                st_sums(c_buf, blk2, 2)
                st_bcast(N_SG + j, 2, 4)
                pe.wait_ge(gn_ready, j + 1)
                transposes(gv[:, 0, :], 2, g_tr)
                pe.wait_ge(gt_ready, j + 1)
                for hh in range(2):
                    for c in range(KT):
                        last = mm(ps[:, 4 + 2 * hh + c // 4, (c % 4) * P:(c % 4 + 1) * P], gvt[:, c, :],
                                  gw[:, 2 * j + hh, :], start=True, stop=True)
                last.then_inc(gs_mm, 1)

            mixed_out(U_OUT2, F_MIX2)
            f = F_FF2
            for gi, n in enumerate(GROUPS2):
                if gi == 0:
                    normed_unit(N_2, Q_2, U_F1[0], Q_2 + KT)
                    gemm(U_F1[0] + 1, 1, a_hi, a_lo, KT)
                    gemm_loop(U_F1[0], n, a_hi, a_lo, KT, first=1)
                else:
                    gemm_loop(U_F1[gi], n, a_hi, a_lo, KT)
                f += n
                gemm_loop(U_F2[gi], KT, b_hi, b_lo, n,
                          lambda k: k == n - 1 and pe.wait_ge(f_lo, f))
            embedding(N_3, Q_3, U_PLE2, 1)

        @block.vector
        def _(dve):
            tt = nc.vector.tensor_tensor
            ts = nc.vector.tensor_scalar
            stt = nc.vector.scalar_tensor_tensor
            steps = [0]

            def step(ins):
                ins.then_inc(dve_step, 1)
                steps[0] += 1
                dve.wait_ge(dve_step, steps[0])

            def col(name, j=0, n=1):
                return vec[:, bass.ds(VEC[name] + j, n)]

            def dcol(name, j=0, n=1):
                return der[:, bass.ds(DER[name] + j, n)]

            def leave(u, dst, first=0):
                for hf in range(2):
                    dve.wait_ge(acc_full, half_no(u, hf))
                    tt(dst[:, first + hf * HALF:first + (hf + 1) * HALF], ps[:, hf, :],
                       rstd[:, hf * HALF:(hf + 1) * HALF], ALU.mult).then_inc(acc_free, 1)

            def prep(q, k, gain, xk):
                dve.wait_ge(h_hi, q + k + 1)
                stt(a_lo[:, k, :], xk, gain, a_hi[:, k, :].bitcast(F32), ALU.mult,
                    ALU.subtract).then_inc(h_lo, 1)
                dve.wait_ge(sq_ready, q + k + 1)
                if q + k:
                    dve.wait_ge(ss_ready, q + k)
                tt(ss[:, :], ss[:, :], sq[:, k % 2, 0:T], ALU.add).then_inc(ss_ready, 1)

            def st_inverse(n, ncols, scale):
                dve.wait_ge(st_sum, n + 1)
                ts(sm[:, 1, 0:ncols], ps[:, 7, 0:ncols], scale, EPS, ALU.mult, ALU.add).then_inc(st_var, 1)
                dve.wait_ge(st_root, n + 1)
                nc.vector.reciprocal(sm[:, 3, 0:ncols], sm[:, 2, 0:ncols]).then_inc(st_inv, 1)

            dve.wait_ge(param_in, 48)
            step(tt(dcol("fin_n1", 0, 8), col("final", 0, 8), col("norm1", 0, 8), ALU.mult))
            step(ts(dcol("subln"), col("subln"), 1.0 - LAMBDA_INIT, None, ALU.mult))
            step(ts(dcol("qn"), col("qn"), 0.125, None, ALU.mult))
            step(tt(dcol("lamp"), col("lam", 0), col("lam", 1), ALU.mult))
            tt(dcol("lamp", 1), col("lam", 2), col("lam", 3), ALU.mult).then_inc(lam_ready, 1)
            step(tt(dcol("lb", 0, 8), col("gamma0", 0, 8), col("gamma1", 0, 8), ALU.max))
            step(tt(dcol("g0", 0, 8), col("gamma0", 0, 8), dcol("lb", 0, 8), ALU.subtract))
            tt(dcol("g1", 0, 8), col("gamma1", 0, 8), dcol("lb", 0, 8), ALU.subtract).then_inc(g_ready, 1)
            dve.wait_ge(lam_exp, 1)
            step(tt(dcol("g1", 0, 8), dcol("g0", 0, 8), dcol("g1", 0, 8), ALU.add))
            step(nc.vector.reciprocal(dcol("g1", 0, 8), dcol("g1", 0, 8)))
            step(tt(dcol("lb", 0, 8), dcol("g0", 0, 8), dcol("g1", 0, 8), ALU.mult))
            step(ts(dcol("omlb", 0, 8), dcol("lb", 0, 8), -1.0, 1.0, ALU.mult, ALU.add))
            step(stt(dcol("neg_lam"), dcol("lame", 1), LAMBDA_INIT, dcol("lame", 0), ALU.subtract,
                     ALU.subtract))

            step(nc.vector.memset(ss[:, :], 0.0))
            for k in range(KT):
                dve.wait_ge(x_in[k], 16)
                prep(Q_MIX, k, col("norm_mix", k), x[:, k, :])
            st_inverse(N_MIX, 8, 1.0 / T)

            dve.wait_ge(pos_in, 32)
            step(nc.vector.tensor_copy(ang[:, :], posi[:, :]))
            step(ts(ang[:, :], ang[:, :], invf, None, ALU.mult))
            for n, (dst, off) in enumerate(((sinm, 0.0), (cosm, 0.25))):
                step(ts(ang2[:, :], ang[:, :], float(np.float32(1.0 / TWO_PI)), off, ALU.mult, ALU.add))
                step(ts(ang2[:, :], ang2[:, :], MAGIC, None, ALU.add))
                step(ts(ang2[:, :], ang2[:, :], MAGIC, None, ALU.subtract))
                step(stt(dst[:, :], ang2[:, :], -TURN[0], ang[:, :], ALU.mult, ALU.add))
                for part in TURN[1:]:
                    step(stt(dst[:, :], ang2[:, :], -part, dst[:, :], ALU.mult, ALU.add))
                step(ts(dst[:, :], dst[:, :], float(off * TWO_PI), 3.1415925, ALU.add, ALU.min))
                ts(dst[:, :], dst[:, :], -3.1415925, None, ALU.max).then_inc(ang_ready, 1)
            dve.wait_ge(cs_ready, 2)
            dve.wait_ge(rstd_ready, 1)

            def row_max(h, qt):
                g = KT * h + qt
                for m in range(2):
                    dve.wait_ge(scored, 2 * g + m + 1)
                    step(nc.vector.reduce_max(rows[:, m, 0:1], banks(2 + 2 * m), AX_X))
                    if g:
                        dve.wait_ge(exp_done, 2 * (g - 1) + m + 1)
                    ts(rows[:, m, 1:2], rows[:, m, 0:1], -0.125, None, ALU.mult).then_inc(max_ready, 1)

            def combine(h, qt):
                g = KT * h + qt
                r = g % 2
                dve.wait_ge(exp_done, 2 * g + 2)
                step(nc.vector.reciprocal(rows[:, r, 4:6], rows[:, r, 2:4]))
                step(tt(rows[:, r, 6:7], rows[:, r, 5:6], dcol("neg_lam"), ALU.mult))
                step(ts(de[:, r, 0, :], de[:, r, 0, :], rows[:, r, 4:5], None, ALU.mult))
                stt(de[:, r, 0, :], de[:, r, 1, :], rows[:, r, 6:7], de[:, r, 0, :], ALU.mult,
                    ALU.add).then_inc(w_ready, 1)

            for h in range(HEADS):
                u = U_DA + 3 * h
                leave(u, dq[:, 0, :])
                leave(u + 1, dq[:, 1, :])
                leave(u + 2, dv[:, :])
                for t in range(2):
                    dve.wait_ge(swapped, 2 * h + t + 1)
                    step(tt(dtmp[:, :], banks(2 + 2 * t), sinm[:, :], ALU.mult))
                    step(tt(dq[:, t, :], dq[:, t, :], cosm[:, :], ALU.mult))
                    tt(dq[:, t, :], dq[:, t, :], dtmp[:, :], ALU.add).then_inc(qk_ready, 1)
                    if t == 0:
                        dve.wait_ge(qk_ready, 2 * h + 1)
                for qt in range(KT + 1):
                    if qt < KT:
                        row_max(h, qt)
                    if qt:
                        combine(h, qt - 1)
                st_inverse(N_DA + h, 8, 1.0 / P)
                dve.wait_ge(st_bc, N_DA + h + 1)
                stt(mix[:, h, :], mix[:, h, :], dcol("subln"), banks(2), ALU.mult,
                    ALU.mult).then_inc(mix_ready, 1)

            dve.wait_ge(mix_ready, HEADS)
            step(nc.vector.memset(hkt[:, 0, :], 0.0))
            step(nc.vector.memset(hkt[:, 1, :], 0.0))
            step(nc.vector.memset(reset[:, :], 1.0))
            step(nc.vector.memset(reset[:, :].rearrange("p (c t) -> p c t", t=P)[:, :, 0:1], 0.0))

            def chunks(buf, size):
                return buf.rearrange("p (n t) -> p n t", t=size)

            for h in range(HEADS):
                u = U_HG + 5 * h
                leave(u, hq[:, :])
                leave(u + 1, hz[:, 0, :])
                leave(u + 2, hz[:, 1, :])
                leave(u + 3, hv[:, :])
                leave(u + 4, hg[:, :])
                for d in range(2):
                    j = HEADS * d + h
                    dve.wait_ge(sig_done, 4 * h + 2 * d + 2)
                    ts(hd[:, d, :], hd[:, d, :], dcol("omlb", j), dcol("lb", j), ALU.mult,
                       ALU.add).then_inc(f_ready, 1)
                    step(ts(hk[:, d, :], hk[:, d, :], dcol("omlb", j), None, ALU.mult))
                for d in range(2):
                    dve.wait_ge(logf_done, 2 * h + d + 1)
                    if d == 0:
                        step(nc.vector.tensor_tensor_scan(hz[:, d, :], reset[:, :], hd[:, d, :], 0.0,
                                                          ALU.mult, ALU.add))
                    else:
                        step(nc.vector.tensor_tensor_scan(hz[:, d, ::-1], reset[:, :], hd[:, d, ::-1], 0.0,
                                                          ALU.mult, ALU.add))
                tt(hd[:, 0, :], hk[:, 0, :], hk[:, 1, :], ALU.add).then_inc(qk_lvl, 1)
                dve.wait_ge(lvl_mm, 15 * h + 1)
                tt(chunks(hatt[:, :], P), banks(4).rearrange("p (n t) -> p n t", t=P),
                   ident[:, :].rearrange("p (o t) -> p o t", o=1).to_broadcast([P, KT, P]),
                   ALU.mult).then_inc(att_put, 1)

                def halves(l, d):
                    hs = 1 << (l // 2)
                    lower, upper = slice(0, hs), slice(hs, 2 * hs)
                    return (2 * hs, upper, lower, hs - 1) if d == 0 else (2 * hs, lower, upper, hs)

                def distances(l):
                    d = l % 2
                    size, _, _, ref = halves(l, d)
                    b = chunks(hz[:, d, :], size)
                    if l >= 2:
                        dve.wait_ge(qk_lvl, 15 * h + l)
                    tt(chunks(hd[:, d, :], size), b, b[:, :, ref:ref + 1].to_broadcast([P, T // size, size]),
                       ALU.subtract).then_inc(d_ready, 1)

                def operands(l):
                    d = l % 2
                    n = 15 * h + 1 + l
                    size, qs, ks, _ = halves(l, d)
                    dve.wait_ge(e_done, 34 * h + 2 * l + 2)
                    if l >= 2:
                        dve.wait_ge(lvl_mm, n - 1)
                    e = chunks(hd[:, d, :], size)
                    tt(chunks(hqt[:, d, :], size // 2), chunks(hq[:, :], size)[:, :, qs], e[:, :, qs],
                       ALU.mult)
                    tt(chunks(hkt[:, d, :], size)[:, :, ks], chunks(hk[:, d, :], size)[:, :, ks], e[:, :, ks],
                       ALU.mult).then_inc(qk_lvl, 1)

                def put(l):
                    d = l % 2
                    n = 15 * h + 1 + l
                    size, qs, _, _ = halves(l, d)
                    dve.wait_ge(lvl_mm, n + 1)
                    dve.wait_ge(att_put, n)
                    nt = P // size
                    mask = (hmask[:, l, :].rearrange("p (o n t) -> p o n t", o=1, n=nt)
                            .to_broadcast([P, KT, nt, size // 2]))
                    out = hatt[:, :].rearrange("p (c n t) -> p c n t", c=KT, n=nt)[:, :, :, qs]
                    data = ps[:, 4 + d, :].rearrange("p (c n t) -> p c n t", c=KT, n=nt)
                    nc.vector.copy_predicated(out, mask, data).then_inc(att_put, 1)

                dve.wait_ge(hmask_in, 16)
                nl = 2 * LEVELS
                for l in range(nl + 2):
                    if l < nl:
                        distances(l)
                    if 1 <= l <= nl:
                        operands(l - 1)
                    if l >= 2:
                        put(l - 2)

                for d in range(2):
                    b = chunks(hz[:, d, :], P)
                    ref = P - 1 if d == 0 else 0
                    dve.wait_ge(qk_lvl, 15 * h + 15)
                    tt(chunks(hd[:, d, :], P), b, b[:, :, ref:ref + 1].to_broadcast([P, KT, P]),
                       ALU.subtract).then_inc(d_ready, 1)
                for d in range(2):
                    dve.wait_ge(e_done, 34 * h + 28 + 3 * d + 1)
                    dve.wait_ge(lvl_mm, 15 * h + 15)
                    tt(hkt[:, d, :], hk[:, d, :], hd[:, d, :], ALU.mult).then_inc(kd_ready, 1)
                dve.wait_ge(kd_ready, 2 * h + 2)
                for d in range(2):
                    n = 2 * h + d
                    dve.wait_ge(kv_mm, n + 1)
                    order = range(KT) if d == 0 else range(KT - 1, -1, -1)
                    order = list(order)
                    for a, c in zip(order[:-1], order[1:]):
                        kv = ps[:, 4 + a // 4, (a % 4) * P:(a % 4 + 1) * P]
                        dst = hk[:, d, c * P:(c + 1) * P]
                        if a == order[0]:
                            ins = nc.vector.tensor_copy(dst, kv)
                        else:
                            if a == order[1]:
                                dve.wait_ge(e_done, 34 * h + 28 + 3 * d + 2)
                            ins = stt(dst, hk[:, d, a * P:(a + 1) * P], heb[:, d, a:a + 1], kv, ALU.mult,
                                      ALU.add)
                        if c == order[-1]:
                            ins.then_inc(state_ready, 1)
                        else:
                            step(ins)
                for d in range(2):
                    dve.wait_ge(e_done, 34 * h + 28 + 3 * d + 3)
                    tt(hz[:, d, :], hq[:, :], hd[:, d, :], ALU.mult).then_inc(qd_ready, 1)

                st_inverse(N_HG + h, 8, 1.0 / P)
                dve.wait_ge(st_bc, N_HG + h + 1)
                step(stt(mix[:, HEADS + h, :], mix[:, HEADS + h, :], col("hgn"), banks(4), ALU.mult,
                         ALU.mult))
                dve.wait_ge(silu_done, h + 1)
                tt(mix[:, HEADS + h, :], mix[:, HEADS + h, :], hg[:, :], ALU.mult).then_inc(mix_ready, 1)


            def split_mix(f0, m0):
                dve.wait_ge(mix_ready, m0 + KT)
                for k in range(KT):
                    dve.wait_ge(f_hi, f0 + k + 1)
                    tt(b_lo[:, k, :], mix[:, k, :], b_hi[:, k, :].bitcast(F32),
                       ALU.subtract).then_inc(f_lo, 1)

            def add_to_x(u, k):
                for hf in range(2):
                    c = slice(hf * HALF, (hf + 1) * HALF)
                    dve.wait_ge(acc_full, half_no(u, hf))
                    tt(x[:, k, c], ps[:, hf, :], x[:, k, c], ALU.add).then_inc(acc_free, 1)

            def out_projection(u0, f0, m0, turn, q, gain):
                split_mix(f0, m0)
                step(nc.vector.memset(ss[:, :], 0.0))
                for k in range(KT):
                    dve.wait_ge(x_in[k], 16 * turn)
                    add_to_x(u0 + k, k)
                    dve.wait_ge(acc_free, half_no(u0 + k, 1))
                    prep(q, k, col(gain, k), x[:, k, :])

            def down(u0, last, q=0, gain=None):
                if not last:
                    with dve.Fori(0, KT, 1) as i:
                        for hf in range(2):
                            dve.wait_ge(acc_full, half_no(u0 + i, hf))
                            xk = x[:, bass.ds(i, 1), hf * HALF:(hf + 1) * HALF].rearrange("p a b -> p (a b)")
                            tt(xk, ps[:, hf, :], xk, ALU.add).then_inc(acc_free, 1)
                    return
                step(nc.vector.memset(ss[:, :], 0.0))
                for k in range(KT):
                    add_to_x(u0 + k, k)
                    dve.wait_ge(acc_free, half_no(u0 + k, 1))
                    prep(q, k, col(gain, k), x[:, k, :])

            out_projection(U_OUT, F_MIX, 0, 2, Q_FFN, "norm_ffn")
            st_inverse(N_FFN, 8, 1.0 / T)
            dve.wait_ge(ss_ready, Q_FFN + KT)
            for s in range(2):
                step(nc.vector.memset(pad_a[:, s, 0:1], 0.0))
                step(nc.vector.memset(pad_a[:, s, T + 1:T + 2], 0.0))
            dve.wait_ge(rstd_ready, 2)

            def hidden_tile(u, s, f, fi):
                if not (isinstance(fi, int) and fi < 2):
                    dve.wait_ge(f_lo, f - 1)
                leave(u, pad_a[:, s, :], 1)
                dve.wait_ge(acc_free, half_no(u, 1))
                ts(c_buf[:, :], pad_a[:, s, 0:T], col("conv_w0", fi), col("conv_b", fi), ALU.mult,
                   ALU.add).then_inc(conv_done, 1)
                dve.wait_ge(conv_done, 3 * fi + 1)
                stt(c_buf[:, :], pad_a[:, s, 1:T + 1], col("conv_w1", fi), c_buf[:, :], ALU.mult,
                    ALU.add).then_inc(conv_done, 1)
                dve.wait_ge(conv_done, 3 * fi + 2)
                stt(c_buf[:, :], pad_a[:, s, 2:T + 2], col("conv_w2", fi), c_buf[:, :], ALU.mult,
                    ALU.add).then_inc(conv_done, 1)
                dve.wait_ge(conv_done, 3 * fi + 3)
                leave(u + 1, pad_a[:, s, :], 1)
                dve.wait_ge(acc_free, half_no(u + 1, 1))
                dve.wait_ge(act_done, fi + 1)
                tt(pad_a[:, s, 1:T + 1], c_buf[:, :], pad_a[:, s, 1:T + 1], ALU.mult).then_inc(fx_ready, 1)

            def remainder(f, s, j, first):
                dve.wait_ge(f_hi, f + 1)
                lo = b_lo[:, bass.ds(j, 1), :].rearrange("p a b -> p (a b)")
                hi = b_hi[:, bass.ds(j, 1), :].rearrange("p a b -> p (a b)").bitcast(F32)
                tt(lo, pad_a[:, s, first:first + T], hi, ALU.subtract).then_inc(f_lo, 1)

            fi = 0
            for gi, n in enumerate(GROUPS1):
                def pair(i):
                    for s in range(2):
                        t = fi + 2 * i + s
                        hidden_tile(U_GU[gi] + 4 * i + 2 * s, s, F_FF + t, t)
                        remainder(F_FF + t, s, 2 * i + s, 1)
                if gi == 0:
                    pair(0)
                with dve.Fori(1 if gi == 0 else 0, n // 2, 1) as i:
                    pair(i)
                fi += n
                down(U_DN[gi], gi == len(GROUPS1) - 1, Q_PLE, "norm_ple")
            st_inverse(N_PLE, 8, 1.0 / T)

            def embedding(u0, turn, rs):
                for k in range(PT):
                    dve.wait_ge(p_hi, 2 * turn + k + 1)
                    tt(b_lo[:, k, :], p_raw[:, k, :], b_hi[:, k, :].bitcast(F32),
                       ALU.subtract).then_inc(p_lo, 1)
                dve.wait_ge(rstd_ready, rs)
                dve.wait_ge(ss_ready, Q_PLE + KT if turn == 0 else Q_3 + KT)
                with dve.Fori(0, KT, 1) as i:
                    leave(u0 + 2 * i, pad_a[:, 0, :])
                    for hf in range(2):
                        dve.wait_ge(acc_full, half_no(u0 + 2 * i + 1, hf))
                        dve.wait_ge(pg_sig, KT * turn + i + 1)
                        tt(c_buf[:, hf * HALF:(hf + 1) * HALF], ps[:, hf, :],
                           pad_a[:, 0, hf * HALF:(hf + 1) * HALF], ALU.mult).then_inc(acc_free, 1)
                    dve.wait_ge(acc_free, half_no(u0 + 2 * i + 1, 1))
                    xk = x[:, bass.ds(i, 1), :].rearrange("p a b -> p (a b)")
                    tt(xk, xk, c_buf[:, :], ALU.add).then_inc(x_done, 1)
                    dve.wait_ge(x_done, KT * turn + i + 1)

            embedding(U_PLE, 0, 3)

            dve.wait_ge(x_done, KT)
            step(nc.vector.memset(ss[:, :], 0.0))
            step(nc.vector.memset(c_buf[:, :], 0.0))
            for k in range(KT):
                dve.wait_ge(h_hi, Q_1 + k + 1)
                stt(a_lo[:, k, :], x[:, k, :], dcol("fin_n1", k), a_hi[:, k, :].bitcast(F32), ALU.mult,
                    ALU.subtract).then_inc(h_lo, 1)
                dve.wait_ge(sq_ready, Q_1 + k + 1)
                dve.wait_ge(ss_ready, Q_1 + k)
                tt(ss[:, :], ss[:, :], sq[:, 0, 0:T], ALU.add).then_inc(ss_ready, 1)
                dve.wait_ge(sq2_ready, k + 1)
                if k:
                    dve.wait_ge(s2_ready, k)
                tt(c_buf[:, :], c_buf[:, :], sq[:, 1, 0:T], ALU.add).then_inc(s2_ready, 1)
            dve.wait_ge(st_sum, N_FIN + 1)
            ts(sm[:, 1, 0:8], ps[:, 7, 0:8], 1.0 / T, EPS, ALU.mult, ALU.add).then_inc(st_var, 1)
            dve.wait_ge(st_root, N_FIN + 1)
            nc.vector.reciprocal(sm[:, 0, 0:8], sm[:, 2, 0:8]).then_inc(st_inv, 1)
            dve.wait_ge(st_inv, N_FIN + 1)
            dve.wait_ge(st_sum, N_1 + 1)
            step(stt(sm[:, 1, 0:8], ps[:, 7, 0:8], 1.0 / T, sm[:, 0, 0:8], ALU.mult, ALU.mult))
            step(tt(sm[:, 1, 0:8], sm[:, 1, 0:8], sm[:, 0, 0:8], ALU.mult))
            ts(sm[:, 1, 0:8], sm[:, 1, 0:8], EPS, None, ALU.add).then_inc(st_var, 1)
            dve.wait_ge(st_root, N_1 + 1)
            step(nc.vector.reciprocal(sm[:, 3, 0:8], sm[:, 2, 0:8]))
            tt(sm[:, 3, 0:8], sm[:, 3, 0:8], sm[:, 0, 0:8], ALU.mult).then_inc(st_inv, 1)
            dve.wait_ge(st_bc, N_FIN + 2)
            for k in range(KT):
                stt(x[:, k, :], x[:, k, :], col("final", k), banks(5), ALU.mult,
                    ALU.mult).then_inc(xf_ready, 1)
            dve.wait_ge(rstd_ready, 4)

            def place(n):
                th, i, hh = PIECES[n]
                return th, i, hh, max(0, i - 4 * th) * P

            def z_leaves(p, n):
                _, _, _, c0 = place(n)
                s = NPC * p + n
                dve.wait_ge(z_mm, s + 1)
                if s >= 4:
                    dve.wait_ge(sw_exp, s - 3)
                nc.vector.tensor_copy(sz[:, s % 4, c0:], ps[:, 2 + s % 2, c0:]).then_inc(z_out, 1)

            def softplus(p, n):
                th, i, _, c0 = place(n)
                s = NPC * p + n
                dve.wait_ge(l_ready, s + 1)
                if s >= 4:
                    dve.wait_ge(sph_ready, s - 3)
                ins = stt(sp[:, s % 4, c0:], sz[:, s % 4, c0:], 0.0, sl[:, s % 4, c0:], ALU.max, ALU.add)
                if i >= 4 * th:
                    step(ins)
                    ins = tt(sp[:, s % 4, c0:c0 + P], sp[:, s % 4, c0:c0 + P], ctri, ALU.mult)
                ins.then_inc(sp_ready, 1)
                dve.wait_ge(sp_ready, s + 1)
                dve.wait_ge(sph_ready, s + 1)
                if s >= 4:
                    dve.wait_ge(suf_mm, s - 1)
                tt(spl[:, s % 4, c0:], sp[:, s % 4, c0:], sph[:, s % 4, c0:].bitcast(F32),
                   ALU.subtract).then_inc(spl_ready, 1)

            def exponent(p, n):
                th, i, hh, c0 = place(n)
                s = NPC * p + n
                dve.wait_ge(suf_mm, s + 1)
                ins = tt(sz[:, s % 4, c0:], sz[:, s % 4, c0:], ps[:, 4 + hh, c0:], ALU.add)
                if i >= 4 * th:
                    step(ins)
                    ins = ts(sz[:, s % 4, c0:c0 + P], sz[:, s % 4, c0:c0 + P], 0.0, None, ALU.min)
                ins.then_inc(t_ready, 1)

            def causal(p, n):
                th, i, _, c0 = place(n)
                s = NPC * p + n
                if i >= 4 * th:
                    dve.wait_ge(sw_exp, s + 1)
                    tt(sw[:, s % 4, c0:c0 + P], sw[:, s % 4, c0:c0 + P], ctri, ALU.mult).then_inc(sw_ready, 1)

            for p in range(HEADS):
                u = U_SB + 3 * p
                leave(u, sk[:, 0, :])
                leave(u + 1, sk[:, 1, :])
                leave(u + 2, sv[:, :])
                for t, gain in enumerate((dcol("qn"), col("kn"))):
                    n = N_QK + 2 * p + t
                    st_inverse(n, 16, 1.0 / 64)
                    dve.wait_ge(st_bc, n + 1)
                    stt(sk[:, t, :], sk[:, t, :], gain, banks(4), ALU.mult, ALU.mult).then_inc(qk2_ready, 1)
                for n in range(NPC + 3):
                    if n < NPC:
                        z_leaves(p, n)
                    if 1 <= n <= NPC:
                        softplus(p, n - 1)
                    if 2 <= n <= NPC + 1:
                        exponent(p, n - 2)
                    if n >= 3:
                        causal(p, n - 3)

            dve.wait_ge(so_out, 4 * HEADS)
            step(nc.vector.memset(cp[:, 0:2], 0.0))
            for j in range(2):
                u = U_CV + 3 * j
                if j:
                    dve.wait_ge(mix_ready, 2 * HEADS + j)
                for n in range(3):
                    leave(u + n, cc[:, n, :])
                dve.wait_ge(acc_free, half_no(u + 2, 1))
                step(tt(cp[:, 2:T + 2], cc[:, 0, :], cc[:, 1, :], ALU.mult))
                step(ts(cc[:, 0, :], cp[:, 0:T], col("conv2_w0", j), None, ALU.mult))
                step(stt(cc[:, 0, :], cp[:, 1:T + 1], col("conv2_w1", j), cc[:, 0, :], ALU.mult, ALU.add))
                step(stt(cc[:, 0, :], cp[:, 2:T + 2], col("conv2_w2", j), cc[:, 0, :], ALU.mult, ALU.add))
                tt(mix[:, j, :], cc[:, 0, :], cc[:, 2, :], ALU.mult).then_inc(mix_ready, 1)

            dve.wait_ge(gate_in, 48)
            tt(gw[:, :, :], gw[:, :, :], gmask[:, :].rearrange("p (o t) -> p o t", o=1)
               .to_broadcast([P, 4, P]), ALU.mult).then_inc(gw_ready, 1)
            for j in range(2):
                u = U_SG + 2 * j
                if j:
                    dve.wait_ge(mix_ready, 2 * HEADS + 2 + j)
                leave(u, gv[:, 0, :])
                leave(u + 1, gv[:, 1, :])
                st_inverse(N_SG + j, 16, 1.0 / 64)
                dve.wait_ge(st_bc, N_SG + j + 1)
                stt(gv[:, 0, :], gv[:, 0, :], col("sgu_g", j), banks(4), ALU.mult,
                    ALU.mult).then_inc(gn_ready, 1)
                dve.wait_ge(gs_mm, j + 1)
                for hh in range(2):
                    r = slice(64 * hh, 64 * hh + 64)
                    tt(chunks(mix[r, 6 + j, :], P), banks(4 + 2 * hh)[r, :].rearrange("p (n t) -> p n t", t=P),
                       gb[r, j, :].rearrange("p (o t) -> p o t", o=1).to_broadcast([64, KT, P]),
                       ALU.add).then_inc(g_done, 1)
                dve.wait_ge(g_done, 2 * j + 2)
                dve.wait_ge(gelu_done, 2 * j + 2)
                tt(mix[:, 6 + j, :], mix[:, 6 + j, :], gv[:, 1, :], ALU.mult).then_inc(mix_ready, 1)

            out_projection(U_OUT2, F_MIX2, 2 * HEADS - 4, 3, Q_2, "norm2")
            st_inverse(N_2, 8, 1.0 / T)
            dve.wait_ge(ss_ready, Q_2 + KT)
            dve.wait_ge(rstd_ready, 5)

            def hidden2(u, s, f, fi):
                if not (isinstance(fi, int) and fi < 2):
                    dve.wait_ge(f_lo, f - 1)
                if not (isinstance(fi, int) and fi < 1):
                    dve.wait_ge(fx_ready, FT + fi)
                leave(u, c_buf[:, :])
                dve.wait_ge(acc_free, half_no(u, 1))
                stt(pad_a[:, s, 0:T], c_buf[:, :], 0.0, c_buf[:, :], ALU.max, ALU.mult).then_inc(fx_ready, 1)
                dve.wait_ge(fx_ready, FT + fi + 1)

            fi = 0
            for gi, n in enumerate(GROUPS2):
                def pair2(i):
                    for s in range(2):
                        t = fi + 2 * i + s
                        hidden2(U_F1[gi] + 2 * i + s, s, F_FF2 + t, t)
                        remainder(F_FF2 + t, s, 2 * i + s, 0)
                if gi == 0:
                    pair2(0)
                with dve.Fori(1 if gi == 0 else 0, n // 2, 1) as i:
                    pair2(i)
                fi += n
                down(U_F2[gi], gi == len(GROUPS2) - 1, Q_3, "norm3")
            st_inverse(N_3, 8, 1.0 / T)
            embedding(U_PLE2, 1, 6)

        @block.scalar
        def _(act):
            def av(out, in_, f, **kw):
                return nc.scalar.activation(out, in_, f, **kw)

            steps = [0]

            def step(ins):
                ins.then_inc(act_step, 1)
                steps[0] += 1
                act.wait_ge(act_step, steps[0])

            def until(sem_, value):
                act.wait_ge(sem_, value)
                act.wait_ge(param_in, 48)

            def col(name, j=0, n=1):
                return vec[:, VEC[name] + j:VEC[name] + j + n]

            def dcol(name, j=0, n=1):
                return der[:, DER[name] + j:DER[name] + j + n]

            def prep(q, k, gain, xk):
                av(a_hi[:, k, :], xk, ACT.Copy, scale=gain).then_inc(h_hi, 1)
                if q + k >= 2:
                    act.wait_ge(ss_ready, q + k - 1)
                av(sq[:, k % 2, 0:T], xk, ACT.Square).then_inc(sq_ready, 1)

            def st_sqrt(n, ncols):
                act.wait_ge(st_var, n + 1)
                av(sm[:, 2, 0:ncols], sm[:, 1, 0:ncols], ACT.Sqrt).then_inc(st_root, 1)

            def keep_rstd(bc):
                act.wait_ge(st_bc, bc)
                av(rstd[:, :], banks(5), ACT.Copy).then_inc(rstd_ready, 1)

            act.wait_ge(g_ready, 1)
            step(av(dcol("g0", 0, 8), dcol("g0", 0, 8), ACT.Exp))
            step(av(dcol("g1", 0, 8), dcol("g1", 0, 8), ACT.Exp))
            act.wait_ge(lam_mm, 1)
            av(dcol("lame", 0, 2), ps[:, 7, 0:2], ACT.Exp).then_inc(lam_exp, 1)
            act.wait_ge(param_in, 48)
            for k in range(KT):
                act.wait_ge(x_in[k], 16)
                prep(Q_MIX, k, col("norm_mix", k), x[:, k, :])
            st_sqrt(N_MIX, 8)
            keep_rstd(N_MIX + 1)
            for n, m in enumerate((sinm, cosm)):
                act.wait_ge(ang_ready, n + 1)
                av(m[:, :], m[:, :], ACT.Sin).then_inc(cs_ready, 1)

            def exps(h, qt):
                g = KT * h + qt
                for m in range(2):
                    act.wait_ge(max_ready, 2 * g + m + 1)
                    if g >= 2:
                        act.wait_ge(w_tr, 2 * (g - 1))
                    av(de[:, g % 2, m, :], banks(2 + 2 * m), ACT.Exp, scale=0.125, bias=rows[:, m, 1:2],
                       accum_out=rows[:, g % 2, 2 + m:3 + m]).then_inc(exp_done, 1)

            def turned(h, qt):
                g = KT * h + qt
                for r in range(2):
                    act.wait_ge(w_tr, 2 * g + r + 1)
                    if g:
                        act.wait_ge(o_mm, g)
                    av(dwt[:, r, :], ps[:, 6, :], ACT.Copy).then_inc(wt_ready, 1)
                if qt in (3, 7):
                    act.wait_ge(o_mm, g + 1)
                    hf = qt // 4
                    av(mix[:, h, hf * HALF:(hf + 1) * HALF], ps[:, 7, :], ACT.Copy).then_inc(o_out, 1)

            for h in range(HEADS):
                act.wait_ge(v_tr, h + 1)
                av(dvt[:, :, :], banks(6).rearrange("p (c e) -> p c e", c=KT), ACT.Copy).then_inc(v_ready, 1)
                for qt in range(KT + 1):
                    if qt < KT:
                        exps(h, qt)
                    if qt:
                        turned(h, qt - 1)
                act.wait_ge(o_out, 2 * h + 2)
                av(ang[:, :], mix[:, h, :], ACT.Square).then_inc(o_sq, 1)
                st_sqrt(N_DA + h, 8)

            act.wait_ge(mix_ready, HEADS)
            act.dma_start(hmask[:, :, :], io["hmask"]).then_inc(hmask_in, 16)
            for h in range(HEADS):
                u = U_HG + 5 * h
                for d in range(2):
                    act.wait_ge(acc_free, half_no(u + 1 + d, 1))
                    av(hd[:, d, :], hz[:, d, :], ACT.Sigmoid).then_inc(sig_done, 1)
                    av(hk[:, d, :], hz[:, d, :], ACT.Sigmoid, scale=-1.0).then_inc(sig_done, 1)
                for d in range(2):
                    act.wait_ge(f_ready, 2 * h + d + 1)
                    av(hd[:, d, :], hd[:, d, :], ACT.Ln).then_inc(logf_done, 1)
                act.wait_ge(v_tr, HEADS + h + 1)
                av(hvt[:, :, :], banks(2).rearrange("p (c e) -> p c e", c=KT), ACT.Copy).then_inc(v_ready, 1)
                for l in range(2 * LEVELS):
                    d = l % 2
                    hs = 1 << (l // 2)
                    lower, upper = slice(0, hs), slice(hs, 2 * hs)
                    qs, ks = (upper, lower) if d == 0 else (lower, upper)
                    act.wait_ge(d_ready, 16 * h + l + 1)
                    e = hd[:, d, :].rearrange("p (n t) -> p n t", t=2 * hs)
                    av(e[:, :, qs], e[:, :, qs], ACT.Exp).then_inc(e_done, 1)
                    av(e[:, :, ks], e[:, :, ks], ACT.Exp, scale=-1.0).then_inc(e_done, 1)
                for d in range(2):
                    ref = P - 1 if d == 0 else 0
                    act.wait_ge(d_ready, 16 * h + 14 + d + 1)
                    av(hd[:, d, :], hd[:, d, :], ACT.Exp, scale=-1.0).then_inc(e_done, 1)
                    far = hz[:, d, :].rearrange("p (c t) -> p c t", t=P)[:, :, ref:ref + 1]
                    av(heb[:, d, :].rearrange("p (c t) -> p c t", t=1), far, ACT.Exp).then_inc(e_done, 1)
                    act.wait_ge(kd_ready, 2 * h + d + 1)
                    av(hd[:, d, :], hz[:, d, :], ACT.Exp).then_inc(e_done, 1)
                for d in range(2):
                    act.wait_ge(kd_tr, 2 * h + d + 1)
                    if d:
                        act.wait_ge(kv_mm, 2 * h + 1)
                    av(hkd[:, :, :], banks(2).rearrange("p (c e) -> p c e", c=KT),
                       ACT.Copy).then_inc(kdt_ready, 1)
                act.wait_ge(acc_free, half_no(u + 4, 1))
                av(hg[:, :], hg[:, :], ACT.Silu).then_inc(silu_done, 1)
                act.wait_ge(ho_mm, h + 1)
                av(mix[:, HEADS + h, :], banks(6), ACT.Copy).then_inc(ho_out, 1)
                act.wait_ge(ho_out, h + 1)
                av(hv[:, :], mix[:, HEADS + h, :], ACT.Square).then_inc(o_sq, 1)
                st_sqrt(N_HG + h, 8)


            def split_mix(f0, m0, source):
                act.wait_ge(mix_ready, m0 + KT)
                for k in range(KT):
                    av(b_hi[:, k, :], mix[:, k, :], ACT.Copy).then_inc(f_hi, 1)
                for k in range(KT):
                    act.wait_ge(f_lo, f0 + k + 1)
                    act.dma_start(x[:, k, :], source[:, k, :]).then_inc(x_in[k], 16)

            def preps(q, u0, gain):
                for k in range(KT):
                    act.wait_ge(acc_free, half_no(u0 + k, 1))
                    prep(q, k, col(gain, k), x[:, k, :])

            def high(f, s, j, first, fx):
                until(fx_ready, fx)
                av(b_hi[:, bass.ds(j, 1), :].rearrange("p a b -> p (a b)"), pad_a[:, s, first:first + T],
                   ACT.Copy).then_inc(f_hi, 1)

            split_mix(F_MIX, 0, io["x"])
            preps(Q_FFN, U_OUT, "norm_ffn")
            st_sqrt(N_FFN, 8)
            keep_rstd(N_FFN + 1)
            fi = 0
            for gi, n in enumerate(GROUPS1):
                with act.Fori(0, n // 2, 1) as i:
                    for s in range(2):
                        t = fi + 2 * i + s
                        until(conv_done, 3 * t + 3)
                        av(c_buf[:, :], c_buf[:, :], ACT.Gelu).then_inc(act_done, 1)
                        high(F_FF + t, s, 2 * i + s, 1, t + 1)
                fi += n
            preps(Q_PLE, U_DN[-1], "norm_ple")
            st_sqrt(N_PLE, 8)

            def embedding(u0, turn, name, bc, u_last):
                act.wait_ge(acc_free, half_no(u_last + KT - 1, 1))
                act.dma_start(p_raw[:, :, :], io[name]).then_inc(p_in, 16)
                keep_rstd(bc)
                act.wait_ge(p_in, 16 * (turn + 1))
                for k in range(PT):
                    av(b_hi[:, k, :], p_raw[:, k, :], ACT.Copy).then_inc(p_hi, 1)
                with act.Fori(0, KT, 1) as i:
                    until(acc_free, half_no(u0 + 2 * i, 1))
                    av(pad_a[:, 0, 0:T], pad_a[:, 0, 0:T], ACT.Sigmoid).then_inc(pg_sig, 1)
                    if turn:
                        act.wait_ge(x_done, KT + i + 1)
                        act.dma_start(io["out"][:, bass.ds(i, 1), :], x[:, bass.ds(i, 1), :]).then_inc(out_done, 16)

            embedding(U_PLE, 0, "p", N_PLE + 1, U_DN[-1])

            act.wait_ge(x_done, KT)
            for k in range(KT):
                av(a_hi[:, k, :], x[:, k, :], ACT.Copy, scale=dcol("fin_n1", k)).then_inc(h_hi, 1)
                act.wait_ge(ss_ready, Q_1 + k)
                av(sq[:, 0, 0:T], x[:, k, :], ACT.Square).then_inc(sq_ready, 1)
                if k:
                    act.wait_ge(s2_ready, k)
                av(sq[:, 1, 0:T], x[:, k, :], ACT.Square, scale=col("final", k)).then_inc(sq2_ready, 1)
            st_sqrt(N_FIN, 8)
            st_sqrt(N_1, 8)
            keep_rstd(N_FIN + 1)
            act.dma_start(tri_raw[:, :, :], io["tri"]).then_inc(tri_in, 16)
            act.wait_ge(tri_in, 16)
            for n in range(2):
                av(tri[:, n, :], tri_raw[:, n, :], ACT.Copy).then_inc(tri_ready, 1)
            for k in range(KT):
                act.wait_ge(xf_ready, k + 1)
                act.dma_start(x_back[:, k, :], x[:, k, :]).then_inc(x_out, 16)

            def soft(p, n):
                th, i, _ = PIECES[n]
                c0 = max(0, i - 4 * th) * P
                s = NPC * p + n
                act.wait_ge(z_out, s + 1)
                if s >= 4:
                    act.wait_ge(sp_ready, s - 3)
                step(av(sl[:, s % 4, c0:], sz[:, s % 4, c0:], ACT.Abs))
                step(av(sl[:, s % 4, c0:], sl[:, s % 4, c0:], ACT.Exp, scale=-1.0))
                av(sl[:, s % 4, c0:], sl[:, s % 4, c0:], ACT.Ln, bias=1.0).then_inc(l_ready, 1)

            def sp_high(p, n):
                th, i, _ = PIECES[n]
                c0 = max(0, i - 4 * th) * P
                s = NPC * p + n
                act.wait_ge(sp_ready, s + 1)
                if s >= 4:
                    act.wait_ge(spl_ready, s - 3)
                    act.wait_ge(suf_mm, s - 1)
                av(sph[:, s % 4, c0:], sp[:, s % 4, c0:], ACT.Copy).then_inc(sph_ready, 1)

            def weight(p, n):
                th, i, hh = PIECES[n]
                c0 = max(0, i - 4 * th) * P
                s = NPC * p + n
                act.wait_ge(t_ready, s + 1)
                if s >= 4:
                    act.wait_ge(so_mm, s - 3)
                av(sw[:, s % 4, c0:], sz[:, s % 4, c0:], ACT.Exp).then_inc(sw_exp, 1)

            def out_rows(p, n):
                th, i, hh = PIECES[n]
                s = NPC * p + n
                if i == 0:
                    act.wait_ge(so_mm, s + 1)
                    r = slice(64 * hh, 64 * hh + 64)
                    av(mix[r, 2 + p, th * HALF:(th + 1) * HALF], ps[r, 6 + hh, :], ACT.Copy).then_inc(so_out, 1)

            for p in range(HEADS):
                u = U_SB + 3 * p
                for t in range(2):
                    act.wait_ge(acc_free, half_no(u + t, 1))
                    act.wait_ge(st_sum, N_QK + 2 * p + t)
                    av(c_buf[:, :], sk[:, t, :], ACT.Square).then_inc(sq_qk, 1)
                    st_sqrt(N_QK + 2 * p + t, 16)
                act.wait_ge(sv_tr, p + 1)
                av(svt[:, :, :], banks(2).rearrange("p (c e) -> p c e", c=KT), ACT.Copy).then_inc(sv_ready, 1)
                act.wait_ge(x_out, 16 * KT)
                for n in range(NPC + 4):
                    if n < NPC:
                        soft(p, n)
                    if 1 <= n <= NPC:
                        sp_high(p, n - 1)
                    if 2 <= n <= NPC + 1:
                        weight(p, n - 2)
                    if n >= 4:
                        out_rows(p, n - 4)

            act.wait_ge(so_out, 4 * HEADS)
            act.dma_start(gw[:, :, :], io["gw"]).then_inc(gate_in, 16)
            act.dma_start(gb[:, :, :], io["gb"]).then_inc(gate_in, 16)
            act.dma_start(gmask[:, :], io["gmask"]).then_inc(gate_in, 16)
            for j in range(2):
                u = U_SG + 2 * j
                for n in range(2):
                    act.wait_ge(acc_free, half_no(u + n, 1))
                    av(gv[:, n, :], gv[:, n, :], ACT.Gelu).then_inc(gelu_done, 1)
                    if n == 0:
                        act.wait_ge(gelu_done, 2 * j + 1)
                        act.wait_ge(st_sum, N_SG + j)
                        av(c_buf[:, :], gv[:, 0, :], ACT.Square).then_inc(g_sq, 1)
                st_sqrt(N_SG + j, 16)
                act.wait_ge(g_tr, j + 1)
                av(gvt[:, :, :], banks(2).rearrange("p (c e) -> p c e", c=KT), ACT.Copy).then_inc(gt_ready, 1)

            split_mix(F_MIX2, 2 * HEADS - 4, x_back)
            preps(Q_2, U_OUT2, "norm2")
            st_sqrt(N_2, 8)
            keep_rstd(N_2 + 1)
            fi = 0
            for gi, n in enumerate(GROUPS2):
                with act.Fori(0, n // 2, 1) as i:
                    for s in range(2):
                        t = fi + 2 * i + s
                        high(F_FF2 + t, s, 2 * i + s, 0, FT + t + 1)
                fi += n
            preps(Q_3, U_F2[-1], "norm3")
            st_sqrt(N_3, 8)
            embedding(U_PLE2, 1, "p2", N_3 + 1, U_F2[-1])


def constants():
    f = np.float32
    ident = np.eye(P, dtype=f)
    cst = np.zeros((P, 8), f)
    cst[:, 0] = 1.0
    cst[:64, 1] = 1.0
    cst[64:, 2] = 1.0
    half = 8
    freq = f(500000.0) ** (-np.arange(half, dtype=f) / f(half))
    swap = np.zeros((P, P), f)
    for m in range(2):
        for j in range(half):
            a, b = 64 * m + j, 64 * m + half + j
            cst[a, 3] = cst[b, 3] = freq[j]
            swap[b, a] = -1.0
            swap[a, b] = 1.0
    s = np.arange(P)[:, None]
    t = np.arange(P)[None, :]
    tri = np.stack([-(s >= t).astype(f), -(s < t).astype(f), (s < t).astype(f)], 1)
    mask = np.zeros((P, 2 * LEVELS, 64), np.int32)
    for l in range(2 * LEVELS):
        hs = 1 << (l // 2)
        for idx in range(64):
            blk = idx // hs
            lo = blk * 2 * hs + (0 if l % 2 == 0 else hs)
            mask[lo:lo + hs, l, idx] = 1
    return {"ident": ident, "cst": cst, "swap": swap, "tri": np.ascontiguousarray(tri), "hmask": mask,
            "gmask": (s <= t).astype(f)}


def kernel(**inputs):
    import concourse.bacc as bacc
    from concourse.bass_utils import run_bass_kernel_spmd

    v = {k: np.asarray(a) for k, a in inputs.items()}

    def tiles(w, order=None):
        kt, nt = w.shape[0] // P, w.shape[1] // P
        w = w.reshape(kt, P, nt, P).transpose(2, 1, 0, 3).reshape(nt, P, kt * P)
        return w if order is None else w[order]

    def cols(a, n):
        return np.ascontiguousarray(np.asarray(a).reshape(n, P).T)

    def feature_major(a, n):
        return np.ascontiguousarray(a.T.reshape(n, P, -1).transpose(1, 0, 2))

    arrays = dict(constants())
    arrays["x"] = feature_major(v["x"][0], KT)
    arrays["p"] = feature_major(v["p"][0, 0], PT)
    arrays["p2"] = feature_major(v["p_2"][0, 0], PT)
    arrays["pos"] = np.ascontiguousarray(np.broadcast_to(v["positions"].reshape(1, T), (P, T)))
    vecs = {
        "norm_mix": cols(v["norm_mix_g"], 8), "norm_ffn": cols(v["norm_ffn_g"], 8),
        "norm_ple": cols(v["norm_ple_g"], 8), "final": cols(v["final_norm_g"], 8),
        "norm1": cols(v["norm1_g_2"], 8), "norm2": cols(v["norm2_g_2"], 8),
        "norm3": cols(v["norm3_g_2"], 8), "conv_b": cols(v["ffn_conv_b"], FT),
        "qn": cols(np.tile(v["q_norm_g_2"][0], 2), 1), "kn": cols(np.tile(v["k_norm_g_2"][0], 2), 1),
        "sgu_g": cols(v["sgu_norm_g_2"], 2), "subln": cols(v["da_subln_g"], 1),
        "hgn": cols(v["hg_norm_g"], 1), "gamma0": cols(v["hg_lb_gamma"][:, 0], 8),
        "gamma1": cols(v["hg_lb_gamma"][:, 1], 8),
    }
    for j in range(3):
        vecs[f"conv_w{j}"] = cols(v["ffn_conv_w"][0, j], FT)
        vecs[f"conv2_w{j}"] = cols(v["conv_w_2"][0, j], 2)
    lam = np.zeros((P, 4), v["lam_q1"].dtype)
    for j, name in enumerate(("lam_q1", "lam_k1", "lam_q2", "lam_k2")):
        lam[:64, j] = v[name][0]
    vecs["lam"] = lam
    arrays["vec"] = np.ascontiguousarray(np.concatenate([vecs[n] for n in VEC], 1))

    order = [t * HEADS + h for h in range(HEADS) for t in range(3)]
    order += [(3 + t) * HEADS + h for h in range(HEADS) for t in range(5)]
    arrays["w_mix"] = tiles(v["w_in"][0], order)
    arrays["w_out"] = tiles(v["w_out"][0])
    gate, up, dn = tiles(v["w_ffn_gate"][0]), tiles(v["w_ffn_up"][0]), v["w_ffn_down"][0]
    f = 0
    for gi, n in enumerate(GROUPS1):
        arrays[f"w_gu{gi}"] = np.stack([gate[f:f + n], up[f:f + n]], 1).reshape(2 * n, P, T)
        arrays[f"w_dn{gi}"] = tiles(dn[f * P:(f + n) * P])
        f += n

    def ple(gate_w, emb_w):
        g, e = tiles(gate_w), tiles(emb_w)
        out = np.zeros((KT, 2, P, T), g.dtype)
        out[:, 0] = g
        out[:, 1, :, :PT * P] = e
        return out.reshape(2 * KT, P, T)

    arrays["w_ple"] = ple(v["w_ple_gate"][0], v["w_ple"][0])
    order = [b + p for p in range(HEADS) for b in (6, 10, 14)]
    order += [b + j for j in range(2) for b in (2, 4, 0)] + [b + j for j in range(2) for b in (20, 18)]
    arrays["w_mix2"] = tiles(v["w_in_2"][0], order)
    arrays["w_out2"] = tiles(v["w_out_2"][0])
    f1, f2 = tiles(v["w_ff1_2"][0]), v["w_ff2_2"][0]
    f = 0
    for gi, n in enumerate(GROUPS2):
        arrays[f"w_f1{gi}"] = f1[f:f + n]
        arrays[f"w_f2{gi}"] = tiles(f2[f * P:(f + n) * P])
        f += n
    arrays["w_ple2"] = ple(v["w_ple_gate_2"][0], v["w_ple_proj_2"][0])
    arrays["gw"] = v["sgu_w_2"][0].transpose(2, 0, 1)
    arrays["gb"] = np.repeat(v["sgu_b_2"][0].reshape(2, 2, 1, P), 64, axis=2).reshape(2, P, P).transpose(1, 0, 2)

    nc = bacc.Bacc("TRN2", target_bir_lowering=False, num_devices=1)
    arrays = {k: np.ascontiguousarray(a) for k, a in arrays.items()}
    io = {k: nc.dram_tensor(f"in_{k}", a.shape, mybir.dt.from_np(a.dtype), kind="ExternalInput").ap()
          for k, a in arrays.items()}
    io["out"] = nc.dram_tensor("out_x", (P, KT, T), F32, kind="ExternalOutput").ap()
    bass_two_blocks(nc, io)
    r = run_bass_kernel_spmd(nc, [{f"in_{k}": a for k, a in arrays.items()}], core_ids=[0])
    out = r.results[0]["out_x"]
    return np.ascontiguousarray(out.transpose(1, 0, 2).reshape(KT * P, T).T).reshape(1, T, KT * P)
```

```python
from contextlib import ExitStack

import numpy as np

import concourse.bass as bass
from concourse import mybir

F32 = mybir.dt.float32
F32R = mybir.dt.float32r
I32 = mybir.dt.int32
ALU = mybir.AluOpType
ACT = mybir.ActivationFunctionType
AX_X = mybir.AxisListType.X

P = 128
T = 1024
HALF = 512
KT = 8
FT = 22
FT2 = 32
PT = 2
GROUPS1 = (8, 8, 6)
GROUPS2 = (8, 8, 8, 8)
HEADS = 4
LEVELS = 7
EPS = 1e-6
SBUF_BASE = 16512
LAMBDA_INIT = 0.2
TWO_PI = 2.0 * np.pi

VEC = {}
_at = 0
for _name, _n in (("norm_mix", 8), ("norm_ffn", 8), ("norm_ple", 8), ("final", 8), ("norm1", 8),
                  ("norm2", 8), ("norm3", 8), ("conv_w0", FT), ("conv_w1", FT), ("conv_w2", FT),
                  ("conv_b", FT), ("conv2_w0", 2), ("conv2_w1", 2), ("conv2_w2", 2), ("qn", 1),
                  ("kn", 1), ("sgu_g", 2), ("subln", 1), ("hgn", 1), ("gamma0", 8), ("gamma1", 8),
                  ("lam", 4)):
    VEC[_name] = _at
    _at += _n
NVEC = _at
DER = {}
_at = 0
for _name, _n in (("fin_n1", 8), ("subln", 1), ("qn", 1), ("neg_lam", 1), ("lb", 8), ("omlb", 8),
                  ("g0", 8), ("g1", 8), ("lamp", 2), ("lame", 2), ("zero", 1)):
    DER[_name] = _at
    _at += _n
NDER = _at

U_DA = 0
U_HG = U_DA + 3 * HEADS
U_OUT = U_HG + 5 * HEADS
U_GU = []
U_DN = []
_u = U_OUT + KT
for _n in GROUPS1:
    U_GU.append(_u)
    _u += 2 * _n
    U_DN.append(_u)
    _u += KT
U_PLE = _u
U_SB = U_PLE + 2 * KT
U_CV = U_SB + 3 * HEADS
U_SG = U_CV + 3 * 2
U_OUT2 = U_SG + 2 * 2
U_F1 = []
U_F2 = []
_u = U_OUT2 + KT
for _n in GROUPS2:
    U_F1.append(_u)
    _u += _n
    U_F2.append(_u)
    _u += KT
U_PLE2 = _u
U_END = U_PLE2 + 2 * KT

N_MIX = 0
N_DA = 1
N_HG = N_DA + HEADS
N_FFN = N_HG + HEADS
N_PLE = N_FFN + 1
N_FIN = N_PLE + 1
N_1 = N_FIN + 1
N_QK = N_1 + 1
N_SG = N_QK + HEADS
N_2 = N_SG + 2
N_3 = N_2 + 1


F_MIX = 0
F_FF = F_MIX + KT
F_MIX2 = F_FF + FT
F_FF2 = F_MIX2 + KT
Q_MIX, Q_FFN, Q_PLE, Q_1, Q_2, Q_3 = range(0, 6 * KT, KT)

MAGIC = 1.5 * 2.0**23
_c2 = np.floor((TWO_PI - 6.28125) * 2.0**20) / 2.0**20
TURN = (6.28125, float(_c2), float(np.float32(TWO_PI - 6.28125 - _c2)))


def half_no(u, hf):
    return 2 * u + hf + 1


def stick_pieces():
    return [(th, i, hh) for th in range(2) for i in range(4 * th + 3, -1, -1) for hh in range(2)]


PIECES = stick_pieces()
NPC = len(PIECES)


def diagonal_no(p, n):
    in_pair = [i >= 4 * th for th, i, _ in PIECES]
    return sum(in_pair) * p + sum(in_pair[:n + 1])


def filling(u0, n, slots):
    steps = [(u, hf, k) for u in range(u0, u0 + n) for hf in range(2) for k in range(KT)]
    return [steps[i * len(steps) // slots:(i + 1) * len(steps) // slots] for i in range(slots)]


def finished(slot):
    return [(u, hf) for u, hf, k in slot if k == KT - 1]


def da_fill(h):
    return (U_DA + 3 * (h + 1), 2) if h + 1 < HEADS else (U_HG, 3)


def hg_fill(h):
    return (U_HG + 5 * (h + 1), 4) if h + 1 < HEADS else (U_OUT, 0)


def sb_fill(p):
    return (U_SB + 3 * (p + 1), 2) if p + 1 < HEADS else (U_CV, 3)


def bass_two_blocks(nc, io):
    ctx = ExitStack()
    with ctx:
        def at(name, cols, off, dt=F32, parts=P):
            shape = [parts, *cols] if isinstance(cols, tuple) else [parts, cols]
            return nc.alloc_sbuf_tensor_at(name, shape, dt, offset=SBUF_BASE + off)

        def sem(name):
            return ctx.enter_context(nc.semaphore(name))


        KB = 1024
        a_hi = at("a_hi", (KT, T), 0, F32R)
        a_lo = at("a_lo", (KT, T), 32 * KB, F32R)
        b_hi = at("b_hi", (KT, T), 64 * KB, F32R)
        b_lo = at("b_lo", (KT, T), 96 * KB, F32R)
        x = at("x", (KT, T), 128 * KB)
        mix = at("mix", (KT, T), 128 * KB)
        w_raw = at("w_raw", (2, T), 160 * KB)
        w_hi = at("w_hi", (2, T), 168 * KB, F32R)
        w_lo = at("w_lo", (2, T), 176 * KB, F32R)
        rstd = at("rstd", T, 184 * KB)
        TMP = 188 * KB
        pad_a = at("pad_a", (2, 1032), TMP)
        sq = at("sq", (2, 1032), TMP)
        c_buf = at("c_buf", T, TMP + 8256)
        ss = at("ss", T, TMP + 8256 + 4096)
        CST = TMP + 8256 + 8192
        ident = at("ident", P, CST)
        cst = at("cst", 8, CST + 512)
        vec = at("vec", NVEC, CST + 544)
        VEC_END = CST + 544 + (4 * NVEC + 31) // 32 * 32
        der = at("der", NDER, VEC_END)
        sm = at("sm", (4, 32), VEC_END + (4 * NDER + 31) // 32 * 32)
        SM_END = VEC_END + (4 * NDER + 31) // 32 * 32 + 512
        rows = at("rows", (2, 16), SM_END)
        one = cst[:, 0:1]
        blk2 = cst[:, 1:3]
        invf = cst[:, 3:4]

        S0 = 64 * KB
        dq = [at("dq_even", (2, T), S0), at("dq_odd", (2, T), 144 * KB)]
        dv = at("dv", T, S0 + 8 * KB)
        dvt = at("dvt", (KT, P), S0 + 12 * KB)
        de = at("de", (2, 2, T), S0 + 16 * KB)
        dwt = at("dwt", (2, HALF), S0 + 32 * KB)
        dtmp = at("dtmp", T, S0 + 36 * KB)
        cosm = at("cosm", T, S0 + 40 * KB)
        sinm = at("sinm", T, S0 + 44 * KB)
        swapm = at("swapm", P, S0 + 48 * KB)
        ang = at("ang", T, S0 + 49 * KB)
        ang2 = at("ang2", T, S0 + 53 * KB)
        posi = at("posi", T, S0 + 57 * KB, mybir.dt.int32)
        hq = [at("hq_even", T, S0), at("hq_odd", T, TMP)]
        hz = [[at("hzf_even", T, S0 + 4 * KB), at("hzb_even", T, S0 + 8 * KB)],
              [at("hzf_odd", T, TMP + 4 * KB), at("hzb_odd", T, TMP + 8256 + 4096)]]
        hv = at("hv", T, S0 + 12 * KB)
        hg = at("hg", T, S0 + 16 * KB)
        hvt = at("hvt", (KT, P), S0 + 20 * KB)
        hk = at("hk", (2, T), S0 + 24 * KB)
        hd = at("hd", (2, T), S0 + 32 * KB)
        hqt = at("hqt", (2, HALF), S0 + 40 * KB)
        hkt = at("hkt", (2, T), S0 + 44 * KB)
        hatt = at("hatt", T, S0 + 52 * KB)
        hkd = at("hkd", (KT, P), S0 + 56 * KB)
        hkd_flat = hkd[:, :, :].rearrange("p c e -> p (c e)")
        heb = at("heb", (2, KT), S0 + 60 * KB)
        hmask = at("hmask", (2 * LEVELS, 64), S0 + 60 * KB + 256, I32)
        reset = at("reset", T, TMP + 8256)
        sk = [at("sk_even", (2, T), S0), at("sk_odd", (2, T), 128 * KB)]
        sv = at("sv", T, S0 + 8 * KB)
        svt = at("svt", (KT, P), S0 + 12 * KB)
        sz = at("sz", (4, HALF), S0 + 16 * KB)
        sl = at("sl", (4, HALF), S0 + 24 * KB)
        sp = at("sp", (4, HALF), S0 + 32 * KB)
        sph = at("sph", (4, HALF), S0 + 40 * KB, F32R)
        spl = at("spl", (4, HALF), S0 + 48 * KB, F32R)
        sw = at("sw", (4, HALF), S0 + 56 * KB)
        tri = at("tri", (2, P), TMP, F32R)
        tri_raw = at("tri_raw", (3, P), TMP + KB)
        ctri = tri_raw[:, 2, :]
        cc = at("cc", (3, T), S0)
        cp = at("cp", T + 8, S0 + 12 * KB)
        gv = at("gv", (2, T), S0 + 20 * KB)
        gvt = at("gvt", (KT, P), S0 + 28 * KB)
        gw = at("gw", (4, P), S0 + 32 * KB)
        gb = at("gb", (2, P), S0 + 34 * KB)
        gmask = at("gmask", P, S0 + 35 * KB)
        p_raw = at("p_raw", (PT, T), S0 + 16 * KB)

        ps = ctx.enter_context(nc.psum_tensor("ps", [P, 8, HALF], F32))

        def banks(a, n=2):
            return ps[:, a:a + n, :].rearrange("p a b -> p (a b)")

        x_back = nc.dram_tensor("x_back", (P, KT, T), F32, kind="Internal").ap()

        param_in = sem("param_in")
        w_in = [sem(f"w_in{s}") for s in range(2)]
        w_hi_done = sem("w_hi_done")
        w_split = sem("w_split")
        acc_full = sem("acc_full")
        acc_free = sem("acc_free")
        x_in = [sem(f"x_in{k}") for k in range(KT)]
        x_out = sem("x_out")
        out_done = sem("out_done")
        h_hi = sem("h_hi")
        h_lo = sem("h_lo")
        sq_ready = sem("sq_ready")
        ss_ready = sem("ss_ready")
        st_sum = sem("st_sum")
        st_var = sem("st_var")
        st_root = sem("st_root")
        st_inv = sem("st_inv")
        st_bc = sem("st_bc")
        rstd_ready = sem("rstd_ready")
        dve_step = sem("dve_step")
        act_step = sem("act_step")
        x_done = sem("x_done")
        xf_ready = sem("xf_ready")
        fx_ready = sem("fx_ready")
        pos_in = sem("pos_in")
        ang_ready = sem("ang_ready")
        cs_ready = sem("cs_ready")
        der_ready = sem("der_ready")
        lam_mm = sem("lam_mm")
        lam_exp = sem("lam_exp")
        swapped = sem("swapped")
        qk_ready = sem("qk_ready")
        v_tr = sem("v_tr")
        v_ready = sem("v_ready")
        scored = sem("scored")
        max_ready = sem("max_ready")
        exp_done = sem("exp_done")
        w_ready = sem("w_ready")
        w_tr = sem("w_tr")
        wt_ready = sem("wt_ready")
        o_mm = sem("o_mm")
        o_out = sem("o_out")
        o_sq = sem("o_sq")
        mix_ready = sem("mix_ready")
        hmask_in = sem("hmask_in")
        sig_done = sem("sig_done")
        f_ready = sem("f_ready")
        logf_done = sem("logf_done")
        d_ready = sem("d_ready")
        e_done = sem("e_done")
        qk_lvl = sem("qk_lvl")
        lvl_mm = sem("lvl_mm")
        att_put = sem("att_put")
        kd_ready = sem("kd_ready")
        kd_tr = sem("kd_tr")
        kdt_ready = sem("kdt_ready")
        kv_mm = sem("kv_mm")
        state_ready = sem("state_ready")
        silu_done = sem("silu_done")
        tri_in = sem("tri_in")
        tri_ready = sem("tri_ready")
        sq_qk = sem("sq_qk")
        z_mm = sem("z_mm")
        z_out = sem("z_out")
        l_ready = sem("l_ready")
        sp_ready = sem("sp_ready")
        sph_ready = sem("sph_ready")
        spl_ready = sem("spl_ready")
        suf_mm = sem("suf_mm")
        t_ready = sem("t_ready")
        sw_exp = sem("sw_exp")
        sw_ready = sem("sw_ready")
        so_mm = sem("so_mm")
        so_out = sem("so_out")
        gate_in = sem("gate_in")
        gelu_done = sem("gelu_done")
        gw_ready = sem("gw_ready")
        gn_ready = sem("gn_ready")
        g_tr = sem("g_tr")
        gt_ready = sem("gt_ready")
        gs_mm = sem("gs_mm")
        conv_done = sem("conv_done")
        act_done = sem("act_done")
        f_hi = sem("f_hi")
        f_lo = sem("f_lo")
        p_in = sem("p_in")
        p_hi = sem("p_hi")
        p_lo = sem("p_lo")
        pg_sig = sem("pg_sig")

        lam_ready = sem("lam_ready")
        g_ready = sem("g_ready")
        qd_ready = sem("qd_ready")
        ho_mm = sem("ho_mm")
        ho_out = sem("ho_out")
        s2_ready = sem("s2_ready")
        sq2_ready = sem("sq2_ready")
        sv_tr = sem("sv_tr")
        sv_ready = sem("sv_ready")
        qk2_ready = sem("qk2_ready")
        g_sq = sem("g_sq")
        g_done = sem("g_done")
        z_abs = sem("z_abs")
        z_exp = sem("z_exp")

        block = ctx.enter_context(nc.Block())

        @block.sync
        def _(sp_):
            sp_.dma_start(vec[:, :], io["vec"]).then_inc(param_in, 16)
            sp_.dma_start(ident[:, :], io["ident"]).then_inc(param_in, 16)
            sp_.dma_start(cst[:, :], io["cst"]).then_inc(param_in, 16)
            for k in range(KT):
                sp_.dma_start(x[:, k, :], io["x"][:, k, :]).then_inc(x_in[k], 16)
            sp_.dma_start(posi[:, :], io["pos"]).then_inc(pos_in, 16)
            sp_.dma_start(swapm[:, :], io["swap"]).then_inc(pos_in, 16)

            def weights(name, u0, n, cols=(T, T)):
                src = io[name]

                def load(i, s, u):
                    sp_.wait_ge(w_split, u - 1)
                    sp_.dma_start(w_raw[:, s, 0:cols[s]],
                                  src[bass.ds(2 * i + s, 1), :, 0:cols[s]].rearrange("u p n -> (u p) n")
                                  ).then_inc(w_in[s], 16)

                if u0 == 0:
                    for s in range(2):
                        sp_.dma_start(w_raw[:, s, :], src[s]).then_inc(w_in[s], 16)
                    with sp_.Fori(1, n // 2, 1) as i:
                        for s in range(2):
                            load(i, s, u0 + 2 * i + s)
                else:
                    with sp_.Fori(0, n // 2, 1) as i:
                        for s in range(2):
                            load(i, s, u0 + 2 * i + s)

            weights("w_mix", U_DA, U_OUT)
            weights("w_out", U_OUT, KT)
            for gi, n in enumerate(GROUPS1):
                weights(f"w_gu{gi}", U_GU[gi], 2 * n)
                weights(f"w_dn{gi}", U_DN[gi], KT, (n * P, n * P))
            weights("w_ple", U_PLE, 2 * KT, (T, PT * P))
            weights("w_mix2", U_SB, U_OUT2 - U_SB)
            weights("w_out2", U_OUT2, KT)
            for gi, n in enumerate(GROUPS2):
                weights(f"w_f1{gi}", U_F1[gi], n)
                weights(f"w_f2{gi}", U_F2[gi], KT)
            weights("w_ple2", U_PLE2, 2 * KT, (T, PT * P))
            sp_.wait_ge(out_done, 16 * KT)

        @block.gpsimd
        def _(pool):
            pool.memset(der[:, DER["zero"]:DER["zero"] + 1], 0.0).then_inc(der_ready, 1)
            pool.wait_ge(der_ready, 1)
            zero = der[:, DER["zero"]:DER["zero"] + 1]

            def split(u0, n, cols=(T, T)):
                def one_unit(u, s, turn, first):
                    pool.wait_ge(w_in[s], 16 * (turn + 1))
                    if not first:
                        pool.wait_ge(acc_full, half_no(u - 2, 1))
                    nc.gpsimd.tensor_tensor(w_hi[:, s, 0:cols[s]], w_raw[:, s, 0:cols[s]],
                                            zero.to_broadcast([P, cols[s]]), ALU.add).then_inc(w_hi_done, 1)
                    pool.wait_ge(w_hi_done, u + 1)
                    nc.gpsimd.tensor_tensor(w_lo[:, s, 0:cols[s]], w_raw[:, s, 0:cols[s]],
                                            w_hi[:, s, 0:cols[s]].bitcast(F32), ALU.subtract).then_inc(w_split, 1)

                if u0 == 0:
                    for s in range(2):
                        one_unit(s, s, 0, True)
                    with pool.Fori(1, n // 2, 1) as i:
                        for s in range(2):
                            one_unit(2 * i + s, s, i, False)
                else:
                    with pool.Fori(0, n // 2, 1) as i:
                        for s in range(2):
                            one_unit(u0 + 2 * i + s, s, u0 // 2 + i, False)

            split(U_DA, U_GU[0])
            for gi, n in enumerate(GROUPS1):
                split(U_GU[gi], 2 * n)
                split(U_DN[gi], KT, (n * P, n * P))
            split(U_PLE, 2 * KT, (T, PT * P))
            split(U_SB, U_PLE2 - U_SB)
            split(U_PLE2, 2 * KT, (T, PT * P))


        @block.tensor
        def _(pe):
            mm = nc.tensor.matmul

            def k_step(u, hf, k, s, hi, lo, nk):
                if k == 0 and hf == 0:
                    pe.wait_ge(w_split, u + 1)
                if k == 0 and not (isinstance(u, int) and half_no(u, hf) <= 2):
                    pe.wait_ge(acc_free, half_no(u, hf) - 2)
                cols = slice(hf * HALF, hf * HALF + HALF)
                wh, wl = w_hi[:, s, k * P:(k + 1) * P], w_lo[:, s, k * P:(k + 1) * P]
                mm(ps[:, hf, :], wh, hi[:, k, cols], start=(k == 0), stop=False)
                mm(ps[:, hf, :], wh, lo[:, k, cols], start=False, stop=False)
                last = mm(ps[:, hf, :], wl, hi[:, k, cols], start=False, stop=(k == nk - 1))
                if k == nk - 1:
                    last.then_inc(acc_full, 1)

            def gemm_half(u, hf, s, hi, lo, nk, wait_k=None):
                for k in range(nk):
                    if wait_k:
                        wait_k(k)
                    k_step(u, hf, k, s, hi, lo, nk)

            def fill(slot):
                for u, hf, k in slot:
                    k_step(u, hf, k, u % 2, a_hi, a_lo, KT)

            def gemm(u, s, hi, lo, nk, wait_k=None):
                gemm_half(u, 0, s, hi, lo, nk, wait_k)
                gemm_half(u, 1, s, hi, lo, nk)

            def gemm_loop(u0, n, hi, lo, nk, wait_k=None, first=0):
                with pe.Fori(first, n // 2, 1) as i:
                    for s in range(2):
                        gemm(u0 + 2 * i + s, s, hi, lo, nk, wait_k if s == 0 else None)

            def st_sums(src, rhs, ncol, first=0, more=False):
                for c in range(KT):
                    last = mm(ps[:, 7, first + c * ncol:first + (c + 1) * ncol], src[:, c * P:(c + 1) * P],
                              rhs, start=True, stop=True)
                if not more:
                    last.then_inc(st_sum, 1)

            def st_bcast(n, ncol, bank, first=0, more=False):
                pe.wait_ge(st_inv, n + 1)
                rows_ = P // ncol
                for c in range(KT):
                    for j in range(ncol):
                        at_ = first + ncol * c + j
                        lhs = sm[:, 3, at_:at_ + 1].to_broadcast([P, rows_])
                        last = mm(ps[rows_ * j:rows_ * (j + 1), bank + c // 4, (c % 4) * P:(c % 4 + 1) * P],
                                  lhs, ident[:, :], start=True, stop=True)
                if not more:
                    last.then_inc(st_bc, 1)

            def transposes(src, bank, done):
                for c in range(KT):
                    last = nc.tensor.transpose(ps[:, bank + c // 4, (c % 4) * P:(c % 4 + 1) * P],
                                               src[:, c * P:(c + 1) * P], ident[:, :])
                last.then_inc(done, 1)

            def normed_unit(n, q0, u0, ss_count):
                gemm_half(u0, 0, 0, a_hi, a_lo, KT, lambda k: pe.wait_ge(h_lo, q0 + k + 1))
                pe.wait_ge(ss_ready, ss_count)
                st_sums(ss, one, 1)
                gemm_half(u0, 1, 0, a_hi, a_lo, KT)
                st_bcast(n, 1, 5)

            pe.wait_ge(param_in, 48)
            pe.wait_ge(lam_ready, 1)
            mm(ps[:, 7, 0:2], one[0:64, :].to_broadcast([64, P]), der[0:64, DER["lamp"]:DER["lamp"] + 2],
               start=True, stop=True).then_inc(lam_mm, 1)
            pe.wait_ge(lam_exp, 1)
            normed_unit(N_MIX, 0, U_DA, KT)

            def scores(h, qt):
                g = KT * h + qt
                for m in range(2):
                    if g > 0:
                        pe.wait_ge(exp_done, 2 * (g - 1) + m + 1)
                    r = slice(64 * m, 64 * m + 64)
                    for hf in range(2):
                        last = mm(ps[:, 2 + 2 * m + hf, :], dq[h % 2][r, 0, qt * P:(qt + 1) * P],
                                  dq[h % 2][r, 1, hf * HALF:(hf + 1) * HALF], start=True, stop=True)
                    last.then_inc(scored, 1)

            def weigh(h, qt, slot0, slot1):
                g = KT * h + qt
                pe.wait_ge(w_ready, g + 1)
                for r in range(2):
                    if g or r:
                        pe.wait_ge(wt_ready, 2 * g + r)
                    for c in range(4):
                        last = nc.tensor.transpose(ps[:, 6, c * P:(c + 1) * P],
                                                   de[:, g % 2, 0, (4 * r + c) * P:(4 * r + c + 1) * P],
                                                   ident[:, :])
                    last.then_inc(w_tr, 1)
                    fill(slot1 if r else slot0)
                if qt == 4:
                    pe.wait_ge(o_out, 2 * h + 1)
                for c in range(KT):
                    if c % 4 == 0:
                        pe.wait_ge(wt_ready, 2 * g + c // 4 + 1)
                    last = mm(ps[:, 7, (qt % 4) * P:(qt % 4 + 1) * P], dvt[:, c, :],
                              dwt[:, c // 4, (c % 4) * P:(c % 4 + 1) * P], start=(c == 0),
                              stop=(c == KT - 1))
                last.then_inc(o_mm, 1)

            gemm(U_DA + 1, 1, a_hi, a_lo, KT)
            for h in range(HEADS):
                u = U_DA + 3 * h
                if h == 0:
                    pe.wait_ge(pos_in, 32)
                    pe.wait_ge(rstd_ready, 1)
                for t in range(2):
                    pe.wait_ge(acc_free, half_no(u + t, 1))
                    if h:
                        pe.wait_ge(exp_done, 2 * KT * h)
                    for hf in range(2):
                        last = mm(ps[:, 2 + 2 * t + hf, :], swapm[:, :],
                                  dq[h % 2][:, t, hf * HALF:(hf + 1) * HALF], start=True, stop=True)
                    last.then_inc(swapped, 1)
                if h:
                    pe.wait_ge(o_sq, h)
                    st_sums(ang, one, 1)
                gemm_half(u + 2, 0, (u + 2) % 2, a_hi, a_lo, KT)
                if h:
                    st_bcast(N_DA + h - 1, 1, 6)
                gemm_half(u + 2, 1, (u + 2) % 2, a_hi, a_lo, KT)
                pe.wait_ge(qk_ready, 2 * h + 1)
                pe.wait_ge(acc_free, half_no(u + 2, 1))
                transposes(dv, 2, v_tr)
                pe.wait_ge(v_ready, h + 1)
                pe.wait_ge(qk_ready, 2 * h + 2)
                slots = filling(*da_fill(h), 2 * KT)
                for qt in range(KT + 1):
                    if qt < KT:
                        scores(h, qt)
                    if qt == 1 and h:
                        pe.wait_ge(mix_ready, h)
                    if qt:
                        weigh(h, qt - 1, slots[2 * qt - 2], slots[2 * qt - 1])

            for h in range(HEADS):
                u = U_HG + 5 * h
                slots = filling(*hg_fill(h), 2 * LEVELS + 4)
                pe.wait_ge(o_sq, HEADS + h)
                if h:
                    pe.wait_ge(acc_free, half_no(u + 3, 1))
                    transposes(hv, 2, v_tr)
                    st_sums(hkd_flat, one, 1)
                    gemm_half(u + 4, 0, (u + 4) % 2, a_hi, a_lo, KT)
                    st_bcast(N_HG + h - 1, 1, 6)
                    gemm_half(u + 4, 1, (u + 4) % 2, a_hi, a_lo, KT)
                else:
                    st_sums(ang, one, 1)
                    gemm_half(u + 3, 0, (u + 3) % 2, a_hi, a_lo, KT)
                    st_bcast(N_HG - 1, 1, 6)
                    gemm_half(u + 3, 1, (u + 3) % 2, a_hi, a_lo, KT)
                    pe.wait_ge(acc_free, half_no(u + 3, 1))
                    transposes(hv, 2, v_tr)
                    gemm(u + 4, (u + 4) % 2, a_hi, a_lo, KT)
                pe.wait_ge(qk_lvl, 15 * h + 1)
                for c in range(KT):
                    last = mm(ps[:, 4 + c // 4, (c % 4) * P:(c % 4 + 1) * P], hd[:, 0, c * P:(c + 1) * P],
                              hq[h % 2][:, c * P:(c + 1) * P], start=True, stop=True)
                last.then_inc(lvl_mm, 1)
                for l in range(2 * LEVELS):
                    n = 15 * h + 1 + l
                    pe.wait_ge(qk_lvl, n + 1)
                    pe.wait_ge(att_put, n if l < 2 else n - 1)
                    for c in range(KT):
                        last = mm(ps[:, 4 + l % 2, c * 64:(c + 1) * 64], hkt[:, l % 2, c * P:(c + 1) * P],
                                  hqt[:, l % 2, c * 64:(c + 1) * 64], start=True, stop=True)
                    last.then_inc(lvl_mm, 1)
                    fill(slots[l])
                for d in range(2):
                    n = 2 * h + d
                    pe.wait_ge(kd_ready, n + 1)
                    pe.wait_ge(v_ready, HEADS + h + 1)
                    if n:
                        pe.wait_ge(kdt_ready, n)
                    transposes(hkt[:, d, :], 2, kd_tr)
                    fill(slots[2 * LEVELS + 2 * d])
                    pe.wait_ge(kdt_ready, n + 1)
                    pe.wait_ge(att_put, 15 * h + 15)
                    if d:
                        pe.wait_ge(state_ready, 2 * h + 1)
                    for c in range(KT):
                        last = mm(ps[:, 4 + c // 4, (c % 4) * P:(c % 4 + 1) * P], hkd[:, c, :],
                                  hvt[:, c, :], start=True, stop=True)
                    last.then_inc(kv_mm, 1)
                    fill(slots[2 * LEVELS + 2 * d + 1])
                pe.wait_ge(state_ready, 2 * h + 2)
                pe.wait_ge(qd_ready, 2 * h + 2)
                pe.wait_ge(mix_ready, HEADS + h)
                for c in range(KT):
                    t = slice(c * P, (c + 1) * P)
                    parts = [(hvt[:, c, :], hatt[:, t])]
                    if c > 0:
                        parts.append((hk[:, 0, t], hz[h % 2][0][:, t]))
                    if c < KT - 1:
                        parts.append((hk[:, 1, t], hz[h % 2][1][:, t]))
                    for n, (lhs, rhs) in enumerate(parts):
                        last = mm(ps[:, 6 + c // 4, (c % 4) * P:(c % 4 + 1) * P], lhs, rhs,
                                  start=(n == 0), stop=(n == len(parts) - 1))
                last.then_inc(ho_mm, 1)
            pe.wait_ge(o_sq, 2 * HEADS)
            st_sums(hkd_flat, one, 1)
            st_bcast(N_HG + HEADS - 1, 1, 4)

            def mixed_out(u0, f0):
                gemm_half(u0, 0, 0, b_hi, b_lo, KT, lambda k: pe.wait_ge(f_lo, f0 + k + 1))
                gemm_half(u0, 1, 0, b_hi, b_lo, KT)
                gemm(u0 + 1, 1, b_hi, b_lo, KT)
                gemm_loop(u0, KT, b_hi, b_lo, KT, first=1)

            mixed_out(U_OUT, F_MIX)
            f = F_FF
            for gi, n in enumerate(GROUPS1):
                if gi == 0:
                    normed_unit(N_FFN, Q_FFN, U_GU[0], Q_FFN + KT)
                    gemm(U_GU[0] + 1, 1, a_hi, a_lo, KT)
                    gemm_loop(U_GU[0], 2 * n, a_hi, a_lo, KT, first=1)
                else:
                    gemm_loop(U_GU[gi], 2 * n, a_hi, a_lo, KT)
                f += n
                gemm_loop(U_DN[gi], KT, b_hi, b_lo, n,
                          lambda k: k == n - 1 and pe.wait_ge(f_lo, f))

            def embedding(n, q0, u0, turn):
                normed_unit(n, q0, u0, q0 + KT)
                gemm(u0 + 1, 1, b_hi, b_lo, PT, lambda k: pe.wait_ge(p_lo, 2 * turn + k + 1))
                with pe.Fori(1, KT, 1) as i:
                    gemm(u0 + 2 * i, 0, a_hi, a_lo, KT)
                    gemm(u0 + 2 * i + 1, 1, b_hi, b_lo, PT)

            embedding(N_PLE, Q_PLE, U_PLE, 0)

            gemm_half(U_SB, 0, 0, a_hi, a_lo, KT, lambda k: pe.wait_ge(h_lo, Q_1 + k + 1))
            pe.wait_ge(ss_ready, Q_1 + KT)
            st_sums(ss, one, 1)
            pe.wait_ge(s2_ready, KT)
            pe.wait_ge(st_var, N_FIN + 1)
            st_sums(c_buf, one, 1)
            gemm_half(U_SB, 1, 0, a_hi, a_lo, KT)
            st_bcast(N_1, 1, 5)
            pe.wait_ge(rstd_ready, 4)
            for c in range(KT):
                last = mm(ps[:, 5 + c // 4, (c % 4) * P:(c % 4 + 1) * P], sm[:, 0, c:c + 1].to_broadcast([P, P]),
                          ident[:, :], start=True, stop=True)
            last.then_inc(st_bc, 1)

            def piece(p, n):
                return NPC * p + n

            def logits(p, n):
                th, i, hh = PIECES[n]
                c0 = max(0, i - 4 * th) * P
                s = piece(p, n)
                if s >= 2:
                    pe.wait_ge(z_out, s - 1)
                r = slice(64 * hh, 64 * hh + 64)
                mm(ps[:, 2 + s % 2, c0:], sk[p % 2][r, 1, i * P:(i + 1) * P],
                   sk[p % 2][r, 0, th * HALF + c0:(th + 1) * HALF], start=True, stop=True).then_inc(z_mm, 1)

            def suffix(p, n, which):
                th, i, hh = PIECES[n]
                c0 = max(0, i - 4 * th) * P
                s = piece(p, n)
                first = which == 0 and i == 4 * th + 3
                if which == 0:
                    pe.wait_ge(spl_ready, s + 1)
                else:
                    pe.wait_ge(t_ready, s + 1)
                if first and th:
                    pe.wait_ge(t_ready, s - 1)
                for m, part in enumerate((sph, spl)):
                    last = mm(ps[:, 4 + hh, c0:], tri[:, which, :], part[:, s % 4, c0:],
                              start=(first and m == 0), stop=(m == 1), skip_group_check=True)
                if which == 0:
                    last.then_inc(suf_mm, 1)

            def values(p, n):
                th, i, hh = PIECES[n]
                c0 = max(0, i - 4 * th) * P
                s = piece(p, n)
                if i >= 4 * th:
                    pe.wait_ge(sw_ready, diagonal_no(p, n))
                else:
                    pe.wait_ge(sw_exp, s + 1)
                if i == 4 * th + 3 and (p or th):
                    pe.wait_ge(so_out, 4 * p + 2 * th + hh - 1)
                last = mm(ps[:, 6 + hh, c0:], svt[:, i, :], sw[:, s % 4, c0:], start=(i == 4 * th + 3),
                          stop=(i == 0), skip_group_check=True)
                last.then_inc(so_mm, 1)

            pe.wait_ge(tri_ready, 2)
            gemm(U_SB + 1, 1, a_hi, a_lo, KT)
            for p in range(HEADS):
                u = U_SB + 3 * p
                if p == 0:
                    pe.wait_ge(xf_ready, KT)
                else:
                    pe.wait_ge(so_out, 4 * p)
                    pe.wait_ge(z_out, NPC * p)
                    pe.wait_ge(t_ready, NPC * p)
                pe.wait_ge(sq_qk, 2 * p + 2)
                st_sums(c_buf, blk2, 2, 0, True)
                st_sums(ss, blk2, 2, 16)
                gemm_half(u + 2, 0, (u + 2) % 2, a_hi, a_lo, KT)
                st_bcast(N_QK + p, 2, 4, 0, True)
                st_bcast(N_QK + p, 2, 2, 16)
                gemm_half(u + 2, 1, (u + 2) % 2, a_hi, a_lo, KT)
                pe.wait_ge(acc_free, half_no(u + 2, 1))
                transposes(sv, 6, sv_tr)
                pe.wait_ge(qk2_ready, 2 * p + 2)
                slots = filling(*sb_fill(p), NPC + 3)
                logits(p, 0)
                pe.wait_ge(sv_ready, p + 1)
                for n in range(NPC + 4):
                    if n + 1 < NPC:
                        logits(p, n + 1)
                    if 3 <= n <= NPC + 2 and PIECES[n - 3][1] > 0:
                        suffix(p, n - 3, 1)
                    if 2 <= n <= NPC + 1:
                        suffix(p, n - 2, 0)
                    if n < NPC + 3:
                        fill(slots[n])
                    if n >= 4:
                        values(p, n - 4)

            for j in range(3, 6):
                gemm(U_CV + j, (U_CV + j) % 2, a_hi, a_lo, KT)
            pe.wait_ge(so_out, 4 * HEADS)
            pe.wait_ge(gw_ready, 1)
            for j in range(2):
                u = U_SG + 2 * j
                gemm(u, u % 2, a_hi, a_lo, KT)
                gemm(u + 1, (u + 1) % 2, a_hi, a_lo, KT)
                pe.wait_ge(g_sq, j + 1)
                if j:
                    pe.wait_ge(g_done, 2 * j)
                st_sums(c_buf, blk2, 2)
                st_bcast(N_SG + j, 2, 4)
                pe.wait_ge(gn_ready, j + 1)
                transposes(gv[:, 0, :], 2, g_tr)
                pe.wait_ge(gt_ready, j + 1)
                for hh in range(2):
                    for c in range(KT):
                        last = mm(ps[:, 4 + 2 * hh + c // 4, (c % 4) * P:(c % 4 + 1) * P], gvt[:, c, :],
                                  gw[:, 2 * j + hh, :], start=True, stop=True)
                last.then_inc(gs_mm, 1)

            mixed_out(U_OUT2, F_MIX2)
            f = F_FF2
            for gi, n in enumerate(GROUPS2):
                if gi == 0:
                    normed_unit(N_2, Q_2, U_F1[0], Q_2 + KT)
                    gemm(U_F1[0] + 1, 1, a_hi, a_lo, KT)
                    gemm_loop(U_F1[0], n, a_hi, a_lo, KT, first=1)
                else:
                    gemm_loop(U_F1[gi], n, a_hi, a_lo, KT)
                f += n
                gemm_loop(U_F2[gi], KT, b_hi, b_lo, n,
                          lambda k: k == n - 1 and pe.wait_ge(f_lo, f))
            embedding(N_3, Q_3, U_PLE2, 1)

        @block.vector
        def _(dve):
            tt = nc.vector.tensor_tensor
            ts = nc.vector.tensor_scalar
            stt = nc.vector.scalar_tensor_tensor
            steps = [0]

            def step(ins):
                ins.then_inc(dve_step, 1)
                steps[0] += 1
                dve.wait_ge(dve_step, steps[0])

            def col(name, j=0, n=1):
                return vec[:, bass.ds(VEC[name] + j, n)]

            def dcol(name, j=0, n=1):
                return der[:, bass.ds(DER[name] + j, n)]

            def leave(u, dst, first=0):
                for hf in range(2):
                    dve.wait_ge(acc_full, half_no(u, hf))
                    tt(dst[:, first + hf * HALF:first + (hf + 1) * HALF], ps[:, hf, :],
                       rstd[:, hf * HALF:(hf + 1) * HALF], ALU.mult).then_inc(acc_free, 1)

            def leave_half(u, hf, dst):
                dve.wait_ge(acc_full, half_no(u, hf))
                tt(dst[:, hf * HALF:(hf + 1) * HALF], ps[:, hf, :], rstd[:, hf * HALF:(hf + 1) * HALF],
                   ALU.mult).then_inc(acc_free, 1)

            def evict(slot, u0, dsts):
                for u, hf in finished(slot):
                    leave_half(u, hf, dsts[u - u0])

            def prep(q, k, gain, xk):
                dve.wait_ge(h_hi, q + k + 1)
                stt(a_lo[:, k, :], xk, gain, a_hi[:, k, :].bitcast(F32), ALU.mult,
                    ALU.subtract).then_inc(h_lo, 1)
                dve.wait_ge(sq_ready, q + k + 1)
                if q + k:
                    dve.wait_ge(ss_ready, q + k)
                tt(ss[:, :], ss[:, :], sq[:, k % 2, 0:T], ALU.add).then_inc(ss_ready, 1)

            def st_inverse(n, ncols, scale):
                dve.wait_ge(st_sum, n + 1)
                ts(sm[:, 1, 0:ncols], ps[:, 7, 0:ncols], scale, EPS, ALU.mult, ALU.add).then_inc(st_var, 1)
                dve.wait_ge(st_root, n + 1)
                nc.vector.reciprocal(sm[:, 3, 0:ncols], sm[:, 2, 0:ncols]).then_inc(st_inv, 1)

            dve.wait_ge(param_in, 48)
            step(tt(dcol("fin_n1", 0, 8), col("final", 0, 8), col("norm1", 0, 8), ALU.mult))
            step(ts(dcol("subln"), col("subln"), 1.0 - LAMBDA_INIT, None, ALU.mult))
            step(ts(dcol("qn"), col("qn"), 0.125, None, ALU.mult))
            step(tt(dcol("lamp"), col("lam", 0), col("lam", 1), ALU.mult))
            tt(dcol("lamp", 1), col("lam", 2), col("lam", 3), ALU.mult).then_inc(lam_ready, 1)
            step(tt(dcol("lb", 0, 8), col("gamma0", 0, 8), col("gamma1", 0, 8), ALU.max))
            step(tt(dcol("g0", 0, 8), col("gamma0", 0, 8), dcol("lb", 0, 8), ALU.subtract))
            tt(dcol("g1", 0, 8), col("gamma1", 0, 8), dcol("lb", 0, 8), ALU.subtract).then_inc(g_ready, 1)
            dve.wait_ge(lam_exp, 1)
            step(tt(dcol("g1", 0, 8), dcol("g0", 0, 8), dcol("g1", 0, 8), ALU.add))
            step(nc.vector.reciprocal(dcol("g1", 0, 8), dcol("g1", 0, 8)))
            step(tt(dcol("lb", 0, 8), dcol("g0", 0, 8), dcol("g1", 0, 8), ALU.mult))
            step(ts(dcol("omlb", 0, 8), dcol("lb", 0, 8), -1.0, 1.0, ALU.mult, ALU.add))
            step(stt(dcol("neg_lam"), dcol("lame", 1), LAMBDA_INIT, dcol("lame", 0), ALU.subtract,
                     ALU.subtract))

            step(nc.vector.memset(ss[:, :], 0.0))
            for k in range(KT):
                dve.wait_ge(x_in[k], 16)
                prep(Q_MIX, k, col("norm_mix", k), x[:, k, :])
            st_inverse(N_MIX, 8, 1.0 / T)

            dve.wait_ge(pos_in, 32)
            step(nc.vector.tensor_copy(ang[:, :], posi[:, :]))
            step(ts(ang[:, :], ang[:, :], invf, None, ALU.mult))
            for n, (dst, off) in enumerate(((sinm, 0.0), (cosm, 0.25))):
                step(ts(ang2[:, :], ang[:, :], float(np.float32(1.0 / TWO_PI)), off, ALU.mult, ALU.add))
                step(ts(ang2[:, :], ang2[:, :], MAGIC, None, ALU.add))
                step(ts(ang2[:, :], ang2[:, :], MAGIC, None, ALU.subtract))
                step(stt(dst[:, :], ang2[:, :], -TURN[0], ang[:, :], ALU.mult, ALU.add))
                for part in TURN[1:]:
                    step(stt(dst[:, :], ang2[:, :], -part, dst[:, :], ALU.mult, ALU.add))
                step(ts(dst[:, :], dst[:, :], float(off * TWO_PI), 3.1415925, ALU.add, ALU.min))
                ts(dst[:, :], dst[:, :], -3.1415925, None, ALU.max).then_inc(ang_ready, 1)
            dve.wait_ge(cs_ready, 2)
            dve.wait_ge(rstd_ready, 1)

            def row_max(h, qt):
                g = KT * h + qt
                for m in range(2):
                    dve.wait_ge(scored, 2 * g + m + 1)
                    step(nc.vector.reduce_max(rows[:, m, 0:1], banks(2 + 2 * m), AX_X))
                    if g:
                        dve.wait_ge(exp_done, 2 * (g - 1) + m + 1)
                    ts(rows[:, m, 1:2], rows[:, m, 0:1], -0.125, None, ALU.mult).then_inc(max_ready, 1)

            def combine(h, qt):
                g = KT * h + qt
                r = g % 2
                dve.wait_ge(exp_done, 2 * g + 2)
                step(nc.vector.reciprocal(rows[:, r, 4:6], rows[:, r, 2:4]))
                step(tt(rows[:, r, 6:7], rows[:, r, 5:6], dcol("neg_lam"), ALU.mult))
                step(ts(de[:, r, 0, :], de[:, r, 0, :], rows[:, r, 4:5], None, ALU.mult))
                stt(de[:, r, 0, :], de[:, r, 1, :], rows[:, r, 6:7], de[:, r, 0, :], ALU.mult,
                    ALU.add).then_inc(w_ready, 1)

            def rotate(h, t):
                dve.wait_ge(swapped, 2 * h + t + 1)
                qk = dq[h % 2][:, t, :]
                step(tt(dtmp[:, :], banks(2 + 2 * t), sinm[:, :], ALU.mult))
                step(tt(qk, qk, cosm[:, :], ALU.mult))
                tt(qk, qk, dtmp[:, :], ALU.add).then_inc(qk_ready, 1)
                dve.wait_ge(qk_ready, 2 * h + t + 1)

            def da_norm(h, bank):
                dve.wait_ge(st_bc, N_DA + h + 1)
                stt(mix[:, h, :], mix[:, h, :], dcol("subln"), banks(bank), ALU.mult,
                    ALU.mult).then_inc(mix_ready, 1)

            leave(U_DA, dq[0][:, 0, :])
            leave(U_DA + 1, dq[0][:, 1, :])
            for h in range(HEADS):
                u = U_DA + 3 * h
                rotate(h, 0)
                if h:
                    st_inverse(N_DA + h - 1, 8, 1.0 / P)
                rotate(h, 1)
                leave_half(u + 2, 0, dv[:, :])
                if h:
                    da_norm(h - 1, 6)
                leave_half(u + 2, 1, dv[:, :])
                slots = filling(*da_fill(h), 2 * KT)
                if h + 1 < HEADS:
                    next_ = [dq[(h + 1) % 2][:, 0, :], dq[(h + 1) % 2][:, 1, :]]
                else:
                    next_ = [hq[0][:, :], hz[0][0][:, :], hz[0][1][:, :]]
                for qt in range(KT + 1):
                    if qt:
                        combine(h, qt - 1)
                    if qt > 1:
                        evict(slots[2 * qt - 4] + slots[2 * qt - 3], da_fill(h)[0], next_)
                    if qt < KT:
                        row_max(h, qt)
                evict(slots[-2] + slots[-1], da_fill(h)[0], next_)

            st_inverse(N_HG - 1, 8, 1.0 / P)
            step(nc.vector.memset(reset[:, :], 1.0))
            step(nc.vector.memset(reset[:, :].rearrange("p (c t) -> p c t", t=P)[:, :, 0:1], 0.0))

            def chunks(buf, size):
                return buf.rearrange("p (n t) -> p n t", t=size)

            def hg_norm(h, bank):
                dve.wait_ge(st_bc, N_HG + h + 1)
                step(stt(mix[:, HEADS + h, :], mix[:, HEADS + h, :], col("hgn"), banks(bank), ALU.mult,
                         ALU.mult))
                dve.wait_ge(silu_done, h + 1)
                tt(mix[:, HEADS + h, :], mix[:, HEADS + h, :], hg[:, :], ALU.mult).then_inc(mix_ready, 1)

            for h in range(HEADS):
                u = U_HG + 5 * h
                hqh, hzh = hq[h % 2], hz[h % 2]
                o = (h + 1) % 2
                next_ = [hq[o][:, :], hz[o][0][:, :], hz[o][1][:, :], hv[:, :]]
                u_next = hg_fill(h)[0]
                slots = filling(*hg_fill(h), 2 * LEVELS + 4)
                if h == 0:
                    leave_half(u + 3, 0, hv[:, :])
                else:
                    st_inverse(N_HG + h - 1, 8, 1.0 / P)
                for d in range(2):
                    j = HEADS * d + h
                    dve.wait_ge(sig_done, 4 * h + 2 * d + 2)
                    ts(hd[:, d, :], hd[:, d, :], dcol("omlb", j), dcol("lb", j), ALU.mult,
                       ALU.add).then_inc(f_ready, 1)
                    step(ts(hk[:, d, :], hk[:, d, :], dcol("omlb", j), None, ALU.mult))
                if h == 0:
                    da_norm(HEADS - 1, 6)
                    leave_half(u + 3, 1, hv[:, :])
                    step(nc.vector.memset(hkt[:, 0, :], 0.0))
                    step(nc.vector.memset(hkt[:, 1, :], 0.0))
                for d in range(2):
                    dve.wait_ge(logf_done, 2 * h + d + 1)
                    if d == 0:
                        step(nc.vector.tensor_tensor_scan(hzh[d][:, :], reset[:, :], hd[:, d, :], 0.0,
                                                          ALU.mult, ALU.add))
                    else:
                        step(nc.vector.tensor_tensor_scan(hzh[d][:, ::-1], reset[:, :], hd[:, d, ::-1], 0.0,
                                                          ALU.mult, ALU.add))
                if h:
                    hg_norm(h - 1, 6)
                    dve.wait_ge(mix_ready, HEADS + h)
                leave(u + 4, hg[:, :])
                tt(hd[:, 0, :], hk[:, 0, :], hk[:, 1, :], ALU.add).then_inc(qk_lvl, 1)
                dve.wait_ge(lvl_mm, 15 * h + 1)
                tt(chunks(hatt[:, :], P), banks(4).rearrange("p (n t) -> p n t", t=P),
                   ident[:, :].rearrange("p (o t) -> p o t", o=1).to_broadcast([P, KT, P]),
                   ALU.mult).then_inc(att_put, 1)

                def halves(l, d):
                    hs = 1 << (l // 2)
                    lower, upper = slice(0, hs), slice(hs, 2 * hs)
                    return (2 * hs, upper, lower, hs - 1) if d == 0 else (2 * hs, lower, upper, hs)

                def distances(l):
                    d = l % 2
                    size, _, _, ref = halves(l, d)
                    b = chunks(hzh[d][:, :], size)
                    if l >= 2:
                        dve.wait_ge(qk_lvl, 15 * h + l)
                    tt(chunks(hd[:, d, :], size), b, b[:, :, ref:ref + 1].to_broadcast([P, T // size, size]),
                       ALU.subtract).then_inc(d_ready, 1)

                def operands(l):
                    d = l % 2
                    n = 15 * h + 1 + l
                    size, qs, ks, _ = halves(l, d)
                    dve.wait_ge(e_done, 34 * h + 2 * l + 2)
                    if l >= 2:
                        dve.wait_ge(lvl_mm, n - 1)
                    e = chunks(hd[:, d, :], size)
                    tt(chunks(hqt[:, d, :], size // 2), chunks(hqh[:, :], size)[:, :, qs], e[:, :, qs],
                       ALU.mult)
                    tt(chunks(hkt[:, d, :], size)[:, :, ks], chunks(hk[:, d, :], size)[:, :, ks], e[:, :, ks],
                       ALU.mult).then_inc(qk_lvl, 1)

                def put(l):
                    d = l % 2
                    n = 15 * h + 1 + l
                    size, qs, _, _ = halves(l, d)
                    dve.wait_ge(lvl_mm, n + 1)
                    dve.wait_ge(att_put, n)
                    nt = P // size
                    mask = (hmask[:, l, :].rearrange("p (o n t) -> p o n t", o=1, n=nt)
                            .to_broadcast([P, KT, nt, size // 2]))
                    out = hatt[:, :].rearrange("p (c n t) -> p c n t", c=KT, n=nt)[:, :, :, qs]
                    data = ps[:, 4 + d, :].rearrange("p (c n t) -> p c n t", c=KT, n=nt)
                    nc.vector.copy_predicated(out, mask, data).then_inc(att_put, 1)

                dve.wait_ge(hmask_in, 16)
                nl = 2 * LEVELS
                for l in range(nl + 2):
                    if l < nl:
                        distances(l)
                    if 1 <= l <= nl:
                        operands(l - 1)
                    if l >= 2:
                        put(l - 2)
                    if l >= 2:
                        evict(slots[l - 2], u_next, next_)

                for d in range(2):
                    b = chunks(hzh[d][:, :], P)
                    ref = P - 1 if d == 0 else 0
                    dve.wait_ge(qk_lvl, 15 * h + 15)
                    tt(chunks(hd[:, d, :], P), b, b[:, :, ref:ref + 1].to_broadcast([P, KT, P]),
                       ALU.subtract).then_inc(d_ready, 1)
                for d in range(2):
                    dve.wait_ge(e_done, 34 * h + 28 + 3 * d + 1)
                    dve.wait_ge(lvl_mm, 15 * h + 15)
                    tt(hkt[:, d, :], hk[:, d, :], hd[:, d, :], ALU.mult).then_inc(kd_ready, 1)
                evict(slots[2 * LEVELS], u_next, next_)
                dve.wait_ge(kd_ready, 2 * h + 2)
                for d in range(2):
                    n = 2 * h + d
                    dve.wait_ge(kv_mm, n + 1)
                    order = range(KT) if d == 0 else range(KT - 1, -1, -1)
                    order = list(order)
                    for a, c in zip(order[:-1], order[1:]):
                        kv = ps[:, 4 + a // 4, (a % 4) * P:(a % 4 + 1) * P]
                        dst = hk[:, d, c * P:(c + 1) * P]
                        if a == order[0]:
                            ins = nc.vector.tensor_copy(dst, kv)
                        else:
                            if a == order[1]:
                                dve.wait_ge(e_done, 34 * h + 28 + 3 * d + 2)
                            ins = stt(dst, hk[:, d, a * P:(a + 1) * P], heb[:, d, a:a + 1], kv, ALU.mult,
                                      ALU.add)
                        if c == order[-1]:
                            ins.then_inc(state_ready, 1)
                        else:
                            step(ins)
                    if d == 0:
                        evict(slots[2 * LEVELS + 1] + slots[2 * LEVELS + 2], u_next, next_)
                for d in range(2):
                    dve.wait_ge(e_done, 34 * h + 28 + 3 * d + 3)
                    tt(hzh[d][:, :], hqh[:, :], hd[:, d, :], ALU.mult).then_inc(qd_ready, 1)

                evict(slots[2 * LEVELS + 3], u_next, next_)
            st_inverse(N_HG + HEADS - 1, 8, 1.0 / P)
            hg_norm(HEADS - 1, 4)


            def split_mix(f0, m0):
                dve.wait_ge(mix_ready, m0 + KT)
                for k in range(KT):
                    dve.wait_ge(f_hi, f0 + k + 1)
                    tt(b_lo[:, k, :], mix[:, k, :], b_hi[:, k, :].bitcast(F32),
                       ALU.subtract).then_inc(f_lo, 1)

            def add_to_x(u, k):
                for hf in range(2):
                    c = slice(hf * HALF, (hf + 1) * HALF)
                    dve.wait_ge(acc_full, half_no(u, hf))
                    tt(x[:, k, c], ps[:, hf, :], x[:, k, c], ALU.add).then_inc(acc_free, 1)

            def out_projection(u0, f0, m0, turn, q, gain):
                split_mix(f0, m0)
                step(nc.vector.memset(ss[:, :], 0.0))
                for k in range(KT):
                    dve.wait_ge(x_in[k], 16 * turn)
                    add_to_x(u0 + k, k)
                    dve.wait_ge(acc_free, half_no(u0 + k, 1))
                    prep(q, k, col(gain, k), x[:, k, :])

            def down(u0, last, q=0, gain=None):
                if not last:
                    with dve.Fori(0, KT, 1) as i:
                        for hf in range(2):
                            dve.wait_ge(acc_full, half_no(u0 + i, hf))
                            xk = x[:, bass.ds(i, 1), hf * HALF:(hf + 1) * HALF].rearrange("p a b -> p (a b)")
                            tt(xk, ps[:, hf, :], xk, ALU.add).then_inc(acc_free, 1)
                    return
                step(nc.vector.memset(ss[:, :], 0.0))
                for k in range(KT):
                    add_to_x(u0 + k, k)
                    dve.wait_ge(acc_free, half_no(u0 + k, 1))
                    prep(q, k, col(gain, k), x[:, k, :])

            out_projection(U_OUT, F_MIX, 0, 2, Q_FFN, "norm_ffn")
            st_inverse(N_FFN, 8, 1.0 / T)
            dve.wait_ge(ss_ready, Q_FFN + KT)
            for s in range(2):
                step(nc.vector.memset(pad_a[:, s, 0:1], 0.0))
                step(nc.vector.memset(pad_a[:, s, T + 1:T + 2], 0.0))
            dve.wait_ge(rstd_ready, 2)

            def hidden_tile(u, s, f, fi):
                if not (isinstance(fi, int) and fi < 2):
                    dve.wait_ge(f_lo, f - 1)
                leave(u, pad_a[:, s, :], 1)
                dve.wait_ge(acc_free, half_no(u, 1))
                ts(c_buf[:, :], pad_a[:, s, 0:T], col("conv_w0", fi), col("conv_b", fi), ALU.mult,
                   ALU.add).then_inc(conv_done, 1)
                dve.wait_ge(conv_done, 3 * fi + 1)
                stt(c_buf[:, :], pad_a[:, s, 1:T + 1], col("conv_w1", fi), c_buf[:, :], ALU.mult,
                    ALU.add).then_inc(conv_done, 1)
                dve.wait_ge(conv_done, 3 * fi + 2)
                stt(c_buf[:, :], pad_a[:, s, 2:T + 2], col("conv_w2", fi), c_buf[:, :], ALU.mult,
                    ALU.add).then_inc(conv_done, 1)
                dve.wait_ge(conv_done, 3 * fi + 3)
                leave(u + 1, pad_a[:, s, :], 1)
                dve.wait_ge(acc_free, half_no(u + 1, 1))
                dve.wait_ge(act_done, fi + 1)
                tt(pad_a[:, s, 1:T + 1], c_buf[:, :], pad_a[:, s, 1:T + 1], ALU.mult).then_inc(fx_ready, 1)

            def remainder(f, s, j, first):
                dve.wait_ge(f_hi, f + 1)
                lo = b_lo[:, bass.ds(j, 1), :].rearrange("p a b -> p (a b)")
                hi = b_hi[:, bass.ds(j, 1), :].rearrange("p a b -> p (a b)").bitcast(F32)
                tt(lo, pad_a[:, s, first:first + T], hi, ALU.subtract).then_inc(f_lo, 1)

            fi = 0
            for gi, n in enumerate(GROUPS1):
                def pair(i):
                    for s in range(2):
                        t = fi + 2 * i + s
                        hidden_tile(U_GU[gi] + 4 * i + 2 * s, s, F_FF + t, t)
                        remainder(F_FF + t, s, 2 * i + s, 1)
                if gi == 0:
                    pair(0)
                with dve.Fori(1 if gi == 0 else 0, n // 2, 1) as i:
                    pair(i)
                fi += n
                down(U_DN[gi], gi == len(GROUPS1) - 1, Q_PLE, "norm_ple")
            st_inverse(N_PLE, 8, 1.0 / T)

            def embedding(u0, turn, rs):
                for k in range(PT):
                    dve.wait_ge(p_hi, 2 * turn + k + 1)
                    tt(b_lo[:, k, :], p_raw[:, k, :], b_hi[:, k, :].bitcast(F32),
                       ALU.subtract).then_inc(p_lo, 1)
                dve.wait_ge(rstd_ready, rs)
                dve.wait_ge(ss_ready, Q_PLE + KT if turn == 0 else Q_3 + KT)
                with dve.Fori(0, KT, 1) as i:
                    leave(u0 + 2 * i, pad_a[:, 0, :])
                    for hf in range(2):
                        dve.wait_ge(acc_full, half_no(u0 + 2 * i + 1, hf))
                        dve.wait_ge(pg_sig, KT * turn + i + 1)
                        tt(c_buf[:, hf * HALF:(hf + 1) * HALF], ps[:, hf, :],
                           pad_a[:, 0, hf * HALF:(hf + 1) * HALF], ALU.mult).then_inc(acc_free, 1)
                    dve.wait_ge(acc_free, half_no(u0 + 2 * i + 1, 1))
                    xk = x[:, bass.ds(i, 1), :].rearrange("p a b -> p (a b)")
                    tt(xk, xk, c_buf[:, :], ALU.add).then_inc(x_done, 1)
                    dve.wait_ge(x_done, KT * turn + i + 1)

            embedding(U_PLE, 0, 3)

            dve.wait_ge(x_done, KT)
            step(nc.vector.memset(ss[:, :], 0.0))
            step(nc.vector.memset(c_buf[:, :], 0.0))
            for k in range(KT):
                dve.wait_ge(h_hi, Q_1 + k + 1)
                stt(a_lo[:, k, :], x[:, k, :], dcol("fin_n1", k), a_hi[:, k, :].bitcast(F32), ALU.mult,
                    ALU.subtract).then_inc(h_lo, 1)
                dve.wait_ge(sq_ready, Q_1 + k + 1)
                dve.wait_ge(ss_ready, Q_1 + k)
                tt(ss[:, :], ss[:, :], sq[:, 0, 0:T], ALU.add).then_inc(ss_ready, 1)
                dve.wait_ge(sq2_ready, k + 1)
                if k:
                    dve.wait_ge(s2_ready, k)
                tt(c_buf[:, :], c_buf[:, :], sq[:, 1, 0:T], ALU.add).then_inc(s2_ready, 1)
            st_inverse(N_FIN, 8, 1.0 / T)
            dve.wait_ge(st_inv, N_FIN + 1)
            step(nc.vector.tensor_copy(sm[:, 0, 0:8], sm[:, 3, 0:8]))
            dve.wait_ge(st_sum, N_1 + 1)
            step(stt(sm[:, 1, 0:8], ps[:, 7, 0:8], 1.0 / T, sm[:, 0, 0:8], ALU.mult, ALU.mult))
            step(tt(sm[:, 1, 0:8], sm[:, 1, 0:8], sm[:, 0, 0:8], ALU.mult))
            ts(sm[:, 1, 0:8], sm[:, 1, 0:8], EPS, None, ALU.add).then_inc(st_var, 1)
            dve.wait_ge(st_root, N_1 + 1)
            step(nc.vector.reciprocal(sm[:, 3, 0:8], sm[:, 2, 0:8]))
            tt(sm[:, 3, 0:8], sm[:, 3, 0:8], sm[:, 0, 0:8], ALU.mult).then_inc(st_inv, 1)
            dve.wait_ge(st_bc, N_FIN + 2)
            for k in range(KT):
                stt(x[:, k, :], x[:, k, :], col("final", k), banks(5), ALU.mult,
                    ALU.mult).then_inc(xf_ready, 1)
            dve.wait_ge(rstd_ready, 4)

            def place(n):
                th, i, hh = PIECES[n]
                return th, i, hh, max(0, i - 4 * th) * P

            def z_leaves(p, n):
                _, _, _, c0 = place(n)
                s = NPC * p + n
                dve.wait_ge(z_mm, s + 1)
                if s >= 4:
                    dve.wait_ge(sw_exp, s - 3)
                nc.vector.tensor_copy(sz[:, s % 4, c0:], ps[:, 2 + s % 2, c0:]).then_inc(z_out, 1)

            def softplus(p, n):
                th, i, _, c0 = place(n)
                s = NPC * p + n
                dve.wait_ge(l_ready, s + 1)
                if s >= 4:
                    dve.wait_ge(sph_ready, s - 3)
                    dve.wait_ge(spl_ready, s - 3)
                ins = stt(sp[:, s % 4, c0:], sz[:, s % 4, c0:], 0.0, sl[:, s % 4, c0:], ALU.max, ALU.add)
                if i >= 4 * th:
                    step(ins)
                    ins = tt(sp[:, s % 4, c0:c0 + P], sp[:, s % 4, c0:c0 + P], ctri, ALU.mult)
                ins.then_inc(sp_ready, 1)

            def sp_low(p, n):
                c0 = place(n)[3]
                s = NPC * p + n
                dve.wait_ge(sp_ready, s + 1)
                dve.wait_ge(sph_ready, s + 1)
                if s >= 4:
                    dve.wait_ge(suf_mm, s - 2)
                tt(spl[:, s % 4, c0:], sp[:, s % 4, c0:], sph[:, s % 4, c0:].bitcast(F32),
                   ALU.subtract).then_inc(spl_ready, 1)

            def exponent(p, n):
                th, i, hh, c0 = place(n)
                s = NPC * p + n
                dve.wait_ge(suf_mm, s + 1)
                ins = tt(sz[:, s % 4, c0:], sz[:, s % 4, c0:], ps[:, 4 + hh, c0:], ALU.add)
                if i >= 4 * th:
                    step(ins)
                    ins = ts(sz[:, s % 4, c0:c0 + P], sz[:, s % 4, c0:c0 + P], 0.0, None, ALU.min)
                ins.then_inc(t_ready, 1)

            def causal(p, n):
                th, i, _, c0 = place(n)
                s = NPC * p + n
                if i >= 4 * th:
                    dve.wait_ge(sw_exp, s + 1)
                    tt(sw[:, s % 4, c0:c0 + P], sw[:, s % 4, c0:c0 + P], ctri, ALU.mult).then_inc(sw_ready, 1)

            leave(U_SB, sk[0][:, 0, :])
            leave(U_SB + 1, sk[0][:, 1, :])
            for p in range(HEADS):
                u = U_SB + 3 * p
                n = N_QK + p
                st_inverse(n, 32, 1.0 / 64)
                leave_half(u + 2, 0, sv[:, :])
                dve.wait_ge(st_bc, n + 1)
                for t, gain in enumerate((dcol("qn"), col("kn"))):
                    stt(sk[p % 2][:, t, :], sk[p % 2][:, t, :], gain, banks(4 - 2 * t), ALU.mult,
                        ALU.mult).then_inc(qk2_ready, 1)
                leave_half(u + 2, 1, sv[:, :])
                slots = filling(*sb_fill(p), NPC + 3)
                u_next = sb_fill(p)[0]
                if p + 1 < HEADS:
                    next_ = [sk[(p + 1) % 2][:, 0, :], sk[(p + 1) % 2][:, 1, :]]
                else:
                    next_ = [cc[:, j, :] for j in range(3)]
                dve.wait_ge(x_out, 16 * KT)
                for n in range(NPC + 4):
                    if n < NPC:
                        z_leaves(p, n)
                    if 1 <= n <= NPC:
                        softplus(p, n - 1)
                    if n:
                        evict(slots[n - 1], u_next, next_)
                    if 2 <= n <= NPC + 1:
                        exponent(p, n - 2)
                    if 1 <= n <= NPC:
                        sp_low(p, n - 1)
                    if 3 <= n <= NPC + 2:
                        causal(p, n - 3)

            dve.wait_ge(so_out, 4 * HEADS)
            step(nc.vector.memset(cp[:, 0:2], 0.0))
            for j in range(2):
                u = U_CV + 3 * j
                if j:
                    dve.wait_ge(mix_ready, 2 * HEADS + j)
                if j:
                    for n in range(3):
                        leave(u + n, cc[:, n, :])
                dve.wait_ge(acc_free, half_no(u + 2, 1))
                step(tt(cp[:, 2:T + 2], cc[:, 0, :], cc[:, 1, :], ALU.mult))
                step(ts(cc[:, 0, :], cp[:, 0:T], col("conv2_w0", j), None, ALU.mult))
                step(stt(cc[:, 0, :], cp[:, 1:T + 1], col("conv2_w1", j), cc[:, 0, :], ALU.mult, ALU.add))
                step(stt(cc[:, 0, :], cp[:, 2:T + 2], col("conv2_w2", j), cc[:, 0, :], ALU.mult, ALU.add))
                tt(mix[:, j, :], cc[:, 0, :], cc[:, 2, :], ALU.mult).then_inc(mix_ready, 1)

            dve.wait_ge(gate_in, 48)
            tt(gw[:, :, :], gw[:, :, :], gmask[:, :].rearrange("p (o t) -> p o t", o=1)
               .to_broadcast([P, 4, P]), ALU.mult).then_inc(gw_ready, 1)
            for j in range(2):
                u = U_SG + 2 * j
                if j:
                    dve.wait_ge(mix_ready, 2 * HEADS + 2 + j)
                leave(u, gv[:, 0, :])
                leave(u + 1, gv[:, 1, :])
                st_inverse(N_SG + j, 16, 1.0 / 64)
                dve.wait_ge(st_bc, N_SG + j + 1)
                stt(gv[:, 0, :], gv[:, 0, :], col("sgu_g", j), banks(4), ALU.mult,
                    ALU.mult).then_inc(gn_ready, 1)
                dve.wait_ge(gs_mm, j + 1)
                for hh in range(2):
                    r = slice(64 * hh, 64 * hh + 64)
                    tt(chunks(mix[r, 6 + j, :], P), banks(4 + 2 * hh)[r, :].rearrange("p (n t) -> p n t", t=P),
                       gb[r, j, :].rearrange("p (o t) -> p o t", o=1).to_broadcast([64, KT, P]),
                       ALU.add).then_inc(g_done, 1)
                dve.wait_ge(g_done, 2 * j + 2)
                dve.wait_ge(gelu_done, 2 * j + 2)
                tt(mix[:, 6 + j, :], mix[:, 6 + j, :], gv[:, 1, :], ALU.mult).then_inc(mix_ready, 1)

            out_projection(U_OUT2, F_MIX2, 2 * HEADS - 4, 3, Q_2, "norm2")
            st_inverse(N_2, 8, 1.0 / T)
            dve.wait_ge(ss_ready, Q_2 + KT)
            dve.wait_ge(rstd_ready, 5)

            def hidden2(u, s, f, fi):
                if not (isinstance(fi, int) and fi < 2):
                    dve.wait_ge(f_lo, f - 1)
                if not (isinstance(fi, int) and fi < 1):
                    dve.wait_ge(fx_ready, FT + fi)
                leave(u, c_buf[:, :])
                dve.wait_ge(acc_free, half_no(u, 1))
                stt(pad_a[:, s, 0:T], c_buf[:, :], 0.0, c_buf[:, :], ALU.max, ALU.mult).then_inc(fx_ready, 1)
                dve.wait_ge(fx_ready, FT + fi + 1)

            fi = 0
            for gi, n in enumerate(GROUPS2):
                def pair2(i):
                    for s in range(2):
                        t = fi + 2 * i + s
                        hidden2(U_F1[gi] + 2 * i + s, s, F_FF2 + t, t)
                        remainder(F_FF2 + t, s, 2 * i + s, 0)
                if gi == 0:
                    pair2(0)
                with dve.Fori(1 if gi == 0 else 0, n // 2, 1) as i:
                    pair2(i)
                fi += n
                down(U_F2[gi], gi == len(GROUPS2) - 1, Q_3, "norm3")
            st_inverse(N_3, 8, 1.0 / T)
            embedding(U_PLE2, 1, 6)

        @block.scalar
        def _(act):
            def av(out, in_, f, **kw):
                return nc.scalar.activation(out, in_, f, **kw)

            steps = [0]

            def step(ins):
                ins.then_inc(act_step, 1)
                steps[0] += 1
                act.wait_ge(act_step, steps[0])

            def until(sem_, value):
                act.wait_ge(sem_, value)
                act.wait_ge(param_in, 48)

            def col(name, j=0, n=1):
                return vec[:, VEC[name] + j:VEC[name] + j + n]

            def dcol(name, j=0, n=1):
                return der[:, DER[name] + j:DER[name] + j + n]

            def prep(q, k, gain, xk):
                av(a_hi[:, k, :], xk, ACT.Copy, scale=gain).then_inc(h_hi, 1)
                if q + k >= 2:
                    act.wait_ge(ss_ready, q + k - 1)
                av(sq[:, k % 2, 0:T], xk, ACT.Square).then_inc(sq_ready, 1)

            def st_sqrt(n, ncols):
                act.wait_ge(st_var, n + 1)
                av(sm[:, 2, 0:ncols], sm[:, 1, 0:ncols], ACT.Sqrt).then_inc(st_root, 1)

            def keep_rstd(bc):
                act.wait_ge(st_bc, bc)
                av(rstd[:, :], banks(5), ACT.Copy).then_inc(rstd_ready, 1)

            act.wait_ge(g_ready, 1)
            step(av(dcol("g0", 0, 8), dcol("g0", 0, 8), ACT.Exp))
            step(av(dcol("g1", 0, 8), dcol("g1", 0, 8), ACT.Exp))
            act.wait_ge(lam_mm, 1)
            av(dcol("lame", 0, 2), ps[:, 7, 0:2], ACT.Exp).then_inc(lam_exp, 1)
            act.wait_ge(param_in, 48)
            for k in range(KT):
                act.wait_ge(x_in[k], 16)
                prep(Q_MIX, k, col("norm_mix", k), x[:, k, :])
            st_sqrt(N_MIX, 8)
            keep_rstd(N_MIX + 1)
            for n, m in enumerate((sinm, cosm)):
                act.wait_ge(ang_ready, n + 1)
                av(m[:, :], m[:, :], ACT.Sin).then_inc(cs_ready, 1)

            def exps(h, qt, m):
                g = KT * h + qt
                act.wait_ge(max_ready, 2 * g + m + 1)
                if g >= 2:
                    act.wait_ge(w_tr, 2 * (g - 1))
                av(de[:, g % 2, m, :], banks(2 + 2 * m), ACT.Exp, scale=0.125, bias=rows[:, m, 1:2],
                   accum_out=rows[:, g % 2, 2 + m:3 + m]).then_inc(exp_done, 1)

            def turned(h, qt, r):
                g = KT * h + qt
                act.wait_ge(w_tr, 2 * g + r + 1)
                if g:
                    act.wait_ge(o_mm, g)
                av(dwt[:, r, :], ps[:, 6, :], ACT.Copy).then_inc(wt_ready, 1)
                if r == 1 and qt in (3, 7):
                    act.wait_ge(o_mm, g + 1)
                    hf = qt // 4
                    av(mix[:, h, hf * HALF:(hf + 1) * HALF], ps[:, 7, :], ACT.Copy).then_inc(o_out, 1)

            for h in range(HEADS):
                if h:
                    st_sqrt(N_DA + h - 1, 8)
                act.wait_ge(v_tr, h + 1)
                av(dvt[:, :, :], banks(2).rearrange("p (c e) -> p c e", c=KT), ACT.Copy).then_inc(v_ready, 1)
                for qt in range(KT + 1):
                    for m in range(2):
                        if qt < KT:
                            exps(h, qt, m)
                        if qt:
                            turned(h, qt - 1, m)
                act.wait_ge(o_out, 2 * h + 2)
                if h:
                    act.wait_ge(st_sum, N_DA + h)
                av(ang[:, :], mix[:, h, :], ACT.Square).then_inc(o_sq, 1)

            act.dma_start(hmask[:, :, :], io["hmask"]).then_inc(hmask_in, 16)
            for h in range(HEADS):
                u = U_HG + 5 * h
                hzh = hz[h % 2]
                st_sqrt(N_HG + h - 1, 8)
                if h:
                    act.wait_ge(qd_ready, 2 * h)
                for d in range(2):
                    act.wait_ge(acc_free, half_no(u + 1 + d, 1))
                    av(hd[:, d, :], hzh[d][:, :], ACT.Sigmoid).then_inc(sig_done, 1)
                    av(hk[:, d, :], hzh[d][:, :], ACT.Sigmoid, scale=-1.0).then_inc(sig_done, 1)
                nc.scalar.preload_act_table_set("natural_log_exp_and_others")
                for d in range(2):
                    act.wait_ge(f_ready, 2 * h + d + 1)
                    av(hd[:, d, :], hd[:, d, :], ACT.Ln).then_inc(logf_done, 1)
                act.wait_ge(v_tr, HEADS + h + 1)
                av(hvt[:, :, :], banks(2).rearrange("p (c e) -> p c e", c=KT), ACT.Copy).then_inc(v_ready, 1)
                for l in range(2 * LEVELS):
                    d = l % 2
                    hs = 1 << (l // 2)
                    lower, upper = slice(0, hs), slice(hs, 2 * hs)
                    qs, ks = (upper, lower) if d == 0 else (lower, upper)
                    act.wait_ge(d_ready, 16 * h + l + 1)
                    e = hd[:, d, :].rearrange("p (n t) -> p n t", t=2 * hs)
                    av(e[:, :, qs], e[:, :, qs], ACT.Exp).then_inc(e_done, 1)
                    av(e[:, :, ks], e[:, :, ks], ACT.Exp, scale=-1.0).then_inc(e_done, 1)
                for d in range(2):
                    ref = P - 1 if d == 0 else 0
                    act.wait_ge(d_ready, 16 * h + 14 + d + 1)
                    av(hd[:, d, :], hd[:, d, :], ACT.Exp, scale=-1.0).then_inc(e_done, 1)
                    far = hzh[d][:, :].rearrange("p (c t) -> p c t", t=P)[:, :, ref:ref + 1]
                    av(heb[:, d, :].rearrange("p (c t) -> p c t", t=1), far, ACT.Exp).then_inc(e_done, 1)
                    act.wait_ge(kd_ready, 2 * h + d + 1)
                    av(hd[:, d, :], hzh[d][:, :], ACT.Exp).then_inc(e_done, 1)
                for d in range(2):
                    act.wait_ge(kd_tr, 2 * h + d + 1)
                    if d:
                        act.wait_ge(kv_mm, 2 * h + 1)
                    av(hkd[:, :, :], banks(2).rearrange("p (c e) -> p c e", c=KT),
                       ACT.Copy).then_inc(kdt_ready, 1)
                act.wait_ge(acc_free, half_no(u + 4, 1))
                av(hg[:, :], hg[:, :], ACT.Silu).then_inc(silu_done, 1)
                act.wait_ge(ho_mm, h + 1)
                av(mix[:, HEADS + h, :], banks(6), ACT.Copy).then_inc(ho_out, 1)
                act.wait_ge(ho_out, h + 1)
                av(hkd_flat, mix[:, HEADS + h, :], ACT.Square).then_inc(o_sq, 1)

            st_sqrt(N_HG + HEADS - 1, 8)

            def split_mix(f0, m0, source):
                act.wait_ge(mix_ready, m0 + KT)
                for k in range(KT):
                    av(b_hi[:, k, :], mix[:, k, :], ACT.Copy).then_inc(f_hi, 1)
                for k in range(KT):
                    act.wait_ge(f_lo, f0 + k + 1)
                    act.dma_start(x[:, k, :], source[:, k, :]).then_inc(x_in[k], 16)

            def preps(q, u0, gain):
                for k in range(KT):
                    act.wait_ge(acc_free, half_no(u0 + k, 1))
                    prep(q, k, col(gain, k), x[:, k, :])

            def high(f, s, j, first, fx):
                until(fx_ready, fx)
                av(b_hi[:, bass.ds(j, 1), :].rearrange("p a b -> p (a b)"), pad_a[:, s, first:first + T],
                   ACT.Copy).then_inc(f_hi, 1)

            split_mix(F_MIX, 0, io["x"])
            preps(Q_FFN, U_OUT, "norm_ffn")
            st_sqrt(N_FFN, 8)
            keep_rstd(N_FFN + 1)
            fi = 0
            for gi, n in enumerate(GROUPS1):
                with act.Fori(0, n // 2, 1) as i:
                    for s in range(2):
                        t = fi + 2 * i + s
                        until(conv_done, 3 * t + 3)
                        av(c_buf[:, :], c_buf[:, :], ACT.Gelu).then_inc(act_done, 1)
                        high(F_FF + t, s, 2 * i + s, 1, t + 1)
                fi += n
            preps(Q_PLE, U_DN[-1], "norm_ple")

            def embedding(u0, turn, name, bc, u_last):
                act.wait_ge(acc_free, half_no(u_last + KT - 1, 1))
                act.dma_start(p_raw[:, :, :], io[name]).then_inc(p_in, 16)
                keep_rstd(bc)
                act.wait_ge(p_in, 16 * (turn + 1))
                for k in range(PT):
                    av(b_hi[:, k, :], p_raw[:, k, :], ACT.Copy).then_inc(p_hi, 1)
                with act.Fori(0, KT, 1) as i:
                    until(acc_free, half_no(u0 + 2 * i, 1))
                    av(pad_a[:, 0, 0:T], pad_a[:, 0, 0:T], ACT.Sigmoid).then_inc(pg_sig, 1)
                    if turn:
                        act.wait_ge(x_done, KT + i + 1)
                        act.dma_start(io["out"][:, bass.ds(i, 1), :], x[:, bass.ds(i, 1), :]).then_inc(out_done, 16)

            st_sqrt(N_PLE, 8)
            embedding(U_PLE, 0, "p", N_PLE + 1, U_DN[-1])

            act.wait_ge(x_done, KT)
            for k in range(KT):
                av(a_hi[:, k, :], x[:, k, :], ACT.Copy, scale=dcol("fin_n1", k)).then_inc(h_hi, 1)
                act.wait_ge(ss_ready, Q_1 + k)
                av(sq[:, 0, 0:T], x[:, k, :], ACT.Square).then_inc(sq_ready, 1)
                if k:
                    act.wait_ge(s2_ready, k)
                av(sq[:, 1, 0:T], x[:, k, :], ACT.Square, scale=col("final", k)).then_inc(sq2_ready, 1)
            st_sqrt(N_FIN, 8)
            st_sqrt(N_1, 8)
            keep_rstd(N_FIN + 1)
            act.dma_start(tri_raw[:, :, :], io["tri"]).then_inc(tri_in, 16)
            act.wait_ge(tri_in, 16)
            for n in range(2):
                av(tri[:, n, :], tri_raw[:, n, :], ACT.Copy).then_inc(tri_ready, 1)
            for k in range(KT):
                act.wait_ge(xf_ready, k + 1)
                act.dma_start(x_back[:, k, :], x[:, k, :]).then_inc(x_out, 16)

            def soft(p, n, part):
                th, i, _ = PIECES[n]
                c0 = max(0, i - 4 * th) * P
                s = NPC * p + n
                out = sl[:, s % 4, c0:]
                if part == 0:
                    act.wait_ge(z_out, s + 1)
                    if s >= 4:
                        act.wait_ge(sp_ready, s - 3)
                    av(out, sz[:, s % 4, c0:], ACT.Abs).then_inc(z_abs, 1)
                elif part == 1:
                    act.wait_ge(z_abs, s + 1)
                    av(out, out, ACT.Exp, scale=-1.0).then_inc(z_exp, 1)
                else:
                    act.wait_ge(z_exp, s + 1)
                    av(out, out, ACT.Ln, bias=1.0).then_inc(l_ready, 1)

            def sp_high(p, n):
                th, i, _ = PIECES[n]
                c0 = max(0, i - 4 * th) * P
                s = NPC * p + n
                act.wait_ge(sp_ready, s + 1)
                if s >= 4:
                    act.wait_ge(spl_ready, s - 3)
                    act.wait_ge(suf_mm, s - 2)
                av(sph[:, s % 4, c0:], sp[:, s % 4, c0:], ACT.Copy).then_inc(sph_ready, 1)

            def weight(p, n):
                th, i, hh = PIECES[n]
                c0 = max(0, i - 4 * th) * P
                s = NPC * p + n
                act.wait_ge(t_ready, s + 1)
                if s >= 4:
                    act.wait_ge(so_mm, s - 3)
                av(sw[:, s % 4, c0:], sz[:, s % 4, c0:], ACT.Exp).then_inc(sw_exp, 1)

            def out_rows(p, n):
                th, i, hh = PIECES[n]
                s = NPC * p + n
                if i == 0:
                    act.wait_ge(so_mm, s + 1)
                    r = slice(64 * hh, 64 * hh + 64)
                    av(mix[r, 2 + p, th * HALF:(th + 1) * HALF], ps[r, 6 + hh, :], ACT.Copy).then_inc(so_out, 1)

            def square(p, t):
                act.wait_ge(acc_free, half_no(U_SB + 3 * p + t, 1))
                act.wait_ge(st_sum, N_QK + p)
                av((c_buf, ss)[t][:, :], sk[p % 2][:, t, :], ACT.Square).then_inc(sq_qk, 1)

            square(0, 0)
            square(0, 1)
            for p in range(HEADS):
                st_sqrt(N_QK + p, 32)
                nc.scalar.preload_act_table_set("natural_log_exp_and_others")
                act.wait_ge(sv_tr, p + 1)
                av(svt[:, :, :], banks(6).rearrange("p (c e) -> p c e", c=KT), ACT.Copy).then_inc(sv_ready, 1)
                act.wait_ge(x_out, 16 * KT)
                for n in range(NPC + 5):
                    if n < NPC:
                        soft(p, n, 0)
                    if 3 <= n <= NPC + 2:
                        weight(p, n - 3)
                    if n < NPC:
                        soft(p, n, 1)
                    if 1 <= n <= NPC:
                        sp_high(p, n - 1)
                    if n < NPC:
                        soft(p, n, 2)
                    if n >= 5:
                        out_rows(p, n - 5)
                    if n == 20 and p + 1 < HEADS:
                        square(p + 1, 0)
                if p + 1 < HEADS:
                    square(p + 1, 1)

            act.wait_ge(so_out, 4 * HEADS)
            act.dma_start(gw[:, :, :], io["gw"]).then_inc(gate_in, 16)
            act.dma_start(gb[:, :, :], io["gb"]).then_inc(gate_in, 16)
            act.dma_start(gmask[:, :], io["gmask"]).then_inc(gate_in, 16)
            for j in range(2):
                u = U_SG + 2 * j
                for n in range(2):
                    act.wait_ge(acc_free, half_no(u + n, 1))
                    av(gv[:, n, :], gv[:, n, :], ACT.Gelu).then_inc(gelu_done, 1)
                    if n == 0:
                        act.wait_ge(gelu_done, 2 * j + 1)
                        act.wait_ge(st_sum, N_SG + j)
                        av(c_buf[:, :], gv[:, 0, :], ACT.Square).then_inc(g_sq, 1)
                st_sqrt(N_SG + j, 16)
                act.wait_ge(g_tr, j + 1)
                av(gvt[:, :, :], banks(2).rearrange("p (c e) -> p c e", c=KT), ACT.Copy).then_inc(gt_ready, 1)

            split_mix(F_MIX2, 2 * HEADS - 4, x_back)
            preps(Q_2, U_OUT2, "norm2")
            st_sqrt(N_2, 8)
            keep_rstd(N_2 + 1)
            fi = 0
            for gi, n in enumerate(GROUPS2):
                with act.Fori(0, n // 2, 1) as i:
                    for s in range(2):
                        t = fi + 2 * i + s
                        high(F_FF2 + t, s, 2 * i + s, 0, FT + t + 1)
                fi += n
            preps(Q_3, U_F2[-1], "norm3")
            st_sqrt(N_3, 8)
            embedding(U_PLE2, 1, "p2", N_3 + 1, U_F2[-1])


def constants():
    f = np.float32
    ident = np.eye(P, dtype=f)
    cst = np.zeros((P, 8), f)
    cst[:, 0] = 1.0
    cst[:64, 1] = 1.0
    cst[64:, 2] = 1.0
    half = 8
    freq = f(500000.0) ** (-np.arange(half, dtype=f) / f(half))
    swap = np.zeros((P, P), f)
    for m in range(2):
        for j in range(half):
            a, b = 64 * m + j, 64 * m + half + j
            cst[a, 3] = cst[b, 3] = freq[j]
            swap[b, a] = -1.0
            swap[a, b] = 1.0
    s = np.arange(P)[:, None]
    t = np.arange(P)[None, :]
    tri = np.stack([-(s >= t).astype(f), -(s < t).astype(f), (s < t).astype(f)], 1)
    mask = np.zeros((P, 2 * LEVELS, 64), np.int32)
    for l in range(2 * LEVELS):
        hs = 1 << (l // 2)
        for idx in range(64):
            blk = idx // hs
            lo = blk * 2 * hs + (0 if l % 2 == 0 else hs)
            mask[lo:lo + hs, l, idx] = 1
    return {"ident": ident, "cst": cst, "swap": swap, "tri": np.ascontiguousarray(tri), "hmask": mask,
            "gmask": (s <= t).astype(f)}


def kernel(**inputs):
    import concourse.bacc as bacc
    from concourse.bass_utils import run_bass_kernel_spmd

    v = {k: np.asarray(a) for k, a in inputs.items()}

    def tiles(w, order=None):
        kt, nt = w.shape[0] // P, w.shape[1] // P
        w = w.reshape(kt, P, nt, P).transpose(2, 1, 0, 3).reshape(nt, P, kt * P)
        return w if order is None else w[order]

    def cols(a, n):
        return np.ascontiguousarray(np.asarray(a).reshape(n, P).T)

    def feature_major(a, n):
        return np.ascontiguousarray(a.T.reshape(n, P, -1).transpose(1, 0, 2))

    arrays = dict(constants())
    arrays["x"] = feature_major(v["x"][0], KT)
    arrays["p"] = feature_major(v["p"][0, 0], PT)
    arrays["p2"] = feature_major(v["p_2"][0, 0], PT)
    arrays["pos"] = np.ascontiguousarray(np.broadcast_to(v["positions"].reshape(1, T), (P, T)))
    vecs = {
        "norm_mix": cols(v["norm_mix_g"], 8), "norm_ffn": cols(v["norm_ffn_g"], 8),
        "norm_ple": cols(v["norm_ple_g"], 8), "final": cols(v["final_norm_g"], 8),
        "norm1": cols(v["norm1_g_2"], 8), "norm2": cols(v["norm2_g_2"], 8),
        "norm3": cols(v["norm3_g_2"], 8), "conv_b": cols(v["ffn_conv_b"], FT),
        "qn": cols(np.tile(v["q_norm_g_2"][0], 2), 1), "kn": cols(np.tile(v["k_norm_g_2"][0], 2), 1),
        "sgu_g": cols(v["sgu_norm_g_2"], 2), "subln": cols(v["da_subln_g"], 1),
        "hgn": cols(v["hg_norm_g"], 1), "gamma0": cols(v["hg_lb_gamma"][:, 0], 8),
        "gamma1": cols(v["hg_lb_gamma"][:, 1], 8),
    }
    for j in range(3):
        vecs[f"conv_w{j}"] = cols(v["ffn_conv_w"][0, j], FT)
        vecs[f"conv2_w{j}"] = cols(v["conv_w_2"][0, j], 2)
    lam = np.zeros((P, 4), v["lam_q1"].dtype)
    for j, name in enumerate(("lam_q1", "lam_k1", "lam_q2", "lam_k2")):
        lam[:64, j] = v[name][0]
    vecs["lam"] = lam
    arrays["vec"] = np.ascontiguousarray(np.concatenate([vecs[n] for n in VEC], 1))

    order = [t * HEADS + h for h in range(HEADS) for t in range(3)]
    order += [(3 + t) * HEADS + h for h in range(HEADS) for t in range(5)]
    arrays["w_mix"] = tiles(v["w_in"][0], order)
    arrays["w_out"] = tiles(v["w_out"][0])
    gate, up, dn = tiles(v["w_ffn_gate"][0]), tiles(v["w_ffn_up"][0]), v["w_ffn_down"][0]
    f = 0
    for gi, n in enumerate(GROUPS1):
        arrays[f"w_gu{gi}"] = np.stack([gate[f:f + n], up[f:f + n]], 1).reshape(2 * n, P, T)
        arrays[f"w_dn{gi}"] = tiles(dn[f * P:(f + n) * P])
        f += n

    def ple(gate_w, emb_w):
        g, e = tiles(gate_w), tiles(emb_w)
        out = np.zeros((KT, 2, P, T), g.dtype)
        out[:, 0] = g
        out[:, 1, :, :PT * P] = e
        return out.reshape(2 * KT, P, T)

    arrays["w_ple"] = ple(v["w_ple_gate"][0], v["w_ple"][0])
    order = [b + p for p in range(HEADS) for b in (6, 10, 14)]
    order += [b + j for j in range(2) for b in (2, 4, 0)] + [b + j for j in range(2) for b in (20, 18)]
    arrays["w_mix2"] = tiles(v["w_in_2"][0], order)
    arrays["w_out2"] = tiles(v["w_out_2"][0])
    f1, f2 = tiles(v["w_ff1_2"][0]), v["w_ff2_2"][0]
    f = 0
    for gi, n in enumerate(GROUPS2):
        arrays[f"w_f1{gi}"] = f1[f:f + n]
        arrays[f"w_f2{gi}"] = tiles(f2[f * P:(f + n) * P])
        f += n
    arrays["w_ple2"] = ple(v["w_ple_gate_2"][0], v["w_ple_proj_2"][0])
    arrays["gw"] = v["sgu_w_2"][0].transpose(2, 0, 1)
    arrays["gb"] = np.repeat(v["sgu_b_2"][0].reshape(2, 2, 1, P), 64, axis=2).reshape(2, P, P).transpose(1, 0, 2)

    nc = bacc.Bacc("TRN2", target_bir_lowering=False, num_devices=1)
    arrays = {k: np.ascontiguousarray(a) for k, a in arrays.items()}
    io = {k: nc.dram_tensor(f"in_{k}", a.shape, mybir.dt.from_np(a.dtype), kind="ExternalInput").ap()
          for k, a in arrays.items()}
    io["out"] = nc.dram_tensor("out_x", (P, KT, T), F32, kind="ExternalOutput").ap()
    bass_two_blocks(nc, io)
    r = run_bass_kernel_spmd(nc, [{f"in_{k}": a for k, a in arrays.items()}], core_ids=[0])
    out = r.results[0]["out_x"]
    return np.ascontiguousarray(out.transpose(1, 0, 2).reshape(KT * P, T).T).reshape(1, T, KT * P)
```

```python
from contextlib import ExitStack

import numpy as np

import concourse.bass as bass
from concourse import mybir

F32 = mybir.dt.float32
F32R = mybir.dt.float32r
I32 = mybir.dt.int32
ALU = mybir.AluOpType
ACT = mybir.ActivationFunctionType
AX_X = mybir.AxisListType.X

P = 128
T = 1024
HALF = 512
KT = 8
FT = 22
FT2 = 32
PT = 2
GROUPS1 = (8, 8, 6)
GROUPS2 = (8, 6, 6, 6, 6)
NE = 2
HEADS = 4
LEVELS = 7
EPS = 1e-6
SBUF_BASE = 16512
LAMBDA_INIT = 0.2
TWO_PI = 2.0 * np.pi

VEC = {}
_at = 0
for _name, _n in (("norm_mix", 8), ("norm_ffn", 8), ("norm_ple", 8), ("final", 8), ("norm1", 8),
                  ("norm2", 8), ("norm3", 8), ("conv_w0", FT), ("conv_w1", FT), ("conv_w2", FT),
                  ("conv_b", FT), ("conv2_w0", 2), ("conv2_w1", 2), ("conv2_w2", 2), ("qn", 1),
                  ("kn", 1), ("sgu_g", 2), ("subln", 1), ("hgn", 1), ("gamma0", 8), ("gamma1", 8),
                  ("lam", 4)):
    VEC[_name] = _at
    _at += _n
NVEC = _at
DER = {}
_at = 0
for _name, _n in (("fin_n1", 8), ("subln", 1), ("qn", 1), ("neg_lam", 1), ("lb", 8), ("omlb", 8),
                  ("g0", 8), ("g1", 8), ("lamp", 2), ("lame", 2), ("zero", 1)):
    DER[_name] = _at
    _at += _n
NDER = _at

U_DA = 0
U_HG = U_DA + 3 * HEADS
U_OUT = U_HG + 5 * HEADS
U_GU = []
U_DN = []
_u = U_OUT + KT
for _n in GROUPS1:
    U_GU.append(_u)
    _u += 2 * _n
    U_DN.append(_u)
    _u += KT
U_PLE = _u
U_SB = U_PLE + NE + KT
U_CV = U_SB + 3 * HEADS
U_SV = U_CV + 3
U_CV1 = U_SV + 2
U_SU = U_CV1 + 3
U_OUT2 = U_SU + 2
U_F1 = []
U_F2 = []
_u = U_OUT2 + KT
for _n in GROUPS2:
    U_F1.append(_u)
    _u += _n
    U_F2.append(_u)
    _u += KT
U_PLE2 = _u
U_END = U_PLE2 + NE + KT

N_MIX = 0
N_DA = 1
N_HG = N_DA + HEADS
N_FFN = N_HG + HEADS
N_PLE = N_FFN + 1
N_FIN = N_PLE + 1
N_1 = N_FIN + 1
N_QK = N_1 + 1
N_SG = N_QK + HEADS
N_2 = N_SG + 1
N_3 = N_2 + 1


F_MIX = 0
F_FF = F_MIX + KT
F_MIX2 = F_FF + FT
F_FF2 = F_MIX2 + KT
Q_MIX, Q_FFN, Q_PLE, Q_1, Q_2, Q_3 = range(0, 6 * KT, KT)

MAGIC = 1.5 * 2.0**23
_c2 = np.floor((TWO_PI - 6.28125) * 2.0**20) / 2.0**20
TURN = (6.28125, float(_c2), float(np.float32(TWO_PI - 6.28125 - _c2)))


def half_no(u, hf):
    return 2 * u + hf + 1


def stick_pieces():
    return [(th, i, hh) for th in range(2) for i in range(4 * th + 3, -1, -1) for hh in range(2)]


PIECES = stick_pieces()
NPC = len(PIECES)


def diagonal_no(p, n):
    in_pair = [i >= 4 * th for th, i, _ in PIECES]
    return sum(in_pair) * p + sum(in_pair[:n + 1])


def filling(u0, n, slots):
    steps = [(u, hf, k) for u in range(u0, u0 + n) for hf in range(2) for k in range(KT)]
    return [steps[i * len(steps) // slots:(i + 1) * len(steps) // slots] for i in range(slots)]


def finished(slot):
    return [(u, hf) for u, hf, k in slot if k == KT - 1]


def da_fill(h):
    return (U_DA + 3 * (h + 1), 2) if h + 1 < HEADS else (U_HG, 3)


def hg_fill(h):
    return (U_HG + 5 * (h + 1), 3) if h + 1 < HEADS else (U_OUT, 0)


def sb_fill(p):
    return (U_SB + 3 * (p + 1), 2) if p + 1 < HEADS else (U_CV, 3)


def bass_two_blocks(nc, io):
    ctx = ExitStack()
    with ctx:
        def at(name, cols, off, dt=F32, parts=P):
            shape = [parts, *cols] if isinstance(cols, tuple) else [parts, cols]
            return nc.alloc_sbuf_tensor_at(name, shape, dt, offset=SBUF_BASE + off)

        def sem(name):
            return ctx.enter_context(nc.semaphore(name))


        KB = 1024
        a_hi = at("a_hi", (KT, T), 0, F32R)
        a_lo = at("a_lo", (KT, T), 32 * KB, F32R)
        b_hi = at("b_hi", (KT, T), 64 * KB, F32R)
        b_lo = at("b_lo", (KT, T), 96 * KB, F32R)
        x = at("x", (KT, T), 128 * KB)
        mix = at("mix", (KT, T), 128 * KB)
        w_raw = at("w_raw", (2, T), 160 * KB)
        w_hi = at("w_hi", (2, T), 168 * KB, F32R)
        w_lo = at("w_lo", (2, T), 176 * KB, F32R)
        rstd = at("rstd", T, 184 * KB)
        TMP = 188 * KB
        pad_a = at("pad_a", (2, 1032), TMP)
        sq = at("sq", (2, 1032), TMP)
        c_buf = at("c_buf", T, TMP + 8256)
        ss = at("ss", T, TMP + 8256 + 4096)
        CST = TMP + 8256 + 8192
        ident = at("ident", P, CST)
        cst = at("cst", 8, CST + 512)
        vec = at("vec", NVEC, CST + 544)
        VEC_END = CST + 544 + (4 * NVEC + 31) // 32 * 32
        der = at("der", NDER, VEC_END)
        sm = at("sm", (4, 32), VEC_END + (4 * NDER + 31) // 32 * 32)
        SM_END = VEC_END + (4 * NDER + 31) // 32 * 32 + 512
        rows = at("rows", (2, 16), SM_END)
        one = cst[:, 0:1]
        blk2 = cst[:, 1:3]
        invf = cst[:, 3:4]

        S0 = 64 * KB
        dq = [at("dq_even", (2, T), S0), at("dq_odd", (2, T), 144 * KB)]
        dqs = [at(f"dqs{m}", T, (152 + 4 * m) * KB, F32R) for m in range(2)]
        dkk = [at(f"dkk{m}", T, S0 + (53 + 4 * m) * KB, F32R) for m in range(2)]
        dkl = [at("dkl_even", T, S0 + 4 * KB, F32R), at("dkl_odd", T, 148 * KB, F32R)]
        dv = at("dv", T, S0 + 8 * KB)
        dvt = at("dvt", (KT, P), S0 + 12 * KB)
        de = at("de", (2, 2, T), S0 + 16 * KB)
        dwt = at("dwt", (2, HALF), S0 + 32 * KB)
        dtmp = at("dtmp", T, S0 + 36 * KB)
        cosm = at("cosm", T, S0 + 40 * KB)
        sinm = at("sinm", T, S0 + 44 * KB)
        swapm = at("swapm", P, S0 + 48 * KB)
        ang = at("ang", T, S0 + 49 * KB)
        ang2 = at("ang2", T, S0 + 53 * KB)
        posi = at("posi", T, S0 + 57 * KB, mybir.dt.int32)
        hq = [at("hq_even", T, S0), at("hq_odd", T, TMP)]
        hz = [[at("hzf_even", T, S0 + 4 * KB), at("hzb_even", T, S0 + 8 * KB)],
              [at("hzf_odd", T, TMP + 4 * KB), at("hzb_odd", T, TMP + 8256 + 4096)]]
        hv = at("hv", T, S0 + 12 * KB)
        hg = at("hg", T, S0 + 16 * KB)
        hvt = at("hvt", (KT, P), S0 + 20 * KB)
        hk = at("hk", (2, T), S0 + 24 * KB)
        hd = at("hd", (2, T), S0 + 32 * KB)
        hqt = at("hqt", (2, HALF), S0 + 40 * KB)
        hkt = at("hkt", (2, T), S0 + 44 * KB)
        hatt = at("hatt", T, S0 + 52 * KB)
        hkd = at("hkd", (KT, P), S0 + 56 * KB)
        hkd_flat = hkd[:, :, :].rearrange("p c e -> p (c e)")
        heb = at("heb", (2, KT), S0 + 60 * KB)
        hmask = at("hmask", (2 * LEVELS, 64), S0 + 60 * KB + 256, I32)
        reset = at("reset", T, TMP + 8256)
        sk = [at("sk_even", (2, T), S0), at("sk_odd", (2, T), 128 * KB)]
        sv = at("sv", T, S0 + 8 * KB)
        svt = at("svt", (KT, P), S0 + 12 * KB)
        sz = at("sz", (4, HALF), S0 + 16 * KB)
        sl = at("sl", (4, HALF), S0 + 24 * KB)
        sp = at("sp", (4, HALF), S0 + 32 * KB)
        sph = at("sph", (4, HALF), S0 + 40 * KB, F32R)
        spl = at("spl", (4, HALF), S0 + 48 * KB, F32R)
        sw = at("sw", (4, HALF), S0 + 56 * KB)
        tri = at("tri", (2, P), TMP, F32R)
        tri_raw = at("tri_raw", (3, P), TMP + KB)
        ctri = tri_raw[:, 2, :]
        cc = at("cc", (3, T), S0)
        cp = at("cp", T + 8, S0 + 12 * KB)
        gv = at("gv", (2, T), S0 + 20 * KB)
        gu = at("gu", (2, T), S0 + 40 * KB)
        gvt = at("gvt", (2, KT, P), S0 + 48 * KB)
        gw = at("gw", (4, P), S0 + 32 * KB)
        gb = at("gb", (2, P), S0 + 34 * KB)
        gmask = at("gmask", P, S0 + 35 * KB)
        p_raw = at("p_raw", (PT, T), S0 + 56 * KB)
        emb = [at(f"emb{k}", T, S0 + (4 * k if k < 6 else 8 + 4 * k) * KB) for k in range(KT)]
        fsq = at("fsq", (2, T), S0 + 40 * KB)
        fss = at("fss", (2, T), S0 + 48 * KB)

        ps = ctx.enter_context(nc.psum_tensor("ps", [P, 8, HALF], F32))

        def banks(a, n=2):
            return ps[:, a:a + n, :].rearrange("p a b -> p (a b)")

        x_back = nc.dram_tensor("x_back", (P, KT, T), F32, kind="Internal").ap()

        param_in = sem("param_in")
        w_in = [sem(f"w_in{s}") for s in range(2)]
        w_hi_done = sem("w_hi_done")
        w_split = sem("w_split")
        acc_full = sem("acc_full")
        acc_free = sem("acc_free")
        x_in = [sem(f"x_in{k}") for k in range(KT)]
        x_out = sem("x_out")
        out_done = sem("out_done")
        h_hi = sem("h_hi")
        h_lo = sem("h_lo")
        sq_ready = sem("sq_ready")
        ss_ready = sem("ss_ready")
        st_sum = sem("st_sum")
        st_var = sem("st_var")
        st_root = sem("st_root")
        st_inv = sem("st_inv")
        st_bc = sem("st_bc")
        rstd_ready = sem("rstd_ready")
        dve_step = sem("dve_step")
        act_step = sem("act_step")
        x_done = sem("x_done")
        xf_ready = sem("xf_ready")
        fx_ready = sem("fx_ready")
        pos_in = sem("pos_in")
        ang_ready = sem("ang_ready")
        cs_ready = sem("cs_ready")
        der_ready = sem("der_ready")
        lam_mm = sem("lam_mm")
        lam_exp = sem("lam_exp")
        swapped = sem("swapped")
        qk_ready = sem("qk_ready")
        v_tr = sem("v_tr")
        v_ready = sem("v_ready")
        scored = sem("scored")
        max_ready = sem("max_ready")
        exp_done = sem("exp_done")
        w_ready = sem("w_ready")
        w_tr = sem("w_tr")
        wt_ready = sem("wt_ready")
        o_mm = sem("o_mm")
        o_out = sem("o_out")
        o_sq = sem("o_sq")
        mix_ready = sem("mix_ready")
        hmask_in = sem("hmask_in")
        sig_done = sem("sig_done")
        f_ready = sem("f_ready")
        logf_done = sem("logf_done")
        d_ready = sem("d_ready")
        e_done = sem("e_done")
        qk_lvl = sem("qk_lvl")
        lvl_mm = sem("lvl_mm")
        att_put = sem("att_put")
        kd_ready = sem("kd_ready")
        kd_tr = sem("kd_tr")
        kdt_ready = sem("kdt_ready")
        kv_mm = sem("kv_mm")
        state_ready = sem("state_ready")
        silu_done = sem("silu_done")
        tri_in = sem("tri_in")
        tri_ready = sem("tri_ready")
        sq_qk = sem("sq_qk")
        z_mm = sem("z_mm")
        z_out = sem("z_out")
        l_ready = sem("l_ready")
        sp_ready = sem("sp_ready")
        sph_ready = sem("sph_ready")
        spl_ready = sem("spl_ready")
        suf_mm = sem("suf_mm")
        t_ready = sem("t_ready")
        sw_exp = sem("sw_exp")
        sw_ready = sem("sw_ready")
        so_mm = sem("so_mm")
        so_out = sem("so_out")
        gate_in = sem("gate_in")
        gelu_done = sem("gelu_done")
        gw_ready = sem("gw_ready")
        gn_ready = sem("gn_ready")
        g_tr = sem("g_tr")
        gt_ready = sem("gt_ready")
        gs_mm = sem("gs_mm")
        conv_done = sem("conv_done")
        act_done = sem("act_done")
        f_hi = sem("f_hi")
        f_lo = sem("f_lo")
        p_in = sem("p_in")
        p_hi = sem("p_hi")
        p_lo = sem("p_lo")
        pg_sig = sem("pg_sig")
        lam_ready = sem("lam_ready")
        g_ready = sem("g_ready")
        qd_ready = sem("qd_ready")
        ho_mm = sem("ho_mm")
        ho_out = sem("ho_out")
        sv_tr = sem("sv_tr")
        sv_ready = sem("sv_ready")
        qk2_ready = sem("qk2_ready")
        g_sq = sem("g_sq")
        g_done = sem("g_done")
        qk_high = sem("qk_high")
        qk_low = sem("qk_low")
        z_abs = sem("z_abs")
        z_exp = sem("z_exp")
        e_mm = sem("e_mm")
        e_out = sem("e_out")

        block = ctx.enter_context(nc.Block())

        @block.sync
        def _(sp_):
            sp_.dma_start(vec[:, :], io["vec"]).then_inc(param_in, 16)
            sp_.dma_start(ident[:, :], io["ident"]).then_inc(param_in, 16)
            sp_.dma_start(cst[:, :], io["cst"]).then_inc(param_in, 16)
            for k in range(KT):
                sp_.dma_start(x[:, k, :], io["x"][:, k, :]).then_inc(x_in[k], 16)
                if k < 2:
                    sp_.dma_start(w_raw[:, k, :], io["w_mix"][k]).then_inc(w_in[k], 16)
            sp_.dma_start(posi[:, :], io["pos"]).then_inc(pos_in, 16)
            sp_.dma_start(swapm[:, :], io["swap"]).then_inc(pos_in, 16)

            def weights(name, u0, n, cols=(T, T)):
                src = io[name]

                def load(i, s, u):
                    sp_.wait_ge(w_split, u - 1)
                    sp_.dma_start(w_raw[:, s, 0:cols[s]],
                                  src[bass.ds(2 * i + s, 1), :, 0:cols[s]].rearrange("u p n -> (u p) n")
                                  ).then_inc(w_in[s], 16)

                if u0 == 0:
                    with sp_.Fori(1, n // 2, 1) as i:
                        for s in range(2):
                            load(i, s, u0 + 2 * i + s)
                else:
                    with sp_.Fori(0, n // 2, 1) as i:
                        for s in range(2):
                            load(i, s, u0 + 2 * i + s)

            weights("w_mix", U_DA, U_OUT)
            weights("w_out", U_OUT, KT)
            for gi, n in enumerate(GROUPS1):
                weights(f"w_gu{gi}", U_GU[gi], 2 * n)
                weights(f"w_dn{gi}", U_DN[gi], KT, (n * P, n * P))
            weights("w_ple", U_PLE, NE + KT)
            weights("w_mix2", U_SB, U_OUT2 - U_SB)
            weights("w_out2", U_OUT2, KT)
            for gi, n in enumerate(GROUPS2):
                weights(f"w_f1{gi}", U_F1[gi], n)
                weights(f"w_f2{gi}", U_F2[gi], KT, (n * P, n * P))
            weights("w_ple2", U_PLE2, NE + KT)
            sp_.wait_ge(out_done, 16 * KT)

        @block.gpsimd
        def _(pool):
            pool.memset(der[:, DER["zero"]:DER["zero"] + 1], 0.0).then_inc(der_ready, 1)
            pool.wait_ge(der_ready, 1)
            zero = der[:, DER["zero"]:DER["zero"] + 1]

            def split(u0, n, cols=(T, T)):
                def one_unit(u, s, turn, first):
                    pool.wait_ge(w_in[s], 16 * (turn + 1))
                    if not first:
                        pool.wait_ge(acc_full, half_no(u - 2, 1))
                    nc.gpsimd.tensor_tensor(w_hi[:, s, 0:cols[s]], w_raw[:, s, 0:cols[s]],
                                            zero.to_broadcast([P, cols[s]]), ALU.add).then_inc(w_hi_done, 1)
                    pool.wait_ge(w_hi_done, u + 1)
                    nc.gpsimd.tensor_tensor(w_lo[:, s, 0:cols[s]], w_raw[:, s, 0:cols[s]],
                                            w_hi[:, s, 0:cols[s]].bitcast(F32), ALU.subtract).then_inc(w_split, 1)

                if u0 == 0:
                    for s in range(2):
                        one_unit(s, s, 0, True)
                    with pool.Fori(1, n // 2, 1) as i:
                        for s in range(2):
                            one_unit(2 * i + s, s, i, False)
                else:
                    with pool.Fori(0, n // 2, 1) as i:
                        for s in range(2):
                            one_unit(u0 + 2 * i + s, s, u0 // 2 + i, False)

            split(U_DA, U_GU[0])
            for gi, n in enumerate(GROUPS1):
                split(U_GU[gi], 2 * n)
                split(U_DN[gi], KT, (n * P, n * P))
            split(U_PLE, U_F1[0] - U_PLE)
            for gi, n in enumerate(GROUPS2):
                split(U_F1[gi], n)
                split(U_F2[gi], KT, (n * P, n * P))
            split(U_PLE2, NE + KT)


        @block.tensor
        def _(pe):
            mm = nc.tensor.matmul

            def k_step(u, hf, k, s, hi, lo, nk):
                if k == 0 and hf == 0:
                    pe.wait_ge(w_split, u + 1)
                if k == 0 and not (isinstance(u, int) and half_no(u, hf) <= 2):
                    pe.wait_ge(acc_free, half_no(u, hf) - 2)
                cols = slice(hf * HALF, hf * HALF + HALF)
                wh, wl = w_hi[:, s, k * P:(k + 1) * P], w_lo[:, s, k * P:(k + 1) * P]
                mm(ps[:, hf, :], wh, hi[:, k, cols], start=(k == 0), stop=False)
                mm(ps[:, hf, :], wh, lo[:, k, cols], start=False, stop=False)
                last = mm(ps[:, hf, :], wl, hi[:, k, cols], start=False, stop=(k == nk - 1))
                if k == nk - 1:
                    last.then_inc(acc_full, 1)

            def gemm_half(u, hf, s, hi, lo, nk, wait_k=None):
                for k in range(nk):
                    if wait_k:
                        wait_k(k)
                    k_step(u, hf, k, s, hi, lo, nk)

            def fill(slot):
                for u, hf, k in slot:
                    k_step(u, hf, k, u % 2, a_hi, a_lo, KT)

            def gemm(u, s, hi, lo, nk, wait_k=None):
                gemm_half(u, 0, s, hi, lo, nk, wait_k)
                gemm_half(u, 1, s, hi, lo, nk)

            def gemm_loop(u0, n, hi, lo, nk, wait_k=None, first=0):
                with pe.Fori(first, n // 2, 1) as i:
                    for s in range(2):
                        gemm(u0 + 2 * i + s, s, hi, lo, nk, wait_k if s == 0 else None)

            def st_sums(src, rhs, ncol, first=0, more=False):
                for c in range(KT):
                    last = mm(ps[:, 7, first + c * ncol:first + (c + 1) * ncol], src[:, c * P:(c + 1) * P],
                              rhs, start=True, stop=True)
                if not more:
                    last.then_inc(st_sum, 1)

            def st_bcast(n, ncol, bank, first=0, more=False):
                pe.wait_ge(st_inv, n + 1)
                rows_ = P // ncol
                for c in range(KT):
                    for j in range(ncol):
                        at_ = first + ncol * c + j
                        lhs = sm[:, 3, at_:at_ + 1].to_broadcast([P, rows_])
                        last = mm(ps[rows_ * j:rows_ * (j + 1), bank + c // 4, (c % 4) * P:(c % 4 + 1) * P],
                                  lhs, ident[:, :], start=True, stop=True)
                if not more:
                    last.then_inc(st_bc, 1)

            def transposes(src, bank, done):
                for c in range(KT):
                    last = nc.tensor.transpose(ps[:, bank + c // 4, (c % 4) * P:(c % 4 + 1) * P],
                                               src[:, c * P:(c + 1) * P], ident[:, :])
                last.then_inc(done, 1)

            def normed_unit(n, q0, u0, ss_count):
                gemm_half(u0, 0, 0, a_hi, a_lo, KT, lambda k: pe.wait_ge(h_lo, q0 + k + 1))
                pe.wait_ge(ss_ready, ss_count)
                st_sums(ss, one, 1)
                gemm_half(u0, 1, 0, a_hi, a_lo, KT)
                st_bcast(n, 1, 5)

            pe.wait_ge(param_in, 48)
            pe.wait_ge(lam_ready, 1)
            mm(ps[:, 7, 0:2], one[0:64, :].to_broadcast([64, P]), der[0:64, DER["lamp"]:DER["lamp"] + 2],
               start=True, stop=True).then_inc(lam_mm, 1)
            pe.wait_ge(lam_exp, 1)
            normed_unit(N_MIX, 0, U_DA, KT)

            def scores(h, qt):
                g = KT * h + qt
                for m in range(2):
                    if g > 0:
                        pe.wait_ge(exp_done, 2 * (g - 1) + m + 1)
                    r, t = slice(64 * m, 64 * m + 64), slice(qt * P, (qt + 1) * P)
                    for hf in range(2):
                        c = slice(hf * HALF, (hf + 1) * HALF)
                        out = ps[:, 2 + 2 * m + hf, :]
                        mm(out, dqs[m][:, t], dkk[m][:, c], start=True, stop=False)
                        last = mm(out, dqs[m][r, t], dkl[h % 2][r, c], start=False, stop=True)
                    last.then_inc(scored, 1)

            def weigh(h, qt, slot0, slot1):
                g = KT * h + qt
                pe.wait_ge(w_ready, g + 1)
                for r in range(2):
                    if g or r:
                        pe.wait_ge(wt_ready, 2 * g + r)
                    for c in range(4):
                        last = nc.tensor.transpose(ps[:, 6, c * P:(c + 1) * P],
                                                   de[:, g % 2, 0, (4 * r + c) * P:(4 * r + c + 1) * P],
                                                   ident[:, :])
                    last.then_inc(w_tr, 1)
                    fill(slot1 if r else slot0)
                if qt == 4:
                    pe.wait_ge(o_out, 2 * h + 1)
                for c in range(KT):
                    if c % 4 == 0:
                        pe.wait_ge(wt_ready, 2 * g + c // 4 + 1)
                    last = mm(ps[:, 7, (qt % 4) * P:(qt % 4 + 1) * P], dvt[:, c, :],
                              dwt[:, c // 4, (c % 4) * P:(c % 4 + 1) * P], start=(c == 0),
                              stop=(c == KT - 1))
                last.then_inc(o_mm, 1)

            gemm(U_DA + 1, 1, a_hi, a_lo, KT)
            for h in range(HEADS):
                u = U_DA + 3 * h
                if h == 0:
                    pe.wait_ge(pos_in, 32)
                    pe.wait_ge(rstd_ready, 1)
                if h == 0:
                    gemm(u + 2, (u + 2) % 2, a_hi, a_lo, KT)
                for t in range(2):
                    pe.wait_ge(acc_free, half_no(u + t, 1))
                    if h:
                        pe.wait_ge(exp_done, 2 * KT * h)
                    for hf in range(2):
                        last = mm(ps[:, 2 + 2 * t + hf, :], swapm[:, :],
                                  dq[h % 2][:, t, hf * HALF:(hf + 1) * HALF], start=True, stop=True)
                    last.then_inc(swapped, 1)
                if h:
                    pe.wait_ge(o_sq, h)
                    st_sums(ang, one, 1)
                    gemm_half(u + 2, 0, (u + 2) % 2, a_hi, a_lo, KT)
                    st_bcast(N_DA + h - 1, 1, 6)
                    gemm_half(u + 2, 1, (u + 2) % 2, a_hi, a_lo, KT)
                pe.wait_ge(qk_ready, 2 * h + 1)
                pe.wait_ge(acc_free, half_no(u + 2, 1))
                transposes(dv, 2, v_tr)
                pe.wait_ge(v_ready, h + 1)
                pe.wait_ge(qk_low, 2 * h + 2)
                slots = filling(*da_fill(h), 2 * KT)
                for qt in range(KT + 1):
                    if qt < KT:
                        scores(h, qt)
                    if qt == 1 and h:
                        pe.wait_ge(mix_ready, h)
                    if qt:
                        weigh(h, qt - 1, slots[2 * qt - 2], slots[2 * qt - 1])

            for h in range(HEADS):
                u = U_HG + 5 * h
                slots = filling(*hg_fill(h), 2 * LEVELS + 4)
                gemm_half(u + 3, 0, (u + 3) % 2, a_hi, a_lo, KT)
                pe.wait_ge(o_sq, HEADS + h)
                st_sums(hkd_flat if h else ang, one, 1)
                gemm_half(u + 3, 1, (u + 3) % 2, a_hi, a_lo, KT)
                gemm_half(u + 4, 0, (u + 4) % 2, a_hi, a_lo, KT)
                pe.wait_ge(acc_free, half_no(u + 3, 1))
                transposes(hv, 2, v_tr)
                st_bcast(N_HG + h - 1, 1, 6)
                pe.wait_ge(qk_lvl, 15 * h + 1)
                for c in range(KT):
                    last = mm(ps[:, 4 + c // 4, (c % 4) * P:(c % 4 + 1) * P], hd[:, 0, c * P:(c + 1) * P],
                              hq[h % 2][:, c * P:(c + 1) * P], start=True, stop=True)
                last.then_inc(lvl_mm, 1)
                gemm_half(u + 4, 1, (u + 4) % 2, a_hi, a_lo, KT)
                for l in range(2 * LEVELS):
                    n = 15 * h + 1 + l
                    pe.wait_ge(qk_lvl, n + 1)
                    pe.wait_ge(att_put, n if l < 2 else n - 1)
                    for c in range(KT):
                        last = mm(ps[:, 4 + l % 2, c * 64:(c + 1) * 64], hkt[:, l % 2, c * P:(c + 1) * P],
                                  hqt[:, l % 2, c * 64:(c + 1) * 64], start=True, stop=True)
                    last.then_inc(lvl_mm, 1)
                    fill(slots[l])
                for d in range(2):
                    n = 2 * h + d
                    pe.wait_ge(kd_ready, n + 1)
                    pe.wait_ge(v_ready, HEADS + h + 1)
                    if n:
                        pe.wait_ge(kdt_ready, n)
                    transposes(hkt[:, d, :], 2, kd_tr)
                    fill(slots[2 * LEVELS + 2 * d])
                    pe.wait_ge(kdt_ready, n + 1)
                    pe.wait_ge(att_put, 15 * h + 15)
                    if d:
                        pe.wait_ge(state_ready, 2 * h + 1)
                    for c in range(KT):
                        last = mm(ps[:, 4 + c // 4, (c % 4) * P:(c % 4 + 1) * P], hkd[:, c, :],
                                  hvt[:, c, :], start=True, stop=True)
                    last.then_inc(kv_mm, 1)
                    fill(slots[2 * LEVELS + 2 * d + 1])
                pe.wait_ge(state_ready, 2 * h + 2)
                pe.wait_ge(qd_ready, 2 * h + 2)
                pe.wait_ge(mix_ready, HEADS + h)
                for c in range(KT):
                    t = slice(c * P, (c + 1) * P)
                    parts = [(hvt[:, c, :], hatt[:, t])]
                    if c > 0:
                        parts.append((hk[:, 0, t], hz[h % 2][0][:, t]))
                    if c < KT - 1:
                        parts.append((hk[:, 1, t], hz[h % 2][1][:, t]))
                    for n, (lhs, rhs) in enumerate(parts):
                        last = mm(ps[:, 6 + c // 4, (c % 4) * P:(c % 4 + 1) * P], lhs, rhs,
                                  start=(n == 0), stop=(n == len(parts) - 1))
                last.then_inc(ho_mm, 1)
            pe.wait_ge(o_sq, 2 * HEADS)
            st_sums(hkd_flat, one, 1)
            st_bcast(N_HG + HEADS - 1, 1, 4)

            def mixed_out(u0, f0):
                gemm_half(u0, 0, 0, b_hi, b_lo, KT, lambda k: pe.wait_ge(f_lo, f0 + k + 1))
                gemm_half(u0, 1, 0, b_hi, b_lo, KT)
                gemm(u0 + 1, 1, b_hi, b_lo, KT)
                gemm_loop(u0, KT, b_hi, b_lo, KT, first=1)

            mixed_out(U_OUT, F_MIX)
            f = F_FF
            for gi, n in enumerate(GROUPS1):
                if gi == 0:
                    normed_unit(N_FFN, Q_FFN, U_GU[0], Q_FFN + KT)
                    gemm(U_GU[0] + 1, 1, a_hi, a_lo, KT)
                    gemm_loop(U_GU[0], 2 * n, a_hi, a_lo, KT, first=1)
                else:
                    gemm_loop(U_GU[gi], 2 * n, a_hi, a_lo, KT)
                f += n
                gemm_loop(U_DN[gi], KT, b_hi, b_lo, n,
                          lambda k: k == n - 1 and pe.wait_ge(f_lo, f))

            def embedding(n, q0, u0, turn):
                per = KT // NE
                for v in range(NE):
                    u = u0 + v
                    pe.wait_ge(w_split, u + 1)
                    for t in range(per):
                        for hf in range(2):
                            e = 2 * (per * v + t) + hf
                            if e >= 3:
                                pe.wait_ge(e_out, 2 * KT * turn + e - 2)
                            elif turn:
                                pe.wait_ge(e_out, 2 * KT)
                            c = slice(hf * HALF, (hf + 1) * HALF)
                            for k in range(PT):
                                if e == 0:
                                    pe.wait_ge(p_lo, 2 * turn + k + 1)
                                w = slice((PT * t + k) * P, (PT * t + k + 1) * P)
                                out = ps[:, 2 + e % 3, :]
                                mm(out, w_hi[:, u % 2, w], b_hi[:, 6 + k, c], start=(k == 0), stop=False)
                                mm(out, w_hi[:, u % 2, w], b_lo[:, 6 + k, c], start=False, stop=False)
                                last = mm(out, w_lo[:, u % 2, w], b_hi[:, 6 + k, c], start=False,
                                          stop=(k == PT - 1))
                            if t < per - 1 or hf == 0:
                                last.then_inc(e_mm, 1)
                    last.then_inc(acc_full, 2)
                    if v == 0:
                        pe.wait_ge(ss_ready, q0 + KT)
                        st_sums(ss, one, 1)
                st_bcast(n, 1, 5)
                pe.wait_ge(h_lo, q0 + KT)
                gemm_loop(u0 + NE, KT, a_hi, a_lo, KT)

            embedding(N_PLE, Q_PLE, U_PLE, 0)

            gemm_half(U_SB, 0, 0, a_hi, a_lo, KT, lambda k: pe.wait_ge(h_lo, Q_1 + k + 1))
            pe.wait_ge(ss_ready, Q_1 + KT)
            st_sums(fss[:, 0, :], one, 1)
            st_sums(fss[:, 1, :], one, 1, 16)
            gemm_half(U_SB, 1, 0, a_hi, a_lo, KT)
            st_bcast(N_1, 1, 5)
            for c in range(KT):
                last = mm(ps[:, 2 + c // 4, (c % 4) * P:(c % 4 + 1) * P], sm[:, 0, c:c + 1].to_broadcast([P, P]),
                          ident[:, :], start=True, stop=True)
            last.then_inc(st_bc, 1)

            def piece(p, n):
                return NPC * p + n

            def logits(p, n):
                th, i, hh = PIECES[n]
                c0 = max(0, i - 4 * th) * P
                s = piece(p, n)
                if s >= 2:
                    pe.wait_ge(z_out, s - 1)
                r = slice(64 * hh, 64 * hh + 64)
                mm(ps[:, 2 + s % 2, c0:], sk[p % 2][r, 1, i * P:(i + 1) * P],
                   sk[p % 2][r, 0, th * HALF + c0:(th + 1) * HALF], start=True, stop=True).then_inc(z_mm, 1)

            def suffix(p, n, which):
                th, i, hh = PIECES[n]
                c0 = max(0, i - 4 * th) * P
                s = piece(p, n)
                first = which == 0 and i == 4 * th + 3
                if which == 0:
                    pe.wait_ge(spl_ready, s + 1)
                else:
                    pe.wait_ge(t_ready, s + 1)
                if first and th:
                    pe.wait_ge(t_ready, s - 1)
                for m, part in enumerate((sph, spl)):
                    last = mm(ps[:, 4 + hh, c0:], tri[:, which, :], part[:, s % 4, c0:],
                              start=(first and m == 0), stop=(m == 1), skip_group_check=True)
                if which == 0:
                    last.then_inc(suf_mm, 1)

            def values(p, n):
                th, i, hh = PIECES[n]
                c0 = max(0, i - 4 * th) * P
                s = piece(p, n)
                if i >= 4 * th:
                    pe.wait_ge(sw_ready, diagonal_no(p, n))
                else:
                    pe.wait_ge(sw_exp, s + 1)
                if i == 4 * th + 3 and (p or th):
                    pe.wait_ge(so_out, 4 * p + 2 * th + hh - 1)
                last = mm(ps[:, 6 + hh, c0:], svt[:, i, :], sw[:, s % 4, c0:], start=(i == 4 * th + 3),
                          stop=(i == 0), skip_group_check=True)
                last.then_inc(so_mm, 1)

            pe.wait_ge(tri_ready, 2)
            gemm(U_SB + 1, 1, a_hi, a_lo, KT)
            for p in range(HEADS):
                u = U_SB + 3 * p
                gemm_half(u + 2, 0, (u + 2) % 2, a_hi, a_lo, KT)
                if p == 0:
                    pe.wait_ge(xf_ready, KT)
                else:
                    pe.wait_ge(so_out, 4 * p)
                    pe.wait_ge(z_out, NPC * p)
                    pe.wait_ge(t_ready, NPC * p)
                pe.wait_ge(sq_qk, 2 * p + 2)
                st_sums(c_buf, blk2, 2, 0, True)
                st_sums(ss, blk2, 2, 16)
                gemm_half(u + 2, 1, (u + 2) % 2, a_hi, a_lo, KT)
                st_bcast(N_QK + p, 2, 4, 0, True)
                st_bcast(N_QK + p, 2, 2, 16)
                pe.wait_ge(acc_free, half_no(u + 2, 1))
                transposes(sv, 6, sv_tr)
                pe.wait_ge(qk2_ready, 2 * p + 2)
                slots = filling(*sb_fill(p), NPC + 3)
                logits(p, 0)
                pe.wait_ge(sv_ready, p + 1)
                for n in range(NPC + 4):
                    if n + 1 < NPC:
                        logits(p, n + 1)
                    if 3 <= n <= NPC + 2 and PIECES[n - 3][1] > 0:
                        suffix(p, n - 3, 1)
                    if 2 <= n <= NPC + 1:
                        suffix(p, n - 2, 0)
                    if n < NPC + 3:
                        fill(slots[n])
                    if n >= 4:
                        values(p, n - 4)

            def proj(u, hf):
                gemm_half(u, hf, u % 2, a_hi, a_lo, KT)

            def gate_transposes(j, bank):
                pe.wait_ge(gn_ready, j + 1)
                transposes(gv[:, j, :], bank, g_tr)

            def gate_mix(j):
                pe.wait_ge(gt_ready, 2)
                if j:
                    pe.wait_ge(g_done, 2)
                for hh in range(2):
                    for c in range(KT):
                        last = mm(ps[:, 4 + 2 * hh + c // 4, (c % 4) * P:(c % 4 + 1) * P], gvt[:, j, c, :],
                                  gw[:, 2 * j + hh, :], start=True, stop=True)
                last.then_inc(gs_mm, 1)

            for j in range(2):
                gemm(U_SV + j, (U_SV + j) % 2, a_hi, a_lo, KT)
            proj(U_CV1, 0)
            pe.wait_ge(so_out, 4 * HEADS)
            pe.wait_ge(g_sq, 2)
            st_sums(c_buf, blk2, 2, 0, True)
            st_sums(ss, blk2, 2, 16)
            proj(U_CV1, 1)
            proj(U_CV1 + 1, 0)
            st_bcast(N_SG, 2, 4, 0, True)
            st_bcast(N_SG, 2, 2, 16)
            proj(U_CV1 + 1, 1)
            gate_transposes(0, 6)
            proj(U_CV1 + 2, 0)
            gate_transposes(1, 2)
            proj(U_CV1 + 2, 1)
            pe.wait_ge(gw_ready, 1)
            gate_mix(0)
            gemm(U_SU, U_SU % 2, a_hi, a_lo, KT)
            gate_mix(1)
            gemm(U_SU + 1, (U_SU + 1) % 2, a_hi, a_lo, KT)

            mixed_out(U_OUT2, F_MIX2)
            f = F_FF2
            for gi, n in enumerate(GROUPS2):
                if gi == 0:
                    normed_unit(N_2, Q_2, U_F1[0], Q_2 + KT)
                    gemm(U_F1[0] + 1, 1, a_hi, a_lo, KT)
                    gemm_loop(U_F1[0], n, a_hi, a_lo, KT, first=1)
                else:
                    gemm_loop(U_F1[gi], n, a_hi, a_lo, KT)
                f += n
                gemm_loop(U_F2[gi], KT, b_hi, b_lo, n,
                          lambda k: k == n - 1 and pe.wait_ge(f_lo, f))
            embedding(N_3, Q_3, U_PLE2, 1)

        @block.vector
        def _(dve):
            tt = nc.vector.tensor_tensor
            ts = nc.vector.tensor_scalar
            stt = nc.vector.scalar_tensor_tensor
            steps = [0]

            def step(ins):
                ins.then_inc(dve_step, 1)
                steps[0] += 1
                dve.wait_ge(dve_step, steps[0])

            def col(name, j=0, n=1):
                return vec[:, bass.ds(VEC[name] + j, n)]

            def dcol(name, j=0, n=1):
                return der[:, bass.ds(DER[name] + j, n)]

            def leave(u, dst, first=0):
                for hf in range(2):
                    dve.wait_ge(acc_full, half_no(u, hf))
                    tt(dst[:, first + hf * HALF:first + (hf + 1) * HALF], ps[:, hf, :],
                       rstd[:, hf * HALF:(hf + 1) * HALF], ALU.mult).then_inc(acc_free, 1)

            def leave_half(u, hf, dst):
                dve.wait_ge(acc_full, half_no(u, hf))
                tt(dst[:, hf * HALF:(hf + 1) * HALF], ps[:, hf, :], rstd[:, hf * HALF:(hf + 1) * HALF],
                   ALU.mult).then_inc(acc_free, 1)

            def evict(slot, u0, dsts):
                for u, hf in finished(slot):
                    leave_half(u, hf, dsts[u - u0])

            def prep(q, k, gain, xk):
                dve.wait_ge(h_hi, q + k + 1)
                stt(a_lo[:, k, :], xk, gain, a_hi[:, k, :].bitcast(F32), ALU.mult,
                    ALU.subtract).then_inc(h_lo, 1)
                dve.wait_ge(sq_ready, q + k + 1)
                if q + k:
                    dve.wait_ge(ss_ready, q + k)
                tt(ss[:, :], ss[:, :], sq[:, k % 2, 0:T], ALU.add).then_inc(ss_ready, 1)

            def st_inverse(n, ncols, scale):
                dve.wait_ge(st_sum, n + 1)
                ts(sm[:, 1, 0:ncols], ps[:, 7, 0:ncols], scale, EPS, ALU.mult, ALU.add).then_inc(st_var, 1)
                dve.wait_ge(st_root, n + 1)
                nc.vector.reciprocal(sm[:, 3, 0:ncols], sm[:, 2, 0:ncols]).then_inc(st_inv, 1)

            dve.wait_ge(param_in, 48)
            step(tt(dcol("fin_n1", 0, 8), col("final", 0, 8), col("norm1", 0, 8), ALU.mult))
            step(ts(dcol("subln"), col("subln"), 1.0 - LAMBDA_INIT, None, ALU.mult))
            step(ts(dcol("qn"), col("qn"), 0.125, None, ALU.mult))
            step(tt(dcol("lamp"), col("lam", 0), col("lam", 1), ALU.mult))
            tt(dcol("lamp", 1), col("lam", 2), col("lam", 3), ALU.mult).then_inc(lam_ready, 1)
            step(tt(dcol("lb", 0, 8), col("gamma0", 0, 8), col("gamma1", 0, 8), ALU.max))
            step(tt(dcol("g0", 0, 8), col("gamma0", 0, 8), dcol("lb", 0, 8), ALU.subtract))
            tt(dcol("g1", 0, 8), col("gamma1", 0, 8), dcol("lb", 0, 8), ALU.subtract).then_inc(g_ready, 1)
            dve.wait_ge(lam_exp, 1)
            step(tt(dcol("g1", 0, 8), dcol("g0", 0, 8), dcol("g1", 0, 8), ALU.add))
            step(nc.vector.reciprocal(dcol("g1", 0, 8), dcol("g1", 0, 8)))
            step(tt(dcol("lb", 0, 8), dcol("g0", 0, 8), dcol("g1", 0, 8), ALU.mult))
            step(ts(dcol("omlb", 0, 8), dcol("lb", 0, 8), -1.0, 1.0, ALU.mult, ALU.add))
            step(stt(dcol("neg_lam"), dcol("lame", 1), LAMBDA_INIT, dcol("lame", 0), ALU.subtract,
                     ALU.subtract))

            step(nc.vector.memset(ss[:, :], 0.0))
            for k in range(KT):
                dve.wait_ge(x_in[k], 16)
                prep(Q_MIX, k, col("norm_mix", k), x[:, k, :])
            st_inverse(N_MIX, 8, 1.0 / T)

            def table(n, dst, off):
                step(ts(ang2[:, :], ang[:, :], float(np.float32(1.0 / TWO_PI)), off, ALU.mult, ALU.add))
                step(ts(ang2[:, :], ang2[:, :], MAGIC, None, ALU.add))
                step(ts(ang2[:, :], ang2[:, :], MAGIC, None, ALU.subtract))
                step(stt(dst[:, :], ang2[:, :], -TURN[0], ang[:, :], ALU.mult, ALU.add))
                for part in TURN[1:]:
                    step(stt(dst[:, :], ang2[:, :], -part, dst[:, :], ALU.mult, ALU.add))
                step(ts(dst[:, :], dst[:, :], float(off * TWO_PI), 3.1415925, ALU.add, ALU.min))
                ts(dst[:, :], dst[:, :], -3.1415925, None, ALU.max).then_inc(ang_ready, 1)

            dve.wait_ge(pos_in, 32)
            step(nc.vector.tensor_copy(ang[:, :], posi[:, :]))
            step(ts(ang[:, :], ang[:, :], invf, None, ALU.mult))
            dve.wait_ge(rstd_ready, 1)
            leave(U_DA, dq[0][:, 0, :])
            table(0, sinm, 0.0)
            leave(U_DA + 1, dq[0][:, 1, :])
            table(1, cosm, 0.25)
            leave(U_DA + 2, dv[:, :])
            dve.wait_ge(cs_ready, 2)

            def row_max(h, qt):
                g = KT * h + qt
                for m in range(2):
                    dve.wait_ge(scored, 2 * g + m + 1)
                    step(nc.vector.reduce_max(rows[:, m, 0:1], banks(2 + 2 * m), AX_X))
                    if g:
                        dve.wait_ge(exp_done, 2 * (g - 1) + m + 1)
                    ts(rows[:, m, 1:2], rows[:, m, 0:1], -0.125, None, ALU.mult).then_inc(max_ready, 1)

            def combine(h, qt):
                g = KT * h + qt
                r = g % 2
                dve.wait_ge(exp_done, 2 * g + 2)
                step(nc.vector.reciprocal(rows[:, r, 4:6], rows[:, r, 2:4]))
                step(tt(rows[:, r, 6:7], rows[:, r, 5:6], dcol("neg_lam"), ALU.mult))
                step(ts(de[:, r, 0, :], de[:, r, 0, :], rows[:, r, 4:5], None, ALU.mult))
                stt(de[:, r, 0, :], de[:, r, 1, :], rows[:, r, 6:7], de[:, r, 0, :], ALU.mult,
                    ALU.add).then_inc(w_ready, 1)

            def rotate(h, t):
                dve.wait_ge(swapped, 2 * h + t + 1)
                qk = dq[h % 2][:, t, :]
                step(tt(dtmp[:, :], banks(2 + 2 * t), sinm[:, :], ALU.mult))
                step(tt(qk, qk, cosm[:, :], ALU.mult))
                tt(qk, qk, dtmp[:, :], ALU.add).then_inc(qk_ready, 1)
                dve.wait_ge(qk_ready, 2 * h + t + 1)

            def low(h, t):
                dve.wait_ge(qk_high, 2 * h + t + 1)
                for m in range(2):
                    r, o = slice(64 * m, 64 * m + 64), slice(64 * (1 - m), 64 * (1 - m) + 64)
                    hi = (dkk if t else dqs)[m][r, :].bitcast(F32)
                    ins = tt(dkl[h % 2][r, :] if t else dqs[m][o, :], dq[h % 2][r, t, :], hi, ALU.subtract)
                ins.then_inc(qk_low, 1)

            def da_norm(h, bank):
                dve.wait_ge(st_bc, N_DA + h + 1)
                stt(mix[:, h, :], mix[:, h, :], dcol("subln"), banks(bank), ALU.mult,
                    ALU.mult).then_inc(mix_ready, 1)

            for h in range(HEADS):
                u = U_DA + 3 * h
                rotate(h, 0)
                if h:
                    st_inverse(N_DA + h - 1, 8, 1.0 / P)
                rotate(h, 1)
                if h:
                    leave_half(u + 2, 0, dv[:, :])
                low(h, 0)
                if h:
                    da_norm(h - 1, 6)
                    leave_half(u + 2, 1, dv[:, :])
                low(h, 1)
                slots = filling(*da_fill(h), 2 * KT)
                if h + 1 < HEADS:
                    next_ = [dq[(h + 1) % 2][:, 0, :], dq[(h + 1) % 2][:, 1, :]]
                else:
                    next_ = [hq[0][:, :], hz[0][0][:, :], hz[0][1][:, :]]
                for qt in range(KT + 1):
                    if qt:
                        combine(h, qt - 1)
                    if qt > 1:
                        evict(slots[2 * qt - 4] + slots[2 * qt - 3], da_fill(h)[0], next_)
                    if qt < KT:
                        row_max(h, qt)
                evict(slots[-2] + slots[-1], da_fill(h)[0], next_)

            step(nc.vector.memset(reset[:, :], 1.0))
            step(nc.vector.memset(reset[:, :].rearrange("p (c t) -> p c t", t=P)[:, :, 0:1], 0.0))

            def chunks(buf, size):
                return buf.rearrange("p (n t) -> p n t", t=size)

            def hg_norm(h, bank):
                dve.wait_ge(st_bc, N_HG + h + 1)
                step(stt(mix[:, HEADS + h, :], mix[:, HEADS + h, :], col("hgn"), banks(bank), ALU.mult,
                         ALU.mult))
                dve.wait_ge(silu_done, h + 1)
                tt(mix[:, HEADS + h, :], mix[:, HEADS + h, :], hg[:, :], ALU.mult).then_inc(mix_ready, 1)

            for h in range(HEADS):
                u = U_HG + 5 * h
                hqh, hzh = hq[h % 2], hz[h % 2]
                o = (h + 1) % 2
                next_ = [hq[o][:, :], hz[o][0][:, :], hz[o][1][:, :]]
                u_next = hg_fill(h)[0]
                slots = filling(*hg_fill(h), 2 * LEVELS + 4)
                for d in range(2):
                    j = HEADS * d + h
                    dve.wait_ge(sig_done, 4 * h + 2 * d + 2)
                    ts(hd[:, d, :], hd[:, d, :], dcol("omlb", j), dcol("lb", j), ALU.mult,
                       ALU.add).then_inc(f_ready, 1)
                    step(ts(hk[:, d, :], hk[:, d, :], dcol("omlb", j), None, ALU.mult))
                for d in range(2):
                    dve.wait_ge(logf_done, 2 * h + d + 1)
                    if d == 0:
                        step(nc.vector.tensor_tensor_scan(hzh[d][:, :], reset[:, :], hd[:, d, :], 0.0,
                                                          ALU.mult, ALU.add))
                    else:
                        step(nc.vector.tensor_tensor_scan(hzh[d][:, ::-1], reset[:, :], hd[:, d, ::-1], 0.0,
                                                          ALU.mult, ALU.add))
                leave(u + 3, hv[:, :])
                tt(hd[:, 0, :], hk[:, 0, :], hk[:, 1, :], ALU.add).then_inc(qk_lvl, 1)
                st_inverse(N_HG + h - 1, 8, 1.0 / P)
                if h == 0:
                    step(nc.vector.memset(hkt[:, 0, :], 0.0))
                    step(nc.vector.memset(hkt[:, 1, :], 0.0))
                    da_norm(HEADS - 1, 6)
                else:
                    hg_norm(h - 1, 6)
                    dve.wait_ge(mix_ready, HEADS + h)
                leave_half(u + 4, 0, hg[:, :])
                dve.wait_ge(lvl_mm, 15 * h + 1)
                tt(chunks(hatt[:, :], P), banks(4).rearrange("p (n t) -> p n t", t=P),
                   ident[:, :].rearrange("p (o t) -> p o t", o=1).to_broadcast([P, KT, P]),
                   ALU.mult).then_inc(att_put, 1)

                def halves(l, d):
                    hs = 1 << (l // 2)
                    lower, upper = slice(0, hs), slice(hs, 2 * hs)
                    return (2 * hs, upper, lower, hs - 1) if d == 0 else (2 * hs, lower, upper, hs)

                def distances(l):
                    d = l % 2
                    size, _, _, ref = halves(l, d)
                    b = chunks(hzh[d][:, :], size)
                    if l >= 2:
                        dve.wait_ge(qk_lvl, 15 * h + l)
                    tt(chunks(hd[:, d, :], size), b, b[:, :, ref:ref + 1].to_broadcast([P, T // size, size]),
                       ALU.subtract).then_inc(d_ready, 1)

                def operands(l):
                    d = l % 2
                    n = 15 * h + 1 + l
                    size, qs, ks, _ = halves(l, d)
                    dve.wait_ge(e_done, 34 * h + 2 * l + 2)
                    if l >= 2:
                        dve.wait_ge(lvl_mm, n - 1)
                    e = chunks(hd[:, d, :], size)
                    tt(chunks(hqt[:, d, :], size // 2), chunks(hqh[:, :], size)[:, :, qs], e[:, :, qs],
                       ALU.mult)
                    tt(chunks(hkt[:, d, :], size)[:, :, ks], chunks(hk[:, d, :], size)[:, :, ks], e[:, :, ks],
                       ALU.mult).then_inc(qk_lvl, 1)

                def put(l):
                    d = l % 2
                    n = 15 * h + 1 + l
                    size, qs, _, _ = halves(l, d)
                    dve.wait_ge(lvl_mm, n + 1)
                    dve.wait_ge(att_put, n)
                    nt = P // size
                    mask = (hmask[:, l, :].rearrange("p (o n t) -> p o n t", o=1, n=nt)
                            .to_broadcast([P, KT, nt, size // 2]))
                    out = hatt[:, :].rearrange("p (c n t) -> p c n t", c=KT, n=nt)[:, :, :, qs]
                    data = ps[:, 4 + d, :].rearrange("p (c n t) -> p c n t", c=KT, n=nt)
                    nc.vector.copy_predicated(out, mask, data).then_inc(att_put, 1)

                dve.wait_ge(hmask_in, 16)
                nl = 2 * LEVELS
                for l in range(nl + 3):
                    if l < nl:
                        distances(l)
                    if l == 0:
                        leave_half(u + 4, 1, hg[:, :])
                    if l >= 3:
                        put(l - 3)
                    if 1 <= l <= nl:
                        operands(l - 1)
                    if l >= 3:
                        evict(slots[l - 3], u_next, next_)

                for d in range(2):
                    b = chunks(hzh[d][:, :], P)
                    ref = P - 1 if d == 0 else 0
                    dve.wait_ge(qk_lvl, 15 * h + 15)
                    tt(chunks(hd[:, d, :], P), b, b[:, :, ref:ref + 1].to_broadcast([P, KT, P]),
                       ALU.subtract).then_inc(d_ready, 1)
                for d in range(2):
                    dve.wait_ge(e_done, 34 * h + 28 + 3 * d + 1)
                    dve.wait_ge(lvl_mm, 15 * h + 15)
                    tt(hkt[:, d, :], hk[:, d, :], hd[:, d, :], ALU.mult).then_inc(kd_ready, 1)
                evict(slots[2 * LEVELS], u_next, next_)
                dve.wait_ge(kd_ready, 2 * h + 2)
                for d in range(2):
                    n = 2 * h + d
                    dve.wait_ge(kv_mm, n + 1)
                    order = range(KT) if d == 0 else range(KT - 1, -1, -1)
                    order = list(order)
                    for a, c in zip(order[:-1], order[1:]):
                        kv = ps[:, 4 + a // 4, (a % 4) * P:(a % 4 + 1) * P]
                        dst = hk[:, d, c * P:(c + 1) * P]
                        if a == order[0]:
                            ins = nc.vector.tensor_copy(dst, kv)
                        else:
                            if a == order[1]:
                                dve.wait_ge(e_done, 34 * h + 28 + 3 * d + 2)
                            ins = stt(dst, hk[:, d, a * P:(a + 1) * P], heb[:, d, a:a + 1], kv, ALU.mult,
                                      ALU.add)
                        if c == order[-1]:
                            ins.then_inc(state_ready, 1)
                        else:
                            step(ins)
                    if d == 0:
                        evict(slots[2 * LEVELS + 1] + slots[2 * LEVELS + 2], u_next, next_)
                for d in range(2):
                    dve.wait_ge(e_done, 34 * h + 28 + 3 * d + 3)
                    tt(hzh[d][:, :], hqh[:, :], hd[:, d, :], ALU.mult).then_inc(qd_ready, 1)

                evict(slots[2 * LEVELS + 3], u_next, next_)
            st_inverse(N_HG + HEADS - 1, 8, 1.0 / P)
            hg_norm(HEADS - 1, 4)


            def split_mix(f0, m0):
                dve.wait_ge(mix_ready, m0 + KT)
                for k in range(KT):
                    dve.wait_ge(f_hi, f0 + k + 1)
                    tt(b_lo[:, k, :], mix[:, k, :], b_hi[:, k, :].bitcast(F32),
                       ALU.subtract).then_inc(f_lo, 1)

            def add_to_x(u, k):
                for hf in range(2):
                    c = slice(hf * HALF, (hf + 1) * HALF)
                    dve.wait_ge(acc_full, half_no(u, hf))
                    tt(x[:, k, c], ps[:, hf, :], x[:, k, c], ALU.add).then_inc(acc_free, 1)

            def out_projection(u0, f0, m0, turn, q, gain):
                split_mix(f0, m0)
                step(nc.vector.memset(ss[:, :], 0.0))
                for k in range(KT):
                    dve.wait_ge(x_in[k], 16 * turn)
                    add_to_x(u0 + k, k)
                    dve.wait_ge(acc_free, half_no(u0 + k, 1))
                    prep(q, k, col(gain, k), x[:, k, :])

            def down(u0, last, q=0, gain=None):
                if not last:
                    with dve.Fori(0, KT, 1) as i:
                        for hf in range(2):
                            dve.wait_ge(acc_full, half_no(u0 + i, hf))
                            xk = x[:, bass.ds(i, 1), hf * HALF:(hf + 1) * HALF].rearrange("p a b -> p (a b)")
                            tt(xk, ps[:, hf, :], xk, ALU.add).then_inc(acc_free, 1)
                    return
                step(nc.vector.memset(ss[:, :], 0.0))
                for k in range(KT):
                    add_to_x(u0 + k, k)
                    dve.wait_ge(acc_free, half_no(u0 + k, 1))
                    prep(q, k, col(gain, k), x[:, k, :])

            out_projection(U_OUT, F_MIX, 0, 2, Q_FFN, "norm_ffn")
            st_inverse(N_FFN, 8, 1.0 / T)
            dve.wait_ge(ss_ready, Q_FFN + KT)
            for s in range(2):
                step(nc.vector.memset(pad_a[:, s, 0:1], 0.0))
                step(nc.vector.memset(pad_a[:, s, T + 1:T + 2], 0.0))
            dve.wait_ge(rstd_ready, 2)

            def hidden_tile(u, s, f, fi):
                if not (isinstance(fi, int) and fi < 2):
                    dve.wait_ge(f_lo, f - 1)
                leave(u, pad_a[:, s, :], 1)
                dve.wait_ge(acc_free, half_no(u, 1))
                ts(c_buf[:, :], pad_a[:, s, 0:T], col("conv_w0", fi), col("conv_b", fi), ALU.mult,
                   ALU.add).then_inc(conv_done, 1)
                dve.wait_ge(conv_done, 3 * fi + 1)
                stt(c_buf[:, :], pad_a[:, s, 1:T + 1], col("conv_w1", fi), c_buf[:, :], ALU.mult,
                    ALU.add).then_inc(conv_done, 1)
                dve.wait_ge(conv_done, 3 * fi + 2)
                stt(c_buf[:, :], pad_a[:, s, 2:T + 2], col("conv_w2", fi), c_buf[:, :], ALU.mult,
                    ALU.add).then_inc(conv_done, 1)
                dve.wait_ge(conv_done, 3 * fi + 3)
                leave(u + 1, pad_a[:, s, :], 1)
                dve.wait_ge(acc_free, half_no(u + 1, 1))
                dve.wait_ge(act_done, fi + 1)
                tt(pad_a[:, s, 1:T + 1], c_buf[:, :], pad_a[:, s, 1:T + 1], ALU.mult).then_inc(fx_ready, 1)

            def remainder(f, s, j, first):
                dve.wait_ge(f_hi, f + 1)
                lo = b_lo[:, bass.ds(j, 1), :].rearrange("p a b -> p (a b)")
                hi = b_hi[:, bass.ds(j, 1), :].rearrange("p a b -> p (a b)").bitcast(F32)
                tt(lo, pad_a[:, s, first:first + T], hi, ALU.subtract).then_inc(f_lo, 1)

            def split_embedding(turn):
                for k in range(PT):
                    dve.wait_ge(p_hi, 2 * turn + k + 1)
                    tt(b_lo[:, 6 + k, :], p_raw[:, k, :], b_hi[:, 6 + k, :].bitcast(F32),
                       ALU.subtract).then_inc(p_lo, 1)

            fi = 0
            for gi, n in enumerate(GROUPS1):
                def pair(i):
                    for s in range(2):
                        t = fi + 2 * i + s
                        hidden_tile(U_GU[gi] + 4 * i + 2 * s, s, F_FF + t, t)
                        remainder(F_FF + t, s, 2 * i + s, 1)
                if gi == 0:
                    pair(0)
                with dve.Fori(1 if gi == 0 else 0, n // 2, 1) as i:
                    pair(i)
                fi += n
                if gi == len(GROUPS1) - 1:
                    split_embedding(0)
                down(U_DN[gi], gi == len(GROUPS1) - 1, Q_PLE, "norm_ple")
            st_inverse(N_PLE, 8, 1.0 / T)

            def final_low(k):
                dve.wait_ge(h_hi, Q_1 + k + 1)
                stt(a_lo[:, k, :], x[:, k, :], dcol("fin_n1", k), a_hi[:, k, :].bitcast(F32), ALU.mult,
                    ALU.subtract).then_inc(h_lo, 1)

            def add_squares(k):
                dve.wait_ge(sq_ready, Q_1 + k + 1)
                tt(fss[:, :, :], fss[:, :, :], fsq[:, :, :], ALU.add).then_inc(ss_ready, 1)
                dve.wait_ge(ss_ready, Q_1 + k + 1)

            def embedding(u0, turn, rs):
                if turn == 0:
                    step(nc.vector.memset(fss[:, :, :], 0.0))
                dve.wait_ge(rstd_ready, rs)
                dve.wait_ge(ss_ready, Q_PLE + KT if turn == 0 else Q_3 + KT)
                dve.wait_ge(e_out, 2 * KT * (turn + 1))
                for k in range(KT):
                    leave(u0 + NE + k, pad_a[:, 0, :])
                    for hf in range(2):
                        c = slice(hf * HALF, (hf + 1) * HALF)
                        dve.wait_ge(pg_sig, 2 * (KT * turn + k) + hf + 1)
                        ins = tt(c_buf[:, c], emb[k][:, c], pad_a[:, 0, c], ALU.mult)
                        if hf == 0:
                            ins.then_inc(dve_step, 1)
                            steps[0] += 1
                        else:
                            step(ins)
                    tt(x[:, k, :], x[:, k, :], c_buf[:, :], ALU.add).then_inc(x_done, 1)
                    dve.wait_ge(x_done, KT * turn + k + 1)
                    if turn == 0:
                        if k == KT - 1:
                            for j in range(3):
                                final_low(j)
                        add_squares(k)

            embedding(U_PLE, 0, 3)

            dve.wait_ge(x_done, KT)
            for k in range(3, KT):
                final_low(k)
            dve.wait_ge(st_sum, N_1 + 1)
            ts(sm[:, 1, 0:8], ps[:, 7, 0:8], 1.0 / T, EPS, ALU.mult, ALU.add).then_inc(st_var, 1)
            dve.wait_ge(st_root, N_FIN + 1)
            nc.vector.reciprocal(sm[:, 0, 0:8], sm[:, 2, 0:8]).then_inc(st_inv, 1)
            dve.wait_ge(st_inv, N_FIN + 1)
            step(stt(sm[:, 1, 0:8], ps[:, 7, 16:24], 1.0 / T, sm[:, 0, 0:8], ALU.mult, ALU.mult))
            step(tt(sm[:, 1, 0:8], sm[:, 1, 0:8], sm[:, 0, 0:8], ALU.mult))
            ts(sm[:, 1, 0:8], sm[:, 1, 0:8], EPS, None, ALU.add).then_inc(st_var, 1)
            dve.wait_ge(st_root, N_1 + 1)
            step(nc.vector.reciprocal(sm[:, 3, 0:8], sm[:, 2, 0:8]))
            tt(sm[:, 3, 0:8], sm[:, 3, 0:8], sm[:, 0, 0:8], ALU.mult).then_inc(st_inv, 1)
            dve.wait_ge(rstd_ready, 4)
            leave(U_SB, sk[0][:, 0, :])
            dve.wait_ge(st_bc, N_1 + 1)
            for k in range(KT):
                stt(x[:, k, :], x[:, k, :], col("final", k), banks(2), ALU.mult,
                    ALU.mult).then_inc(xf_ready, 1)

            def place(n):
                th, i, hh = PIECES[n]
                return th, i, hh, max(0, i - 4 * th) * P

            def z_leaves(p, n):
                _, _, _, c0 = place(n)
                s = NPC * p + n
                dve.wait_ge(z_mm, s + 1)
                if s >= 4:
                    dve.wait_ge(sw_exp, s - 3)
                nc.vector.tensor_copy(sz[:, s % 4, c0:], ps[:, 2 + s % 2, c0:]).then_inc(z_out, 1)

            def softplus(p, n):
                th, i, _, c0 = place(n)
                s = NPC * p + n
                dve.wait_ge(l_ready, s + 1)
                if s >= 4:
                    dve.wait_ge(sph_ready, s - 3)
                    dve.wait_ge(spl_ready, s - 3)
                ins = stt(sp[:, s % 4, c0:], sz[:, s % 4, c0:], 0.0, sl[:, s % 4, c0:], ALU.max, ALU.add)
                if i >= 4 * th:
                    step(ins)
                    ins = tt(sp[:, s % 4, c0:c0 + P], sp[:, s % 4, c0:c0 + P], ctri, ALU.mult)
                ins.then_inc(sp_ready, 1)

            def sp_low(p, n):
                c0 = place(n)[3]
                s = NPC * p + n
                dve.wait_ge(sp_ready, s + 1)
                dve.wait_ge(sph_ready, s + 1)
                if s >= 4:
                    dve.wait_ge(suf_mm, s - 2)
                tt(spl[:, s % 4, c0:], sp[:, s % 4, c0:], sph[:, s % 4, c0:].bitcast(F32),
                   ALU.subtract).then_inc(spl_ready, 1)

            def exponent(p, n):
                th, i, hh, c0 = place(n)
                s = NPC * p + n
                dve.wait_ge(suf_mm, s + 1)
                ins = tt(sz[:, s % 4, c0:], sz[:, s % 4, c0:], ps[:, 4 + hh, c0:], ALU.add)
                if i >= 4 * th:
                    step(ins)
                    ins = ts(sz[:, s % 4, c0:c0 + P], sz[:, s % 4, c0:c0 + P], 0.0, None, ALU.min)
                ins.then_inc(t_ready, 1)

            def causal(p, n):
                th, i, _, c0 = place(n)
                s = NPC * p + n
                if i >= 4 * th:
                    dve.wait_ge(sw_exp, s + 1)
                    tt(sw[:, s % 4, c0:c0 + P], sw[:, s % 4, c0:c0 + P], ctri, ALU.mult).then_inc(sw_ready, 1)

            leave(U_SB + 1, sk[0][:, 1, :])
            for p in range(HEADS):
                u = U_SB + 3 * p
                n = N_QK + p
                leave_half(u + 2, 0, sv[:, :])
                st_inverse(n, 32, 1.0 / 64)
                dve.wait_ge(st_bc, n + 1)
                for t, gain in enumerate((dcol("qn"), col("kn"))):
                    stt(sk[p % 2][:, t, :], sk[p % 2][:, t, :], gain, banks(4 - 2 * t), ALU.mult,
                        ALU.mult).then_inc(qk2_ready, 1)
                leave_half(u + 2, 1, sv[:, :])
                slots = filling(*sb_fill(p), NPC + 3)
                u_next = sb_fill(p)[0]
                if p + 1 < HEADS:
                    next_ = [sk[(p + 1) % 2][:, 0, :], sk[(p + 1) % 2][:, 1, :]]
                else:
                    next_ = [cc[:, j, :] for j in range(3)]
                dve.wait_ge(x_out, 16 * KT)
                for n in range(NPC + 4):
                    if n < NPC:
                        z_leaves(p, n)
                    if 1 <= n <= NPC:
                        softplus(p, n - 1)
                    if n:
                        evict(slots[n - 1], u_next, next_)
                    if 2 <= n <= NPC + 1:
                        exponent(p, n - 2)
                    if 1 <= n <= NPC:
                        sp_low(p, n - 1)
                    if 3 <= n <= NPC + 2:
                        causal(p, n - 3)

            def short_conv(j):
                dve.wait_ge(acc_free, half_no((U_CV1 if j else U_CV) + 2, 1))
                step(tt(cp[:, 2:T + 2], cc[:, 0, :], cc[:, 1, :], ALU.mult))
                step(ts(cc[:, 0, :], cp[:, 0:T], col("conv2_w0", j), None, ALU.mult))
                step(stt(cc[:, 0, :], cp[:, 1:T + 1], col("conv2_w1", j), cc[:, 0, :], ALU.mult, ALU.add))
                step(stt(cc[:, 0, :], cp[:, 2:T + 2], col("conv2_w2", j), cc[:, 0, :], ALU.mult, ALU.add))
                tt(mix[:, j, :], cc[:, 0, :], cc[:, 2, :], ALU.mult).then_inc(mix_ready, 1)
                dve.wait_ge(mix_ready, 2 * HEADS + j + 1)

            def gate_bias(j):
                dve.wait_ge(gs_mm, j + 1)
                for hh in range(2):
                    r = slice(64 * hh, 64 * hh + 64)
                    tt(chunks(mix[r, 6 + j, :], P), banks(4 + 2 * hh)[r, :].rearrange("p (n t) -> p n t", t=P),
                       gb[r, j, :].rearrange("p (o t) -> p o t", o=1).to_broadcast([64, KT, P]),
                       ALU.add).then_inc(g_done, 1)

            def gate(j):
                dve.wait_ge(g_done, 2 * j + 2)
                dve.wait_ge(gelu_done, j + 3)
                tt(mix[:, 6 + j, :], mix[:, 6 + j, :], gu[:, j, :], ALU.mult).then_inc(mix_ready, 1)

            dve.wait_ge(so_out, 4 * HEADS)
            step(nc.vector.memset(cp[:, 0:2], 0.0))
            leave(U_SV, gv[:, 0, :])
            short_conv(0)
            leave(U_SV + 1, gv[:, 1, :])
            leave(U_CV1, cc[:, 0, :])
            st_inverse(N_SG, 32, 1.0 / 64)
            leave_half(U_CV1 + 1, 0, cc[:, 1, :])
            dve.wait_ge(gate_in, 48)
            tt(gw[:, :, :], gw[:, :, :], gmask[:, :].rearrange("p (o t) -> p o t", o=1)
               .to_broadcast([P, 4, P]), ALU.mult).then_inc(gw_ready, 1)
            dve.wait_ge(st_bc, N_SG + 1)
            for j in range(2):
                stt(gv[:, j, :], gv[:, j, :], col("sgu_g", j), banks(4 - 2 * j), ALU.mult,
                    ALU.mult).then_inc(gn_ready, 1)
            leave_half(U_CV1 + 1, 1, cc[:, 1, :])
            leave(U_CV1 + 2, cc[:, 2, :])
            gate_bias(0)
            short_conv(1)
            leave(U_SU, gu[:, 0, :])
            gate_bias(1)
            gate(0)
            leave(U_SU + 1, gu[:, 1, :])
            gate(1)

            out_projection(U_OUT2, F_MIX2, 2 * HEADS - 4, 3, Q_2, "norm2")
            st_inverse(N_2, 8, 1.0 / T)
            dve.wait_ge(ss_ready, Q_2 + KT)
            dve.wait_ge(rstd_ready, 5)

            def hidden2(u, s, f, fi):
                if not (isinstance(fi, int) and fi < 2):
                    dve.wait_ge(f_lo, f - 1)
                if not (isinstance(fi, int) and fi < 1):
                    dve.wait_ge(fx_ready, FT + fi)
                leave(u, c_buf[:, :])
                dve.wait_ge(acc_free, half_no(u, 1))
                stt(pad_a[:, s, 0:T], c_buf[:, :], 0.0, c_buf[:, :], ALU.max, ALU.mult).then_inc(fx_ready, 1)
                dve.wait_ge(fx_ready, FT + fi + 1)

            fi = 0
            for gi, n in enumerate(GROUPS2):
                def pair2(i):
                    for s in range(2):
                        t = fi + 2 * i + s
                        hidden2(U_F1[gi] + 2 * i + s, s, F_FF2 + t, t)
                        remainder(F_FF2 + t, s, 2 * i + s, 0)
                if gi == 0:
                    pair2(0)
                with dve.Fori(1 if gi == 0 else 0, n // 2, 1) as i:
                    pair2(i)
                fi += n
                if gi == len(GROUPS2) - 1:
                    split_embedding(1)
                down(U_F2[gi], gi == len(GROUPS2) - 1, Q_3, "norm3")
            st_inverse(N_3, 8, 1.0 / T)
            embedding(U_PLE2, 1, 6)

        @block.scalar
        def _(act):
            def av(out, in_, f, **kw):
                return nc.scalar.activation(out, in_, f, **kw)

            steps = [0]

            def step(ins):
                ins.then_inc(act_step, 1)
                steps[0] += 1
                act.wait_ge(act_step, steps[0])

            def until(sem_, value):
                act.wait_ge(sem_, value)
                act.wait_ge(param_in, 48)

            def col(name, j=0, n=1):
                return vec[:, VEC[name] + j:VEC[name] + j + n]

            def dcol(name, j=0, n=1):
                return der[:, DER[name] + j:DER[name] + j + n]

            def prep(q, k, gain, xk):
                av(a_hi[:, k, :], xk, ACT.Copy, scale=gain).then_inc(h_hi, 1)
                if q + k >= 2:
                    act.wait_ge(ss_ready, q + k - 1)
                av(sq[:, k % 2, 0:T], xk, ACT.Square).then_inc(sq_ready, 1)

            def st_sqrt(n, ncols):
                act.wait_ge(st_var, n + 1)
                av(sm[:, 2, 0:ncols], sm[:, 1, 0:ncols], ACT.Sqrt).then_inc(st_root, 1)

            def keep_rstd(bc):
                act.wait_ge(st_bc, bc)
                av(rstd[:, :], banks(5), ACT.Copy).then_inc(rstd_ready, 1)

            act.wait_ge(g_ready, 1)
            step(av(dcol("g0", 0, 8), dcol("g0", 0, 8), ACT.Exp))
            step(av(dcol("g1", 0, 8), dcol("g1", 0, 8), ACT.Exp))
            act.wait_ge(lam_mm, 1)
            av(dcol("lame", 0, 2), ps[:, 7, 0:2], ACT.Exp).then_inc(lam_exp, 1)
            act.wait_ge(param_in, 48)
            for k in range(KT):
                act.wait_ge(x_in[k], 16)
                prep(Q_MIX, k, col("norm_mix", k), x[:, k, :])
            st_sqrt(N_MIX, 8)
            keep_rstd(N_MIX + 1)
            for n, m in enumerate((sinm, cosm)):
                act.wait_ge(ang_ready, n + 1)
                av(m[:, :], m[:, :], ACT.Sin).then_inc(cs_ready, 1)

            def exps(h, qt, m):
                g = KT * h + qt
                act.wait_ge(max_ready, 2 * g + m + 1)
                if g >= 2:
                    act.wait_ge(w_tr, 2 * (g - 1))
                av(de[:, g % 2, m, :], banks(2 + 2 * m), ACT.Exp, scale=0.125, bias=rows[:, m, 1:2],
                   accum_out=rows[:, g % 2, 2 + m:3 + m]).then_inc(exp_done, 1)

            def turned(h, qt, r):
                g = KT * h + qt
                act.wait_ge(w_tr, 2 * g + r + 1)
                if g:
                    act.wait_ge(o_mm, g)
                av(dwt[:, r, :], ps[:, 6, :], ACT.Copy).then_inc(wt_ready, 1)
                if r == 1 and qt in (3, 7):
                    act.wait_ge(o_mm, g + 1)
                    hf = qt // 4
                    av(mix[:, h, hf * HALF:(hf + 1) * HALF], ps[:, 7, :], ACT.Copy).then_inc(o_out, 1)

            def high_qk(h, t):
                act.wait_ge(qk_ready, 2 * h + t + 1)
                for m in range(2):
                    r, o = slice(64 * m, 64 * m + 64), slice(64 * (1 - m), 64 * (1 - m) + 64)
                    if t:
                        av(dkk[m][o, :], dq[h % 2][r, 1, :], ACT.Copy)
                    ins = av((dkk if t else dqs)[m][r, :], dq[h % 2][r, t, :], ACT.Copy)
                ins.then_inc(qk_high, 1)

            for h in range(HEADS):
                high_qk(h, 0)
                if h:
                    st_sqrt(N_DA + h - 1, 8)
                high_qk(h, 1)
                act.wait_ge(v_tr, h + 1)
                av(dvt[:, :, :], banks(2).rearrange("p (c e) -> p c e", c=KT), ACT.Copy).then_inc(v_ready, 1)
                for qt in range(KT + 1):
                    for m in range(2):
                        if qt < KT:
                            exps(h, qt, m)
                        if qt:
                            turned(h, qt - 1, m)
                act.wait_ge(o_out, 2 * h + 2)
                if h:
                    act.wait_ge(st_sum, N_DA + h)
                av(ang[:, :], mix[:, h, :], ACT.Square).then_inc(o_sq, 1)

            act.dma_start(hmask[:, :, :], io["hmask"]).then_inc(hmask_in, 16)
            for h in range(HEADS):
                u = U_HG + 5 * h
                hzh = hz[h % 2]
                if h:
                    act.wait_ge(qd_ready, 2 * h)
                for d in range(2):
                    act.wait_ge(acc_free, half_no(u + 1 + d, 1))
                    av(hd[:, d, :], hzh[d][:, :], ACT.Sigmoid).then_inc(sig_done, 1)
                    av(hk[:, d, :], hzh[d][:, :], ACT.Sigmoid, scale=-1.0).then_inc(sig_done, 1)
                nc.scalar.preload_act_table_set("natural_log_exp_and_others")
                for d in range(2):
                    act.wait_ge(f_ready, 2 * h + d + 1)
                    av(hd[:, d, :], hd[:, d, :], ACT.Ln).then_inc(logf_done, 1)
                st_sqrt(N_HG + h - 1, 8)
                act.wait_ge(v_tr, HEADS + h + 1)
                av(hvt[:, :, :], banks(2).rearrange("p (c e) -> p c e", c=KT), ACT.Copy).then_inc(v_ready, 1)
                for l in range(2 * LEVELS):
                    d = l % 2
                    hs = 1 << (l // 2)
                    lower, upper = slice(0, hs), slice(hs, 2 * hs)
                    qs, ks = (upper, lower) if d == 0 else (lower, upper)
                    act.wait_ge(d_ready, 16 * h + l + 1)
                    e = hd[:, d, :].rearrange("p (n t) -> p n t", t=2 * hs)
                    av(e[:, :, qs], e[:, :, qs], ACT.Exp).then_inc(e_done, 1)
                    av(e[:, :, ks], e[:, :, ks], ACT.Exp, scale=-1.0).then_inc(e_done, 1)
                for d in range(2):
                    ref = P - 1 if d == 0 else 0
                    act.wait_ge(d_ready, 16 * h + 14 + d + 1)
                    av(hd[:, d, :], hd[:, d, :], ACT.Exp, scale=-1.0).then_inc(e_done, 1)
                    far = hzh[d][:, :].rearrange("p (c t) -> p c t", t=P)[:, :, ref:ref + 1]
                    av(heb[:, d, :].rearrange("p (c t) -> p c t", t=1), far, ACT.Exp).then_inc(e_done, 1)
                    act.wait_ge(kd_ready, 2 * h + d + 1)
                    av(hd[:, d, :], hzh[d][:, :], ACT.Exp).then_inc(e_done, 1)
                for d in range(2):
                    act.wait_ge(kd_tr, 2 * h + d + 1)
                    if d:
                        act.wait_ge(kv_mm, 2 * h + 1)
                    av(hkd[:, :, :], banks(2).rearrange("p (c e) -> p c e", c=KT),
                       ACT.Copy).then_inc(kdt_ready, 1)
                act.wait_ge(acc_free, half_no(u + 4, 1))
                av(hg[:, :], hg[:, :], ACT.Silu).then_inc(silu_done, 1)
                act.wait_ge(ho_mm, h + 1)
                av(mix[:, HEADS + h, :], banks(6), ACT.Copy).then_inc(ho_out, 1)
                act.wait_ge(ho_out, h + 1)
                av(hkd_flat, mix[:, HEADS + h, :], ACT.Square).then_inc(o_sq, 1)

            st_sqrt(N_HG + HEADS - 1, 8)

            def split_mix(f0, m0, source):
                act.wait_ge(mix_ready, m0 + KT)
                for k in range(KT):
                    av(b_hi[:, k, :], mix[:, k, :], ACT.Copy).then_inc(f_hi, 1)
                for k in range(KT):
                    act.wait_ge(f_lo, f0 + k + 1)
                    act.dma_start(x[:, k, :], source[:, k, :]).then_inc(x_in[k], 16)

            def preps(q, u0, gain):
                for k in range(KT):
                    act.wait_ge(acc_free, half_no(u0 + k, 1))
                    prep(q, k, col(gain, k), x[:, k, :])

            def high(f, s, j, first, fx):
                until(fx_ready, fx)
                av(b_hi[:, bass.ds(j, 1), :].rearrange("p a b -> p (a b)"), pad_a[:, s, first:first + T],
                   ACT.Copy).then_inc(f_hi, 1)

            def round_embedding(turn, name, u_before):
                act.wait_ge(acc_full, half_no(u_before + KT - 1, 1))
                act.dma_start(p_raw[:, :, :], io[name]).then_inc(p_in, 16)
                act.wait_ge(p_in, 16 * (turn + 1))
                for k in range(PT):
                    av(b_hi[:, 6 + k, :], p_raw[:, k, :], ACT.Copy).then_inc(p_hi, 1)

            split_mix(F_MIX, 0, io["x"])
            preps(Q_FFN, U_OUT, "norm_ffn")
            st_sqrt(N_FFN, 8)
            keep_rstd(N_FFN + 1)
            fi = 0
            for gi, n in enumerate(GROUPS1):
                with act.Fori(0, n // 2, 1) as i:
                    for s in range(2):
                        t = fi + 2 * i + s
                        until(conv_done, 3 * t + 3)
                        av(c_buf[:, :], c_buf[:, :], ACT.Gelu).then_inc(act_done, 1)
                        high(F_FF + t, s, 2 * i + s, 1, t + 1)
                fi += n
            round_embedding(0, "p", U_DN[-2])
            preps(Q_PLE, U_DN[-1], "norm_ple")

            def final_high(k):
                av(a_hi[:, k, :], x[:, k, :], ACT.Copy, scale=dcol("fin_n1", k)).then_inc(h_hi, 1)

            def embedding(u0, turn, n):
                for e in range(2 * KT):
                    if e == KT:
                        st_sqrt(n, 8)
                    k, hf = e // 2, e % 2
                    c = slice(hf * HALF, (hf + 1) * HALF)
                    if e % KT == KT - 1:
                        act.wait_ge(acc_full, half_no(u0 + e // KT, 1))
                    else:
                        act.wait_ge(e_mm, (KT - 1) * (2 * turn + e // KT) + e % KT + 1)
                    ins = av(emb[k][:, c], ps[:, 2 + e % 3, :], ACT.Copy)
                    ins.then_inc(e_out, 1)
                    if e % KT == KT - 1:
                        act.wait_ge(e_out, 2 * KT * turn + e + 1)
                        act.sem_inc(acc_free, 2)
                keep_rstd(n + 1)
                for k in range(KT):
                    for hf in range(2):
                        c = slice(hf * HALF, (hf + 1) * HALF)
                        act.wait_ge(acc_free, half_no(u0 + NE + k, hf))
                        av(pad_a[:, 0, c], pad_a[:, 0, c], ACT.Sigmoid).then_inc(pg_sig, 1)
                    if turn == 0 and k == KT - 1:
                        for j in range(3):
                            final_high(j)
                    act.wait_ge(x_done, KT * turn + k + 1)
                    if turn:
                        act.dma_start(io["out"][:, k, :], x[:, k, :]).then_inc(out_done, 16)
                    else:
                        av(fsq[:, 0, :], x[:, k, :], ACT.Square)
                        av(fsq[:, 1, :], x[:, k, :], ACT.Square, scale=col("final", k)).then_inc(sq_ready, 1)

            embedding(U_PLE, 0, N_PLE)

            for k in range(3, KT):
                final_high(k)
            st_sqrt(N_FIN, 8)
            st_sqrt(N_1, 8)
            keep_rstd(N_FIN + 1)
            act.dma_start(tri_raw[:, :, :], io["tri"]).then_inc(tri_in, 16)
            act.wait_ge(tri_in, 16)
            for n in range(2):
                av(tri[:, n, :], tri_raw[:, n, :], ACT.Copy).then_inc(tri_ready, 1)
            for k in range(KT):
                act.wait_ge(xf_ready, k + 1)
                act.dma_start(x_back[:, k, :], x[:, k, :]).then_inc(x_out, 16)

            def soft(p, n, part):
                th, i, _ = PIECES[n]
                c0 = max(0, i - 4 * th) * P
                s = NPC * p + n
                out = sl[:, s % 4, c0:]
                if part == 0:
                    act.wait_ge(z_out, s + 1)
                    if s >= 4:
                        act.wait_ge(sp_ready, s - 3)
                    av(out, sz[:, s % 4, c0:], ACT.Abs).then_inc(z_abs, 1)
                elif part == 1:
                    act.wait_ge(z_abs, s + 1)
                    av(out, out, ACT.Exp, scale=-1.0).then_inc(z_exp, 1)
                else:
                    act.wait_ge(z_exp, s + 1)
                    av(out, out, ACT.Ln, bias=1.0).then_inc(l_ready, 1)

            def sp_high(p, n):
                th, i, _ = PIECES[n]
                c0 = max(0, i - 4 * th) * P
                s = NPC * p + n
                act.wait_ge(sp_ready, s + 1)
                if s >= 4:
                    act.wait_ge(spl_ready, s - 3)
                    act.wait_ge(suf_mm, s - 2)
                av(sph[:, s % 4, c0:], sp[:, s % 4, c0:], ACT.Copy).then_inc(sph_ready, 1)

            def weight(p, n):
                th, i, hh = PIECES[n]
                c0 = max(0, i - 4 * th) * P
                s = NPC * p + n
                act.wait_ge(t_ready, s + 1)
                if s >= 4:
                    act.wait_ge(so_mm, s - 3)
                av(sw[:, s % 4, c0:], sz[:, s % 4, c0:], ACT.Exp).then_inc(sw_exp, 1)

            def out_rows(p, n):
                th, i, hh = PIECES[n]
                s = NPC * p + n
                if i == 0:
                    act.wait_ge(so_mm, s + 1)
                    r = slice(64 * hh, 64 * hh + 64)
                    av(mix[r, 2 + p, th * HALF:(th + 1) * HALF], ps[r, 6 + hh, :], ACT.Copy).then_inc(so_out, 1)

            def square(p, t):
                act.wait_ge(acc_free, half_no(U_SB + 3 * p + t, 1))
                act.wait_ge(st_sum, N_QK + p)
                av((c_buf, ss)[t][:, :], sk[p % 2][:, t, :], ACT.Square).then_inc(sq_qk, 1)

            square(0, 0)
            square(0, 1)
            for p in range(HEADS):
                st_sqrt(N_QK + p, 32)
                nc.scalar.preload_act_table_set("natural_log_exp_and_others")
                act.wait_ge(sv_tr, p + 1)
                av(svt[:, :, :], banks(6).rearrange("p (c e) -> p c e", c=KT), ACT.Copy).then_inc(sv_ready, 1)
                act.wait_ge(x_out, 16 * KT)
                for n in range(NPC + 5):
                    if n < NPC:
                        soft(p, n, 0)
                    if 3 <= n <= NPC + 2:
                        weight(p, n - 3)
                    if n < NPC:
                        soft(p, n, 1)
                    if 1 <= n <= NPC:
                        sp_high(p, n - 1)
                    if n < NPC:
                        soft(p, n, 2)
                    if n >= 5:
                        out_rows(p, n - 5)
                    if n == 20 and p + 1 < HEADS:
                        square(p + 1, 0)
                if p + 1 < HEADS:
                    square(p + 1, 1)

            act.wait_ge(so_out, 4 * HEADS)
            act.dma_start(gw[:, :, :], io["gw"]).then_inc(gate_in, 16)
            act.dma_start(gb[:, :, :], io["gb"]).then_inc(gate_in, 16)
            act.dma_start(gmask[:, :], io["gmask"]).then_inc(gate_in, 16)
            for j in range(2):
                act.wait_ge(acc_free, half_no(U_SV + j, 1))
                av(gv[:, j, :], gv[:, j, :], ACT.Gelu).then_inc(gelu_done, 1)
                act.wait_ge(gelu_done, j + 1)
                act.wait_ge(st_sum, N_SG)
                av((c_buf, ss)[j][:, :], gv[:, j, :], ACT.Square).then_inc(g_sq, 1)
            st_sqrt(N_SG, 32)
            for j in range(2):
                act.wait_ge(g_tr, j + 1)
                av(gvt[:, j, :, :], banks(6 - 4 * j).rearrange("p (c e) -> p c e", c=KT),
                   ACT.Copy).then_inc(gt_ready, 1)
            for j in range(2):
                act.wait_ge(acc_free, half_no(U_SU + j, 1))
                av(gu[:, j, :], gu[:, j, :], ACT.Gelu).then_inc(gelu_done, 1)

            split_mix(F_MIX2, 2 * HEADS - 4, x_back)
            preps(Q_2, U_OUT2, "norm2")
            st_sqrt(N_2, 8)
            keep_rstd(N_2 + 1)
            fi = 0
            for gi, n in enumerate(GROUPS2):
                with act.Fori(0, n // 2, 1) as i:
                    for s in range(2):
                        t = fi + 2 * i + s
                        high(F_FF2 + t, s, 2 * i + s, 0, FT + t + 1)
                fi += n
            round_embedding(1, "p2", U_F2[-2])
            preps(Q_3, U_F2[-1], "norm3")
            embedding(U_PLE2, 1, N_3)


def constants():
    f = np.float32
    ident = np.eye(P, dtype=f)
    cst = np.zeros((P, 8), f)
    cst[:, 0] = 1.0
    cst[:64, 1] = 1.0
    cst[64:, 2] = 1.0
    half = 8
    freq = f(500000.0) ** (-np.arange(half, dtype=f) / f(half))
    swap = np.zeros((P, P), f)
    for m in range(2):
        for j in range(half):
            a, b = 64 * m + j, 64 * m + half + j
            cst[a, 3] = cst[b, 3] = freq[j]
            swap[b, a] = -1.0
            swap[a, b] = 1.0
    s = np.arange(P)[:, None]
    t = np.arange(P)[None, :]
    tri = np.stack([-(s >= t).astype(f), -(s < t).astype(f), (s < t).astype(f)], 1)
    mask = np.zeros((P, 2 * LEVELS, 64), np.int32)
    for l in range(2 * LEVELS):
        hs = 1 << (l // 2)
        for idx in range(64):
            blk = idx // hs
            lo = blk * 2 * hs + (0 if l % 2 == 0 else hs)
            mask[lo:lo + hs, l, idx] = 1
    return {"ident": ident, "cst": cst, "swap": swap, "tri": np.ascontiguousarray(tri), "hmask": mask,
            "gmask": (s <= t).astype(f)}


def kernel(**inputs):
    import concourse.bacc as bacc
    from concourse.bass_utils import run_bass_kernel_spmd

    v = {k: np.asarray(a) for k, a in inputs.items()}

    def tiles(w, order=None):
        kt, nt = w.shape[0] // P, w.shape[1] // P
        w = w.reshape(kt, P, nt, P).transpose(2, 1, 0, 3).reshape(nt, P, kt * P)
        return w if order is None else w[order]

    def cols(a, n):
        return np.ascontiguousarray(np.asarray(a).reshape(n, P).T)

    def feature_major(a, n):
        return np.ascontiguousarray(a.T.reshape(n, P, -1).transpose(1, 0, 2))

    arrays = dict(constants())
    arrays["x"] = feature_major(v["x"][0], KT)
    arrays["p"] = feature_major(v["p"][0, 0], PT)
    arrays["p2"] = feature_major(v["p_2"][0, 0], PT)
    arrays["pos"] = np.ascontiguousarray(np.broadcast_to(v["positions"].reshape(1, T), (P, T)))
    vecs = {
        "norm_mix": cols(v["norm_mix_g"], 8), "norm_ffn": cols(v["norm_ffn_g"], 8),
        "norm_ple": cols(v["norm_ple_g"], 8), "final": cols(v["final_norm_g"], 8),
        "norm1": cols(v["norm1_g_2"], 8), "norm2": cols(v["norm2_g_2"], 8),
        "norm3": cols(v["norm3_g_2"], 8), "conv_b": cols(v["ffn_conv_b"], FT),
        "qn": cols(np.tile(v["q_norm_g_2"][0], 2), 1), "kn": cols(np.tile(v["k_norm_g_2"][0], 2), 1),
        "sgu_g": cols(v["sgu_norm_g_2"], 2), "subln": cols(v["da_subln_g"], 1),
        "hgn": cols(v["hg_norm_g"], 1), "gamma0": cols(v["hg_lb_gamma"][:, 0], 8),
        "gamma1": cols(v["hg_lb_gamma"][:, 1], 8),
    }
    for j in range(3):
        vecs[f"conv_w{j}"] = cols(v["ffn_conv_w"][0, j], FT)
        vecs[f"conv2_w{j}"] = cols(v["conv_w_2"][0, j], 2)
    lam = np.zeros((P, 4), v["lam_q1"].dtype)
    for j, name in enumerate(("lam_q1", "lam_k1", "lam_q2", "lam_k2")):
        lam[:64, j] = v[name][0]
    vecs["lam"] = lam
    arrays["vec"] = np.ascontiguousarray(np.concatenate([vecs[n] for n in VEC], 1))

    order = [t * HEADS + h for h in range(HEADS) for t in range(3)]
    order += [(3 + t) * HEADS + h for h in range(HEADS) for t in range(5)]
    arrays["w_mix"] = tiles(v["w_in"][0], order)
    arrays["w_out"] = tiles(v["w_out"][0])
    gate, up, dn = tiles(v["w_ffn_gate"][0]), tiles(v["w_ffn_up"][0]), v["w_ffn_down"][0]
    f = 0
    for gi, n in enumerate(GROUPS1):
        arrays[f"w_gu{gi}"] = np.stack([gate[f:f + n], up[f:f + n]], 1).reshape(2 * n, P, T)
        arrays[f"w_dn{gi}"] = tiles(dn[f * P:(f + n) * P])
        f += n

    def ple(gate_w, emb_w):
        g, e = tiles(gate_w), tiles(emb_w)
        e = e.reshape(NE, KT // NE, P, PT * P).transpose(0, 2, 1, 3).reshape(NE, P, T)
        return np.concatenate([e, g], 0)

    arrays["w_ple"] = ple(v["w_ple_gate"][0], v["w_ple"][0])
    order = [b + p for p in range(HEADS) for b in (6, 10, 14)]
    order += [2, 4, 0, 20, 21, 3, 5, 1, 18, 19]
    arrays["w_mix2"] = tiles(v["w_in_2"][0], order)
    arrays["w_out2"] = tiles(v["w_out_2"][0])
    f1, f2 = tiles(v["w_ff1_2"][0]), v["w_ff2_2"][0]
    f = 0
    for gi, n in enumerate(GROUPS2):
        arrays[f"w_f1{gi}"] = f1[f:f + n]
        arrays[f"w_f2{gi}"] = tiles(f2[f * P:(f + n) * P])
        f += n
    arrays["w_ple2"] = ple(v["w_ple_gate_2"][0], v["w_ple_proj_2"][0])
    arrays["gw"] = v["sgu_w_2"][0].transpose(2, 0, 1)
    arrays["gb"] = np.repeat(v["sgu_b_2"][0].reshape(2, 2, 1, P), 64, axis=2).reshape(2, P, P).transpose(1, 0, 2)

    nc = bacc.Bacc("TRN2", target_bir_lowering=False, num_devices=1)
    arrays = {k: np.ascontiguousarray(a) for k, a in arrays.items()}
    io = {k: nc.dram_tensor(f"in_{k}", a.shape, mybir.dt.from_np(a.dtype), kind="ExternalInput").ap()
          for k, a in arrays.items()}
    io["out"] = nc.dram_tensor("out_x", (P, KT, T), F32, kind="ExternalOutput").ap()
    bass_two_blocks(nc, io)
    r = run_bass_kernel_spmd(nc, [{f"in_{k}": a for k, a in arrays.items()}], core_ids=[0])
    out = r.results[0]["out_x"]
    return np.ascontiguousarray(out.transpose(1, 0, 2).reshape(KT * P, T).T).reshape(1, T, KT * P)
```
